# Optimizing a Trainium2 kernel written in Bass

```python
import math
import jax, jax.numpy as jnp
from jax import lax
import numpy as np

D_MODEL = 1024
BATCH = 1
SEQ = 256
DEPTH = 2

N_HEADS = 16
HEAD_DIM = D_MODEL // N_HEADS
ROPE_DIM = HEAD_DIM // 4
ROPE_THETA = 500000.0
ATTN_SCALE = HEAD_DIM ** -0.5
DILATED_PAIRS = ((128, 1), (512, 4), (2048, 16))
N_DIL = len(DILATED_PAIRS)
BAND_BLOCK = 128
MOBA_BLOCK = 256
MOBA_TOPK = 3
MOBA_QCHUNK = 128
D_FF = 2816
CONV_WIDTH = 3
RMS_EPS = 1e-6
N_LAYERS_A = (DEPTH + 1) // 2
N_LAYERS_B = DEPTH // 2


def rmsnorm(x, gain):
    xf = x.astype(jnp.float32)
    y = xf * lax.rsqrt(jnp.mean(xf * xf, axis=-1, keepdims=True) + RMS_EPS)
    return (y * gain.astype(jnp.float32)).astype(x.dtype)

def rope_tables(seq_len):
    pos = jnp.arange(seq_len, dtype=jnp.float32)
    inv_freq = ROPE_THETA ** (-jnp.arange(0, ROPE_DIM, 2, dtype=jnp.float32) / ROPE_DIM)
    ang = pos[:, None] * inv_freq[None, :]
    return jnp.cos(ang), jnp.sin(ang)

def apply_partial_rope(x, cos, sin):
    extra = x.ndim - 3
    c = cos.reshape((cos.shape[0],) + (1,) * extra + (cos.shape[1],)).astype(x.dtype)
    s = sin.reshape((sin.shape[0],) + (1,) * extra + (sin.shape[1],)).astype(x.dtype)
    half = ROPE_DIM // 2
    x1, x2, xp = x[..., :half], x[..., half:ROPE_DIM], x[..., ROPE_DIM:]
    return jnp.concatenate([x1 * c - x2 * s, x2 * c + x1 * s, xp], axis=-1)

def band_attention(q, k, v, dil, window):
    S, H, hd = q.shape
    reach = window // dil
    assert reach <= BAND_BLOCK
    span = dil * BAND_BLOCK
    s_pad = -(-S // span) * span
    L = s_pad // dil
    nb = L // BAND_BLOCK

    def to_res(t):
        t = jnp.pad(t, ((0, s_pad - S), (0, 0), (0, 0)))
        return t.reshape(L, dil, H, hd).transpose(1, 0, 2, 3).reshape(dil, nb, BAND_BLOCK, H, hd)

    qr, kr, vr = to_res(q), to_res(k), to_res(v)

    def with_prev(t):
        prev = jnp.concatenate([jnp.zeros_like(t[:, :1]), t[:, :-1]], axis=1)
        return jnp.concatenate([prev, t], axis=2)

    kc, vc = with_prev(kr), with_prev(vr)
    scores = jnp.einsum('rnqhd,rnkhd->rnhqk', qr, kc).astype(jnp.float32) * ATTN_SCALE
    qi = jnp.arange(BAND_BLOCK)
    kj = jnp.arange(2 * BAND_BLOCK)
    dist = qi[:, None] + BAND_BLOCK - kj[None, :]
    kpos = jnp.arange(nb)[:, None] * BAND_BLOCK - BAND_BLOCK + kj[None, :]
    mask = ((dist >= 0) & (dist <= reach))[None] & (kpos >= 0)[:, None, :]
    scores = jnp.where(mask[None, :, None], scores, -jnp.inf)
    m = scores.max(axis=-1)
    p = jnp.exp(scores - m[..., None])
    den = p.sum(axis=-1)
    num = jnp.einsum('rnhqk,rnkhd->rnqhd', p, vc.astype(jnp.float32))
    m_t = m.transpose(0, 1, 3, 2)
    den_t = den.transpose(0, 1, 3, 2)
    o = num / den_t[..., None]

    def from_res(t):
        t = t.reshape((dil, L) + t.shape[3:])
        t = jnp.swapaxes(t, 0, 1)
        return t.reshape((s_pad,) + t.shape[2:])[:S]

    return from_res(o), from_res(m_t), from_res(den_t)

def mixer_dilated(h, w_qkv, q_gain, k_gain, w_o, cos, sin):
    B, S, _ = h.shape
    qkv = (h @ w_qkv).reshape(B, S, 3, N_DIL, N_HEADS, HEAD_DIM)
    q = apply_partial_rope(rmsnorm(qkv[:, :, 0], q_gain[:, None, :]), cos, sin)
    k = apply_partial_rope(rmsnorm(qkv[:, :, 1], k_gain[:, None, :]), cos, sin)
    v = qkv[:, :, 2]

    def one_sequence(args):
        qb, kb, vb = args
        outs, maxes, dens = [], [], []
        for g, (window, dil) in enumerate(DILATED_PAIRS):
            o, m, d = band_attention(qb[:, g], kb[:, g], vb[:, g], dil, window)
            outs.append(o)
            maxes.append(m)
            dens.append(d)
        o = jnp.stack(outs)
        m = jnp.stack(maxes)
        d = jnp.stack(dens)
        wgt = d * jnp.exp(m - m.max(axis=0, keepdims=True))
        wgt = wgt / wgt.sum(axis=0, keepdims=True)
        return jnp.einsum('gsh,gshd->shd', wgt, o)

    attn = lax.map(one_sequence, (q, k, v))
    return attn.reshape(B, S, N_HEADS * HEAD_DIM).astype(h.dtype) @ w_o

def mixer_moba(h, w_qkv, q_gain, k_gain, w_o, cos, sin):
    B, S, _ = h.shape
    qkv = (h @ w_qkv).reshape(B, S, 3, N_HEADS, HEAD_DIM)
    q = apply_partial_rope(rmsnorm(qkv[:, :, 0], q_gain), cos, sin)
    k = apply_partial_rope(rmsnorm(qkv[:, :, 1], k_gain), cos, sin)
    v = qkv[:, :, 2]
    s_pad = -(-S // MOBA_BLOCK) * MOBA_BLOCK
    nblk = s_pad // MOBA_BLOCK
    n_chunk = s_pad // MOBA_QCHUNK
    topk = min(MOBA_TOPK, nblk)

    def to_bhsd(t):
        return jnp.pad(t, ((0, 0), (0, s_pad - S), (0, 0), (0, 0))).transpose(0, 2, 1, 3)

    q, k, v = to_bhsd(q), to_bhsd(k), to_bhsd(v)
    k_blocks = k.reshape(B, N_HEADS, nblk, MOBA_BLOCK, HEAD_DIM)
    v_blocks = v.reshape(B, N_HEADS, nblk, MOBA_BLOCK, HEAD_DIM)
    k_mean = k_blocks.astype(jnp.float32).mean(axis=3)
    gate = jnp.einsum('bhsd,bhnd->bhsn', q.astype(jnp.float32), k_mean)
    own_blk = jnp.arange(s_pad) // MOBA_BLOCK
    fully_past = jnp.arange(nblk)[None, :] < own_blk[:, None]
    gate = jnp.where(fully_past, gate, -jnp.inf)
    _, sel = lax.top_k(gate, topk)

    def to_chunks(t):
        t = t.reshape(B, N_HEADS, n_chunk, MOBA_QCHUNK, t.shape[-1])
        return t.transpose(0, 2, 1, 3, 4).reshape(B * n_chunk, N_HEADS, MOBA_QCHUNK, t.shape[-1])

    q_chunks = to_chunks(q)
    sel_chunks = to_chunks(sel)
    chunk_ids = jnp.arange(B * n_chunk, dtype=jnp.int32)
    n_sel = topk * MOBA_BLOCK

    def one_chunk(args):
        qc, selc, cid = args
        b = cid // n_chunk
        c = cid % n_chunk
        kb = k_blocks[b]
        vb = v_blocks[b]
        qpos = c * MOBA_QCHUNK + jnp.arange(MOBA_QCHUNK)
        ob = (c * MOBA_QCHUNK) // MOBA_BLOCK
        h_idx = jnp.arange(N_HEADS)[:, None, None]
        k_sel = kb[h_idx, selc]
        v_sel = vb[h_idx, selc]
        s_sel = jnp.einsum('hqd,hqnkd->hqnk', qc, k_sel).astype(jnp.float32) * ATTN_SCALE
        valid = jnp.arange(topk) < ob
        s_sel = jnp.where(valid[None, None, :, None], s_sel, -jnp.inf)
        s_sel = s_sel.reshape(N_HEADS, MOBA_QCHUNK, n_sel)
        k_own = lax.dynamic_index_in_dim(kb, ob, axis=1, keepdims=False)
        v_own = lax.dynamic_index_in_dim(vb, ob, axis=1, keepdims=False)
        s_own = jnp.einsum('hqd,hkd->hqk', qc, k_own).astype(jnp.float32) * ATTN_SCALE
        kpos = ob * MOBA_BLOCK + jnp.arange(MOBA_BLOCK)
        s_own = jnp.where((kpos[None, :] <= qpos[:, None])[None], s_own, -jnp.inf)
        p = jax.nn.softmax(jnp.concatenate([s_sel, s_own], axis=-1), axis=-1).astype(v_sel.dtype)
        o = jnp.einsum('hqn,hqnd->hqd', p[..., :n_sel],
                       v_sel.reshape(N_HEADS, MOBA_QCHUNK, n_sel, HEAD_DIM))
        return o + jnp.einsum('hqk,hkd->hqd', p[..., n_sel:], v_own)

    out = lax.map(one_chunk, (q_chunks, sel_chunks, chunk_ids))
    out = out.reshape(B, n_chunk, N_HEADS, MOBA_QCHUNK, HEAD_DIM).transpose(0, 1, 3, 2, 4)
    out = out.reshape(B, s_pad, N_HEADS * HEAD_DIM)[:, :S]
    return out.astype(h.dtype) @ w_o

def conv_ffn(h, w_up, conv_w, conv_b, w_down):
    S = h.shape[1]
    u = h @ w_up
    up = jnp.pad(u, ((0, 0), (CONV_WIDTH - 1, 0), (0, 0)))
    uc = conv_b + sum(conv_w[j] * up[:, j:j + S] for j in range(CONV_WIDTH))
    gate, val = uc[..., :D_FF], uc[..., D_FF:]
    return (jax.nn.silu(gate) * val) @ w_down

def first_inputs(seed: int = 0) -> dict:
    key = jax.random.key(seed)
    ks = jax.random.split(key, 16)
    hd_all = N_HEADS * HEAD_DIM

    def w(k, shape, fan_in):
        return jax.random.normal(k, shape, jnp.float32) * fan_in ** -0.5

    def gain(k, shape):
        return 1.0 + 0.1 * jax.random.normal(k, shape, jnp.float32)

    return {
        'x': jax.random.normal(ks[0], (BATCH, SEQ, D_MODEL), jnp.float32),
        'attn_norm': gain(ks[1], (DEPTH, D_MODEL)),
        'a_w_qkv': w(ks[2], (N_LAYERS_A, D_MODEL, 3 * N_DIL * hd_all), D_MODEL),
        'a_q_norm': gain(ks[3], (N_LAYERS_A, N_DIL, HEAD_DIM)),
        'a_k_norm': gain(ks[4], (N_LAYERS_A, N_DIL, HEAD_DIM)),
        'a_w_o': w(ks[5], (N_LAYERS_A, hd_all, D_MODEL), hd_all),
        'b_w_qkv': w(ks[6], (N_LAYERS_B, D_MODEL, 3 * hd_all), D_MODEL),
        'b_q_norm': gain(ks[7], (N_LAYERS_B, HEAD_DIM)),
        'b_k_norm': gain(ks[8], (N_LAYERS_B, HEAD_DIM)),
        'b_w_o': w(ks[9], (N_LAYERS_B, hd_all, D_MODEL), hd_all),
        'ffn_norm': gain(ks[10], (DEPTH, D_MODEL)),
        'ffn_w_up': w(ks[11], (DEPTH, D_MODEL, 2 * D_FF), D_MODEL),
        'ffn_conv_w': w(ks[12], (DEPTH, CONV_WIDTH, 2 * D_FF), CONV_WIDTH),
        'ffn_conv_b': 0.01 * jax.random.normal(ks[13], (DEPTH, 2 * D_FF), jnp.float32),
        'ffn_w_down': w(ks[14], (DEPTH, D_FF, D_MODEL), D_FF),
    }

def first_block(x, attn_norm, a_w_qkv, a_q_norm, a_k_norm, a_w_o,
              b_w_qkv, b_q_norm, b_k_norm, b_w_o,
              ffn_norm, ffn_w_up, ffn_conv_w, ffn_conv_b, ffn_w_down):
    cos, sin = rope_tables(x.shape[1])
    for i in range(DEPTH):
        hn = rmsnorm(x, attn_norm[i])
        if i % 2 == 0:
            j = i // 2
            x = x + mixer_dilated(hn, a_w_qkv[j], a_q_norm[j], a_k_norm[j], a_w_o[j], cos, sin)
        else:
            j = i // 2
            x = x + mixer_moba(hn, b_w_qkv[j], b_q_norm[j], b_k_norm[j], b_w_o[j], cos, sin)
        hn = rmsnorm(x, ffn_norm[i])
        x = x + conv_ffn(hn, ffn_w_up[i], ffn_conv_w[i], ffn_conv_b[i], ffn_w_down[i])
    return x


DEPTH_2 = 1

ATT_HEADS = 8
HEAD_DIM_2 = 64
D_ATT = ATT_HEADS * HEAD_DIM_2
Q_BLOCK = 128
ATT_SCALE = HEAD_DIM_2 ** -0.5
FORGET_BIAS_MEAN = 2.0
D_CONV = 256
CONV_WIDTH_2 = 31
POOL_WINDOWS = (2, 4, 8, 16)
N_POOL = len(POOL_WINDOWS)
POOL_GROUP = 64
D_POOL = N_POOL * POOL_GROUP
D_MIX = D_ATT + D_CONV + D_POOL
D_IN = 3 * D_ATT + ATT_HEADS + 2 * D_CONV + D_POOL
FFN_CONV_WIDTH = 3
EPS = 1e-6
NEG = -1e30


def rms_norm(x, g):
    xf = x.astype(jnp.float32)
    y = xf * lax.rsqrt(jnp.mean(xf * xf, axis=-1, keepdims=True) + EPS)
    return (y * g.astype(jnp.float32)).astype(x.dtype)

def layer_norm(x, g, b):
    xf = x.astype(jnp.float32)
    mu = jnp.mean(xf, axis=-1, keepdims=True)
    var = jnp.mean(jnp.square(xf - mu), axis=-1, keepdims=True)
    y = (xf - mu) * lax.rsqrt(var + EPS)
    return (y * g.astype(jnp.float32) + b.astype(jnp.float32)).astype(x.dtype)

def causal_depthwise_conv(x, w):
    width, channels = w.shape
    return lax.conv_general_dilated(
        x, w.astype(x.dtype)[:, None, :], window_strides=(1,),
        padding=[(width - 1, 0)], dimension_numbers=('NWC', 'WIO', 'NWC'),
        feature_group_count=channels)

def forgetting_attention(q, k, v, fg_logit):
    B, S, H, Dh = q.shape
    log_f = jax.nn.log_sigmoid(fg_logit.astype(jnp.float32))
    cum = jnp.transpose(jnp.cumsum(log_f, axis=1), (0, 2, 1))
    outs = []
    for start in range(0, S, Q_BLOCK):
        end = start + Q_BLOCK
        qb = q[:, start:end]
        kb = k[:, :end]
        vb = v[:, :end]
        s = jnp.einsum('bqhd,bkhd->bhqk', qb, kb).astype(jnp.float32) * ATT_SCALE
        s = s + cum[:, :, start:end, None] - cum[:, :, None, :end]
        qi = jnp.arange(start, end)[:, None]
        ki = jnp.arange(end)[None, :]
        s = jnp.where(ki <= qi, s, NEG)
        p = jax.nn.softmax(s, axis=-1).astype(vb.dtype)
        outs.append(jnp.einsum('bhqk,bkhd->bqhd', p, vb))
    return jnp.concatenate(outs, axis=1)

def conformer_conv(u, dw_w, dw_b, ln_g, ln_b, pw_w):
    a, b = jnp.split(u, 2, axis=-1)
    h = a * jax.nn.sigmoid(b)
    h = causal_depthwise_conv(h, dw_w) + dw_b.astype(h.dtype)
    h = layer_norm(h, ln_g, ln_b)
    h = jax.nn.silu(h)
    return h @ pw_w.astype(h.dtype)

def multiscale_pool(u, pool_w, pool_scale):
    B, S, _ = u.shape
    uf = u.astype(jnp.float32)
    cs = jnp.cumsum(uf, axis=1)
    pos = jnp.arange(1, S + 1, dtype=jnp.float32)[:, None]
    diffs = []
    for g, w in enumerate(POOL_WINDOWS):
        sl = slice(g * POOL_GROUP, (g + 1) * POOL_GROUP)
        c = cs[..., sl]
        prev = jnp.pad(c, ((0, 0), (w, 0), (0, 0)))[:, :S]
        mean = (c - prev) / jnp.minimum(pos, float(w))
        diffs.append(mean - uf[..., sl])
    d = jnp.stack(diffs, axis=2)
    y = jnp.einsum('bsgc,gcd->bsgd', d, pool_w.astype(jnp.float32))
    y = y.reshape(B, S, D_POOL) * pool_scale.astype(jnp.float32)
    return y.astype(u.dtype)

def second_inputs(seed: int = 0) -> dict:
    key = jax.random.key(seed)
    ks = jax.random.split(key, 20)
    f32 = jnp.float32
    L = DEPTH_2

    def nrm(k, shape, scale):
        return jax.random.normal(k, shape, f32) * scale

    return {
        'x': nrm(ks[0], (BATCH, SEQ, D_MODEL), 1.0),
        'norm1_g': 1.0 + nrm(ks[1], (L, D_MODEL), 0.02),
        'w_in': nrm(ks[2], (L, D_MODEL, D_IN), D_MODEL ** -0.5),
        'b_f': FORGET_BIAS_MEAN + nrm(ks[3], (L, ATT_HEADS), 0.5),
        'q_norm_g': 1.0 + nrm(ks[4], (L, HEAD_DIM_2), 0.02),
        'k_norm_g': 1.0 + nrm(ks[5], (L, HEAD_DIM_2), 0.02),
        'conv_dw_w': nrm(ks[6], (L, CONV_WIDTH_2, D_CONV), CONV_WIDTH_2 ** -0.5),
        'conv_dw_b': nrm(ks[7], (L, D_CONV), 0.02),
        'conv_ln_g': 1.0 + nrm(ks[8], (L, D_CONV), 0.02),
        'conv_ln_b': nrm(ks[9], (L, D_CONV), 0.02),
        'conv_pw_w': nrm(ks[10], (L, D_CONV, D_CONV), D_CONV ** -0.5),
        'pool_w': nrm(ks[11], (L, N_POOL, POOL_GROUP, POOL_GROUP), POOL_GROUP ** -0.5),
        'pool_scale': 1.0 + nrm(ks[12], (L, D_POOL), 0.1),
        'w_out': nrm(ks[13], (L, D_MIX, D_MODEL), D_MIX ** -0.5),
        'norm2_g': 1.0 + nrm(ks[14], (L, D_MODEL), 0.02),
        'w_up': nrm(ks[15], (L, D_MODEL, 2 * D_FF), D_MODEL ** -0.5),
        'ffn_dw_w': nrm(ks[16], (L, FFN_CONV_WIDTH, 2 * D_FF), FFN_CONV_WIDTH ** -0.5),
        'w_down': nrm(ks[17], (L, D_FF, D_MODEL), D_FF ** -0.5),
    }

def second_block(x, norm1_g, w_in, b_f, q_norm_g, k_norm_g, conv_dw_w, conv_dw_b,
              conv_ln_g, conv_ln_b, conv_pw_w, pool_w, pool_scale, w_out,
              norm2_g, w_up, ffn_dw_w, w_down):
    B, S, _ = x.shape
    for l in range(DEPTH_2):
        h = rms_norm(x, norm1_g[l])
        proj = h @ w_in[l].astype(h.dtype)
        o = 0
        q = proj[..., o:o + D_ATT]; o += D_ATT
        k = proj[..., o:o + D_ATT]; o += D_ATT
        v = proj[..., o:o + D_ATT]; o += D_ATT
        fg = proj[..., o:o + ATT_HEADS]; o += ATT_HEADS
        conv_in = proj[..., o:o + 2 * D_CONV]; o += 2 * D_CONV
        pool_in = proj[..., o:o + D_POOL]

        q = rms_norm(q.reshape(B, S, ATT_HEADS, HEAD_DIM_2), q_norm_g[l])
        k = rms_norm(k.reshape(B, S, ATT_HEADS, HEAD_DIM_2), k_norm_g[l])
        v = v.reshape(B, S, ATT_HEADS, HEAD_DIM_2)
        fg = fg + b_f[l].astype(fg.dtype)
        att = forgetting_attention(q, k, v, fg).reshape(B, S, D_ATT)

        conv = conformer_conv(conv_in, conv_dw_w[l], conv_dw_b[l],
                              conv_ln_g[l], conv_ln_b[l], conv_pw_w[l])
        pool = multiscale_pool(pool_in, pool_w[l], pool_scale[l])

        mix = jnp.concatenate([att, conv, pool], axis=-1)
        x = x + mix @ w_out[l].astype(mix.dtype)

        h2 = rms_norm(x, norm2_g[l])
        up = h2 @ w_up[l].astype(h2.dtype)
        up = causal_depthwise_conv(up, ffn_dw_w[l])
        gate, val = jnp.split(up, 2, axis=-1)
        x = x + (jax.nn.silu(gate) * val) @ w_down[l].astype(up.dtype)
    return x


def setup_inputs(seed=0):
    out = dict(first_inputs(seed))
    for name, value in second_inputs(seed + 1).items():
        if name != "x":
            out[name + "_2"] = value
    return out


def reference(
    x, attn_norm, a_w_qkv, a_q_norm, a_k_norm, a_w_o, b_w_qkv, b_q_norm, b_k_norm, b_w_o,
    ffn_norm, ffn_w_up, ffn_conv_w, ffn_conv_b, ffn_w_down, norm1_g_2, w_in_2, b_f_2,
    q_norm_g_2, k_norm_g_2, conv_dw_w_2, conv_dw_b_2, conv_ln_g_2, conv_ln_b_2, conv_pw_w_2,
    pool_w_2, pool_scale_2, w_out_2, norm2_g_2, w_up_2, ffn_dw_w_2, w_down_2,
):
    x = first_block(
        x, attn_norm, a_w_qkv, a_q_norm, a_k_norm, a_w_o, b_w_qkv, b_q_norm, b_k_norm, b_w_o,
        ffn_norm, ffn_w_up, ffn_conv_w, ffn_conv_b, ffn_w_down,
    )
    return second_block(
        x, norm1_g_2, w_in_2, b_f_2, q_norm_g_2, k_norm_g_2, conv_dw_w_2, conv_dw_b_2,
        conv_ln_g_2, conv_ln_b_2, conv_pw_w_2, pool_w_2, pool_scale_2, w_out_2, norm2_g_2,
        w_up_2, ffn_dw_w_2, w_down_2,
    )


_drawn_inputs = setup_inputs


def setup_inputs(seed=0):
    import zlib

    import numpy as np

    out = dict(_drawn_inputs(seed))
    spreads = {}
    factors = {'b_q_norm': 3.173,
     'b_k_norm': 3.525,
     'ffn_conv_b': 4.743,
     'norm1_g_2': 5.416,
     'q_norm_g_2': 8.0,
     'k_norm_g_2': 8.0,
     'conv_dw_b_2': 6.513,
     'conv_ln_g_2': 33.474,
     'conv_ln_b_2': 34.803,
     'norm2_g_2': 5.31}
    for name, (base, spread) in spreads.items():
        noise = np.random.default_rng([zlib.crc32(name.encode()), seed]).standard_normal(out[name].shape)
        drawn = base * np.exp(spread * noise) if base else spread * noise
        out[name] = __import__('jax').numpy.asarray(drawn.astype(out[name].dtype))
    for name, factor in factors.items():
        out[name] = (out[name] * factor).astype(out[name].dtype)
    return out
```

```python
import itertools

import numpy as np

import concourse.bass as bass
from concourse import mybir
from concourse.alu_op_type import AluOpType as ALU

P = 128
D = 1024
TOK = 256
KT = D // P
HEADS_A = 16
HD = 64
NDIL = 3
DILATED_PAIRS = ((128, 1), (512, 4), (2048, 16))
ROPE_DIM = HD // 4
ROPE_THETA = 500000.0
PAIRS_AB = HEADS_A // 2
HEADS_C = 8
PAIRS_C = HEADS_C // 2
D_FF = 2816
FT = D_FF // P
CONV_C = 31
PADC = CONV_C - 1
POOL_PAD = 16
POOL_WINDOWS = (2, 4, 8, 16)
EPS = 1e-6
NEG = -1e30
RING = 6
AHEAD = 3
AHEAD_HI = AHEAD + 1
CHUNK = KT * P

A_QKV = 0
A_OUT = A_QKV + 3 * NDIL * PAIRS_AB
A_FFN = A_OUT + KT
B_QKV = A_FFN + 3 * FT
B_OUT = B_QKV + 3 * PAIRS_AB
B_FFN = B_OUT + KT
C_PRE = B_FFN + 3 * FT
N_PRE = 7
C_QKV = C_PRE + N_PRE
C_OUT = C_QKV + 3 * PAIRS_C
C_FFN = C_OUT + KT
N_CHUNKS = C_FFN + 3 * FT

PAR_NORM = 0
PAR_GAIN = PAR_NORM + 6 * KT
PAR_SWAP = PAR_GAIN + 2 * NDIL + 4
PAR_FFN = PAR_SWAP + 2 * NDIL + 2
PAR_DW = PAR_FFN + 3 * FT * 8
PAR_DWB = PAR_DW + 2 * CONV_C
PAR_LNG = PAR_DWB + 2
PAR_LNB = PAR_LNG + 2
PAR_PSC = PAR_LNB + 2
PAR_BF = PAR_PSC + 2
PAR_POOLW = PAR_BF + 1
PAR_PW = PAR_POOLW + 2 * HD
N_PAR = PAR_PW + 2 * 2 * P

CON_ID = 0
CON_ONES = CON_ID + P
CON_BLK = CON_ONES + P
CON_EPS = CON_BLK + P
CON_COS = CON_EPS + 2
CON_SIN = CON_COS + TOK
CON_MASKA = CON_SIN + TOK
CON_MASK1 = CON_MASKA + 3 * NDIL * P
CON_INV = CON_MASK1 + 3 * P
N_CON = CON_INV + 2 * TOK


def shape_constants():
    con = np.zeros((P, N_CON), np.float32)
    pos = np.arange(TOK, dtype=np.float32)
    inv_freq = np.float32(ROPE_THETA) ** (-np.arange(0, ROPE_DIM, 2, dtype=np.float32) / np.float32(ROPE_DIM))
    ang = (pos[:, None] * inv_freq[None, :]).astype(np.float32)
    cos, sin = np.cos(ang).T, np.sin(ang).T
    half = ROPE_DIM // 2
    con[:, CON_COS:CON_COS + TOK] = 1.0
    for b in (0, HD):
        con[b:b + half, CON_COS:CON_COS + TOK] = cos
        con[b + half:b + ROPE_DIM, CON_COS:CON_COS + TOK] = cos
        con[b:b + half, CON_SIN:CON_SIN + TOK] = -sin
        con[b + half:b + ROPE_DIM, CON_SIN:CON_SIN + TOK] = sin

    def mask(window, dil, qt, keys):
        d = (qt * P + np.arange(P))[:, None] - np.arange(keys)[None, :]
        ok = (d >= 0) & (d <= window) & (d % dil == 0)
        return np.where(ok, 0.0, NEG)

    o = CON_MASKA
    for qt in range(2):
        for w, d in DILATED_PAIRS:
            con[:, o:o + (qt + 1) * P] = mask(w, d, qt, (qt + 1) * P)
            o += (qt + 1) * P
    o = CON_MASK1
    for qt in range(2):
        con[:, o:o + (qt + 1) * P] = mask(TOK, 1, qt, (qt + 1) * P)
        o += (qt + 1) * P
    con[:, CON_ID:CON_ID + P] = np.eye(P)
    con[:, CON_ONES:CON_ONES + P] = 1.0
    for b in (0, HD):
        con[b:b + HD, CON_BLK + b:CON_BLK + b + HD] = 1.0
    for g, w in enumerate(POOL_WINDOWS):
        b = HD * (g % 2)
        con[b:b + HD, CON_INV + (g // 2) * TOK:CON_INV + (g // 2 + 1) * TOK] = 1.0 / np.minimum(pos + 1, w)
    con[:, CON_EPS] = EPS
    con[:, CON_EPS + 1] = HD * EPS
    return con


def build(nc, x_d, stream_d, par_d, con_d, out_d):
    F32 = mybir.dt.float32
    F32R = mybir.dt.float32r
    BF16 = mybir.dt.bfloat16
    ACT = mybir.ActivationFunctionType
    ds = bass.ds

    def sb(name, shape, dt=F32):
        return nc.alloc_sbuf_tensor(name, shape, dt)

    def sem(name):
        return nc.alloc_semaphore(name)

    w_raw = [sb(f"w_raw{s}", [P, CHUNK]) for s in range(RING)]
    w_hi = [sb(f"w_hi{s}", [P, CHUNK], F32R) for s in range(RING)]
    w_lo = [sb(f"w_lo{s}", [P, CHUNK], F32R) for s in range(RING)]
    xT = sb("xT", [P, KT, TOK])
    xg_hi = sb("xg_hi", [P, KT, TOK], F32R)
    xg_lo = sb("xg_lo", [P, KT, TOK], F32R)
    mix_hi = sb("mix_hi", [P, KT, TOK], F32R)
    mix_lo = sb("mix_lo", [P, KT, TOK], F32R)
    par = sb("par", [P, N_PAR])
    con = sb("con", [P, N_CON])
    zero = sb("zero", [P, 512], BF16)
    ln_x = sb("ln_x", [P, TOK])
    rms_r = sb("rms_r", [P, TOK])
    rope_t = sb("rope_t", [P, 2 * NDIL, 2, TOK])
    rope_b = sb("rope_b", [P, 2, 2, TOK])
    qk_raw = [sb(f"qk_raw{r}", [P, TOK]) for r in range(2)]
    qk_sq = [sb(f"qk_sq{r}", [P, TOK]) for r in range(2)]
    qk_swap = [sb(f"qk_swap{r}", [P, TOK]) for r in range(2)]
    qk_rope = [sb(f"qk_rope{r}", [P, TOK]) for r in range(2)]
    qk_r = [sb(f"qk_r{r}", [P, TOK]) for r in range(2)]
    rope_1 = sb("rope_1", [P, TOK])
    rope_2 = sb("rope_2", [P, TOK])
    v_t = sb("v_t", [P, TOK])
    sqx = qk_sq + qk_swap + qk_rope + [rope_1, rope_2]
    qk_n = [[[sb(f"qk_n{b}{g}{r}", [P, TOK]) for r in range(2)] for g in range(NDIL)] for b in range(2)]
    v_n = [[sb(f"v_n{b}{g}", [P, 2, P]) for g in range(NDIL)] for b in range(2)]
    prob = [sb(f"prob{h}", [P, 3 * NDIL * P]) for h in range(2)]
    prob_t = [sb(f"prob_t{h}", [P, NDIL, 3 * P]) for h in range(2)]
    smax = [sb(f"smax{h}", [P, 2]) for h in range(2)]
    nmax = [sb(f"nmax{h}", [P, 2]) for h in range(2)]
    ssum = [sb(f"ssum{h}", [P, 2]) for h in range(2)]
    rsum = [sb(f"rsum{h}", [P, 2]) for h in range(2)]
    scratch = sb("scratch", [P, 64])
    scratch_col = itertools.count()
    up_s = [[qk_n[b][1][s] for s in range(2)] for b in range(2)]
    cv_s = [[qk_n[b][2][s] for s in range(2)] for b in range(2)]
    gate_s, gated = qk_raw
    g_hi = [sb(f"g_hi{b}", [P, TOK], F32R) for b in range(2)]
    g_lo = [sb(f"g_lo{b}", [P, TOK], F32R) for b in range(2)]
    bias_k = rope_t[0:HEADS_C, 0:4].rearrange("p a b t -> p (a b t)")
    fg = [rope_t[0:HEADS_C, 4 + n // 2, n % 2, :] for n in range(4)] + [rope_b[0:HEADS_C, 0, n, :] for n in range(2)]
    cv_a = [qk_n[0][1][i] for i in range(2)]
    cv_b = [qk_n[0][2][i] for i in range(2)]
    cv_e = [qk_n[1][1][i] for i in range(2)]
    cv_acc = [qk_n[1][2][i] for i in range(2)]
    cv_h = [sb(f"cv_h{i}", [P, PADC + TOK]) for i in range(2)]
    W_PL = POOL_PAD + TOK
    prob_t_flat = [prob_t[h][:].rearrange("p g c -> p (g c)") for h in range(2)]
    pl = [[prob[i][:, 3 * P:3 * P + W_PL], prob[i][:, 3 * P + W_PL:3 * P + 2 * W_PL],
           prob_t_flat[i][:, 3 * P:3 * P + W_PL]] for i in range(2)]

    ps = nc.alloc_psum_tensor("ps", [P, 8 * 512], F32)

    def bank(b, lo=0, n=TOK):
        return ps[:, b * 512 + lo:b * 512 + lo + n]

    SS = 3

    w_loaded = [sem(f"w_loaded{s}") for s in range(RING)]
    w_hi_done = sem("w_hi_done")
    w_lo_done = sem("w_lo_done")
    tiles = sem("tiles")
    x_in = sem("x_in")
    par_in = sem("par_in")
    con_in = sem("con_in")
    rest_in = sem("rest_in")
    pl_zeroed = sem("pl_zeroed")
    zeroed = sem("zeroed")
    acc_done = sem("acc_done")
    x_new = sem("x_new")
    x_sq = sem("x_sq")
    x_hi = sem("x_hi")
    x_lo = sem("x_lo")
    x_ss = sem("x_ss")
    x_ln = sem("x_ln")
    x_r = sem("x_r")
    tables = sem("tables")
    stored = sem("stored")

    class Att:

        def __init__(self, n):
            self.raw = sem(f"{n}_raw")
            self.sq = sem(f"{n}_sq")
            self.swap = sem(f"{n}_swap")
            self.rot1 = sem(f"{n}_rot1")
            self.rot2 = sem(f"{n}_rot2")
            self.rope = sem(f"{n}_rope")
            self.aux = sem(f"{n}_aux")
            self.auxr = sem(f"{n}_auxr")
            self.r = sem(f"{n}_r")
            self.qn = sem(f"{n}_qn")
            self.score = sem(f"{n}_score")
            self.mx = sem(f"{n}_mx")
            self.masked = sem(f"{n}_masked")
            self.expd = sem(f"{n}_expd")
            self.rs = sem(f"{n}_rs")
            self.pn = sem(f"{n}_pn")
            self.pt = sem(f"{n}_pt")
            self.ptr = sem(f"{n}_ptr")
            self.pv = sem(f"{n}_pv")
            self.ohi = sem(f"{n}_ohi")
            self.olo = sem(f"{n}_olo")

    class Ffn:

        def __init__(self, n):
            self.up = sem(f"{n}_up")
            self.tap0 = sem(f"{n}_tap0")
            self.tap1 = sem(f"{n}_tap1")
            self.conv = sem(f"{n}_conv")
            self.silu = sem(f"{n}_silu")
            self.gated = sem(f"{n}_gated")
            self.ghi = sem(f"{n}_ghi")
            self.glo = sem(f"{n}_glo")

    att = [Att("aA"), Att("aB"), Att("aC")]
    ffn = [Ffn("fA"), Ffn("fB"), Ffn("fC")]
    pre_out = sem("pre_out")
    pre_act = sem("pre_act")
    pre_dve = sem("pre_dve")
    pre_pool = sem("pre_pool")
    tap = sem("tap")
    tap_pool = sem("tap_pool")
    bias_in = sem("bias_in")
    ln_pe = sem("ln_pe")
    ln_dve = sem("ln_dve")
    ln_act = sem("ln_act")
    side_lo = sem("side_lo")

    def at(base, per, i):
        return base if i is None else base + per * i

    def past(eng, s, base, per, i):
        if i is not None or base > 0:
            eng.wait_ge(s, at(base, per, i))

    def own_wait(i):
        if i is not None:
            n = next(scratch_col) % 64
            nc.vector.memset(scratch[:, n:n + 1], 0.0)

    def split_hi(eng, c, per, i):
        c = c + AHEAD_HI
        if i is None and c >= N_CHUNKS:
            return
        s = c % RING
        eng.wait_ge(w_loaded[s], at(16 * (c // RING + 1), 16 * per // RING, i))
        past(eng, tiles, c - RING + 1, per, i)
        nc.scalar.activation(w_hi[s][:], w_raw[s][:], ACT.Copy).then_inc(w_hi_done, 1)

    def split_lo(eng, c, per, i):
        c = c + AHEAD
        if i is None and c >= N_CHUNKS:
            return
        s = c % RING
        eng.wait_ge(w_hi_done, at(c + 1, per, i))
        nc.vector.tensor_tensor(w_lo[s][:], w_raw[s][:], w_hi[s][:].bitcast(F32),
                                ALU.subtract).then_inc(w_lo_done, 1)

    def project(eng, c, per, i, out, hi, lo, split_of=None):
        s = c % RING
        eng.wait_ge(w_lo_done, at(c + 1, per, i))
        for k in range(KT):
            if split_of is not None:
                eng.wait_ge(x_lo, KT * split_of + k + 1)
            wh, wl = w_hi[s][:, k * P:(k + 1) * P], w_lo[s][:, k * P:(k + 1) * P]
            nc.tensor.matmul(out, wh, hi[:, k, :], start=(k == 0), stop=False)
            nc.tensor.matmul(out, wh, lo[:, k, :], start=False, stop=False)
            last = nc.tensor.matmul(out, wl, hi[:, k, :], start=False, stop=(k == KT - 1))
            if k == KT - 1:
                last.then_inc(tiles, 1)
            if split_of is not None:
                resid_pe(eng, split_of, k)

    def resid_dve_add(eng, m, src, c):
        eng.wait_ge(tiles, c + 1)
        nc.vector.tensor_tensor(xT[:, m, :], src, xT[:, m, :], ALU.add).then_inc(x_new, 1)

    def resid_act(eng, e, m):
        if e == 0:
            eng.wait_ge(x_in, 16 * (1 + m // (KT // 2)))
            eng.wait_ge(par_in, 16)
        else:
            eng.wait_ge(x_new, KT * (e - 1) + m + 1)
        g = PAR_NORM + KT * e + m
        nc.scalar.activation(xg_hi[:, m, :], xT[:, m, :], ACT.Copy, scale=par[:, g:g + 1]).then_inc(x_hi, 1)
        nc.scalar.activation(sqx[m][:], xT[:, m, :], ACT.Square).then_inc(x_sq, 1)

    def resid_dve_lo(eng, e, m):
        eng.wait_ge(x_hi, KT * e + m + 1)
        if e == 0:
            eng.wait_ge(x_in, 16 * (1 + m // (KT // 2)))
        g = PAR_NORM + KT * e + m
        nc.vector.scalar_tensor_tensor(xg_lo[:, m, :], xT[:, m, :], par[:, g:g + 1], xg_hi[:, m, :].bitcast(F32),
                                       ALU.mult, ALU.subtract).then_inc(x_lo, 1)

    def resid_pe(eng, e, m):
        eng.wait_ge(x_sq, KT * e + m + 1)
        nc.tensor.matmul(bank(SS), con[:, CON_ONES:CON_ONES + P], sqx[m][:],
                         start=(m == 0), stop=(m == KT - 1)).then_inc(x_ss, 1)

    def resid_act_r(eng, e):
        eng.wait_ge(x_ss, KT * (e + 1))
        eng.wait_ge(con_in, 16)
        nc.scalar.activation(ln_x[:], bank(SS), ACT.Ln, scale=1.0 / D, bias=con[:, CON_EPS:CON_EPS + 1]).then_inc(x_ln, 1)
        eng.wait_ge(x_ln, e + 1)
        nc.scalar.activation(rms_r[:], ln_x[:], ACT.Exp, scale=-0.5).then_inc(x_r, 1)

    EVENTS3 = dict(
        pe=(("S0", 2), ("T0", 5), ("S1", 6), ("T1", 9), ("PV", 10)),
        dve=(("S0", 3), ("N0", 5), ("S1", 7), ("N1", 9), ("X", 12)),
        act=(("S0", 4), ("E0", 6), ("S1", 8), ("E1", 10), ("X", 11)),
        pool=())
    EVENTS1 = dict(
        pe=(("S0", 2), ("S1", 2), ("T0", 5), ("T1", 5), ("PV", 6)),
        dve=(("S0", 3), ("S1", 3), ("N0", 5), ("N1", 5), ("X", 8)),
        act=(("S0", 4), ("S1", 4), ("E0", 6), ("E1", 6), ("X", 7)),
        pool=())
    STAGES = [
        dict(c0=A_QKV, nd=NDIL, pairs=PAIRS_AB, events=EVENTS3, norm=0, rope=rope_t, gain=PAR_GAIN, mask=CON_MASKA),
        dict(c0=B_QKV, nd=1, pairs=PAIRS_AB, events=EVENTS1, norm=2, rope=rope_b, gain=PAR_GAIN + 2 * NDIL, mask=CON_MASK1),
        dict(c0=C_QKV, nd=1, pairs=PAIRS_C, events=EVENTS1, norm=4, rope=None, gain=PAR_GAIN + 2 * NDIL + 2, mask=CON_MASK1),
    ]

    def att_stage(eng, who, st, tile, event, after=None):
        S = STAGES[st]
        T, pairs = 3 * S["nd"], S["pairs"]
        every = [o for evs in S["events"].values() for _, o in evs]
        reach = 1 + max(every) // T

        def window(w, per, i):
            for t in range(T):
                tile(eng, st, w * T + t, per * T, i)
                here = sorted((-(o // T), x) for x, (_, o) in enumerate(S["events"][who]) if o % T == t)
                for late, x in here:
                    pr = w - 1 + late
                    if 0 <= pr < pairs:
                        event(eng, st, S["events"][who][x][0], pr, per, i)
                if after is not None and w >= pairs:
                    after((w - pairs) * T + t)

        for w in range(reach):
            window(w, 0, None)
        turns = (pairs - reach) // 2
        if turns:
            with eng.Fori(0, turns) as i:
                for u in range(2):
                    window(reach + u, 2, i)
        for w in range(reach + 2 * turns, pairs + reach):
            window(w, 0, None)

    def kind(S, n):
        T = 3 * S["nd"]
        return n % 3, (n % T) // 3, (n // T) % 2, n - n // 3 if n % 3 < 2 else None

    def qk_no(n):
        return 2 * (n // 3) + n % 3

    def score_out(S, h, qt, g):
        if S["nd"] == 1:
            o = (3 + h) * 512 + (0, P)[qt]
        else:
            o = 3 * 512 + (g * P if qt == 0 else 512 + g * 2 * P)
        return ps[:, o:o + (qt + 1) * P]

    def score_all(S, h, qt):
        w = S["nd"] * P * (qt + 1)
        o = (3 + h) * 512 + (0, P)[qt] if S["nd"] == 1 else (3 + qt) * 512
        return ps[:, o:o + w]

    def prob_cols(S, qt):
        w = S["nd"] * P
        return (0, w) if qt == 0 else (w, 3 * w)

    def pt_bank(S, h, g):
        return 5 + h if S["nd"] == 1 else 3 + g

    def pv_out(S, b):
        return (7 * 512 + b * TOK) if S["nd"] == 1 else (6 + b) * 512

    def aux_out(m, lo=0, n=TOK):
        return bank((m + 1) % 3, TOK + lo, n)

    def pe_tile(eng, st, n, per, i):
        S, a = STAGES[st], att[st]
        N = 3 * S["nd"] * S["pairs"]
        if i is not None or n < N:
            past(eng, a.raw, n - 2, per, i)
            past(eng, a.auxr, n - 3, per, i)
            project(eng, S["c0"] + n, per, i, bank(n % 3), xg_hi, xg_lo, S["norm"] if n == 0 and i is None and st < 2 else None)
        m = n - 2
        if i is None and (m < 0 or m >= N):
            return
        role = m % 3
        eng.wait_ge(a.raw, at(m + 2 if i is not None else min(m + 2, N), per, i))
        if role < 2:
            eng.wait_ge(a.sq, at(qk_no(m) + 1, per * 2 // 3, i))
            nc.tensor.matmul(aux_out(m), con[:, CON_BLK:CON_BLK + P], qk_sq[role][:],
                             start=True, stop=True).then_inc(a.aux, 1)
        else:
            for tt in range(2):
                last = nc.tensor.transpose(aux_out(m, tt * P, P), v_t[:, tt * P:(tt + 1) * P],
                                           con[:, CON_ID:CON_ID + P])
            last.then_inc(a.aux, 1)

    def pe_event(eng, st, what, pr, per, i):
        S, a = STAGES[st], att[st]
        nd, T, b = S["nd"], 3 * S["nd"], pr % 2
        if what[0] == "S":
            h = int(what[1])
            lo, hi = HD * h, HD * h + HD
            eng.wait_ge(a.qn, at(2 * nd * (pr + 1), 2 * nd * per, i))
            if nd > 1 and h == 1:
                eng.wait_ge(a.ptr, at(2 * pr + 1, 2 * per, i))
            if st == 2:
                eng.wait_ge(bias_in, 1)
            for qt in range(2):
                for g in range(nd):
                    q, k = qk_n[b][g]
                    out = score_out(S, h, qt, g)
                    last = nc.tensor.matmul(out, q[lo:hi, qt * P:(qt + 1) * P], k[lo:hi, 0:(qt + 1) * P],
                                            start=True, stop=(st < 2))
                    if st == 2:
                        last = nc.tensor.matmul(out, con[0:HEADS_C, CON_ONES:CON_ONES + P],
                                                bias_k[:, ds(at((2 * pr + h) * TOK, 2 * per * TOK, i), (qt + 1) * P)],
                                                start=False, stop=True)
            last.then_inc(a.score, 1)
        elif what[0] == "T":
            h = int(what[1])
            eng.wait_ge(a.pn, at(2 * pr + h + 1, 2 * per, i))
            w = nd * P
            for g in range(nd):
                bk = pt_bank(S, h, g)
                for n, o in enumerate((g * P, w + g * 2 * P, w + g * 2 * P + P)):
                    last = nc.tensor.transpose(bank(bk, n * P, P), prob[h][:, o:o + P], con[:, CON_ID:CON_ID + P])
            last.then_inc(a.pt, 1)
        elif what == "PV":
            eng.wait_ge(a.ptr, at(2 * pr + 2, 2 * per, i))
            eng.wait_ge(a.auxr, at(T * pr + T, T * per, i))
            if nd == 1:
                past(eng, a.olo, pr, per, i)
            for g in range(nd):
                for kt, q0 in ((0, 0), (1, P)):
                    for h in range(2):
                        lo, hi = HD * h, HD * h + HD
                        last = nc.tensor.matmul(ps[lo:hi, pv_out(S, b) + q0:pv_out(S, b) + TOK],
                                                v_n[b][g][:, kt, lo:hi],
                                                prob_t[h][:, g, 2 * P * kt:2 * P * kt + TOK - q0],
                                                start=(g == 0 and kt == 0), stop=(g == nd - 1 and kt == 1),
                                                skip_group_check=True)
            last.then_inc(a.pv, 1)

    def act_tile(eng, st, n, per, i):
        S, a = STAGES[st], att[st]
        N = 3 * S["nd"] * S["pairs"]
        if i is not None or n < N + RING - AHEAD_HI:
            split_hi(eng, S["c0"] + n, per, i)
        if n == 1 and st < 2:
            resid_act_r(eng, S["norm"])
        m = n - 1
        if (i is not None or 0 <= m < N) and m % 3 < 2:
            eng.wait_ge(a.raw, at(m + 1, per, i))
            nc.scalar.activation(qk_sq[m % 3][:], qk_raw[m % 3][:], ACT.Square).then_inc(a.sq, 1)
        m = n - 3
        if i is None and (m < 0 or m >= N):
            return
        role, g, b, _ = kind(S, m)
        eng.wait_ge(a.aux, at(m + 1, per, i))
        if role < 2:
            e = CON_EPS + 1 - role
            nc.scalar.activation(qk_r[role][:], aux_out(m), ACT.Ln, scale=(1.0, 1.0 / HD)[role],
                                 bias=con[:, e:e + 1]).then_inc(a.auxr, 1)
            eng.wait_ge(a.auxr, at(m + 1, per, i))
            nc.scalar.activation(qk_r[role][:], qk_r[role][:], ACT.Exp, scale=-0.5).then_inc(a.r, 1)
        else:
            nc.scalar.activation(v_n[b][g][:], aux_out(m).rearrange("p (t c) -> p t c", t=2),
                                 ACT.Copy).then_inc(a.auxr, 1)

    def act_event(eng, st, what, pr, per, i):
        S, a = STAGES[st], att[st]
        nd, b = S["nd"], pr % 2
        if what[0] == "S":
            h = int(what[1])
            eng.wait_ge(a.masked, at(2 * pr + h + 1, 2 * per, i))
            for qt in range(2):
                o0, o1 = prob_cols(S, qt)
                last = nc.scalar.activation(prob[h][:, o0:o1], prob[h][:, o0:o1], ACT.Exp, bias=nmax[h][:, qt:qt + 1],
                                            accum_out=ssum[h][:, qt:qt + 1])
            last.then_inc(a.expd, 1)
        elif what[0] == "E":
            h = int(what[1])
            eng.wait_ge(a.pt, at(2 * pr + h + 1, 2 * per, i))
            b0 = pt_bank(S, h, 0) * 512
            nc.scalar.activation(prob_t[h][:, 0:nd, :],
                                 ps[:, b0:b0 + nd * 512].rearrange("p (g c) -> p g c", c=512)[:, :, 0:3 * P],
                                 ACT.Copy).then_inc(a.ptr, 1)
        elif what == "X":
            eng.wait_ge(a.pv, at(pr + 1, per, i))
            nc.scalar.activation(mix_hi[:, ds(at(pr, per, i), 1), :], ps[:, pv_out(S, b):pv_out(S, b) + TOK].rearrange("p (o t) -> p o t", o=1),
                                 ACT.Copy).then_inc(a.ohi, 1)

    SWAP = [p + ROPE_DIM // 2 if p < ROPE_DIM // 2 else p - ROPE_DIM // 2 if p < ROPE_DIM else p for p in range(32)]

    def dve_tile(eng, st, n, per, i):
        S, a = STAGES[st], att[st]
        N = 3 * S["nd"] * S["pairs"]
        if i is not None or n < N + RING - AHEAD:
            split_lo(eng, S["c0"] + n, per, i)
        m = n - 4
        if (i is not None or 0 <= m < N) and m % 3 < 2:
            role, g, b, _ = kind(S, m)
            eng.wait_ge(a.r, at(qk_no(m) + 1, per * 2 // 3, i))
            if S["rope"] is not None:
                eng.wait_ge(a.rope, at(qk_no(m) + 1, per * 2 // 3, i))
                nc.vector.tensor_tensor(qk_n[b][g][role][:], qk_rope[role][:], qk_r[role][:], ALU.mult).then_inc(a.qn, 1)
            else:
                c = S["gain"] + role
                nc.vector.scalar_tensor_tensor(qk_n[b][g][role][:], qk_raw[role][:], par[:, c:c + 1], qk_r[role][:],
                                               ALU.mult, ALU.mult).then_inc(a.qn, 1)
        m = n - 1
        if i is not None or 0 <= m < N:
            role = m % 3
            eng.wait_ge(tiles, at(S["c0"] + m + 1, per, i))
            if m == 0 and i is None:
                eng.wait_ge(x_r, S["norm"] + 1)
            if S["rope"] is None and role < 2 and m >= 3:
                eng.wait_ge(a.qn, at(qk_no(m - 3) + 1, per * 2 // 3, i))
            nc.vector.tensor_tensor((qk_raw + [v_t])[role][:], bank(m % 3), rms_r[:], ALU.mult).then_inc(a.raw, 1)
            if role < 2 and S["rope"] is not None:
                eng.wait_ge(a.raw, at(m + 1, per, i))
                own_wait(i)
                nc.vector.stream_shuffle(qk_swap[role][:], qk_raw[role][:], SWAP).then_inc(a.swap, 1)
        if st == 2:
            conv_taps(eng, n)

    def dve_event(eng, st, what, pr, per, i):
        S, a = STAGES[st], att[st]
        b = pr % 2
        if what[0] == "S":
            h = int(what[1])
            eng.wait_ge(a.score, at(2 * pr + h + 1, 2 * per, i))
            own_wait(i)
            mo = S["mask"]
            if st == 0 and i is None and pr == 0:
                eng.wait_ge(rest_in, 32)
            for qt in range(2):
                o0, o1 = prob_cols(S, qt)
                last = nc.vector.tensor_tensor_reduce(prob[h][:, o0:o1], score_all(S, h, qt), con[:, mo + o0:mo + o1],
                                                      1.0, NEG, ALU.add, ALU.max, smax[h][:, qt:qt + 1])
            last.then_inc(a.mx, 1)
            eng.wait_ge(a.mx, at(2 * pr + h + 1, 2 * per, i))
            nc.vector.tensor_scalar(nmax[h][:], smax[h][:], -1.0, None, ALU.mult).then_inc(a.masked, 1)
        elif what[0] == "N":
            h = int(what[1])
            eng.wait_ge(a.expd, at(2 * pr + h + 1, 2 * per, i))
            nc.vector.reciprocal(rsum[h][:], ssum[h][:]).then_inc(a.rs, 1)
            eng.wait_ge(a.rs, at(2 * pr + h + 1, 2 * per, i))
            for qt in range(2):
                o0, o1 = prob_cols(S, qt)
                last = nc.vector.tensor_scalar(prob[h][:, o0:o1], prob[h][:, o0:o1], rsum[h][:, qt:qt + 1], None, ALU.mult)
            last.then_inc(a.pn, 1)
        elif what == "X":
            eng.wait_ge(a.ohi, at(pr + 1, per, i))
            nc.vector.tensor_tensor(mix_lo[:, ds(at(pr, per, i), 1), :], ps[:, pv_out(S, b):pv_out(S, b) + TOK].rearrange("p (o t) -> p o t", o=1),
                                    mix_hi[:, ds(at(pr, per, i), 1), :].bitcast(F32), ALU.subtract).then_inc(a.olo, 1)

    def pool_tile(eng, st, n, per, i):
        S, a = STAGES[st], att[st]
        N = 3 * S["nd"] * S["pairs"]
        m = n - 1
        if (i is None and not 0 <= m < N) or m % 3 == 2:
            return
        role, g, _, _ = kind(S, m)
        k, kp = qk_no(m) + 1, per * 2 // 3
        tab = S["rope"]
        eng.wait_ge(a.swap, at(k, kp, i))
        nc.gpsimd.tensor_tensor(rope_1[:], qk_raw[role][:], tab[:, 2 * g + role, 0, :], ALU.mult).then_inc(a.rot1, 1)
        nc.gpsimd.tensor_tensor(rope_2[:], qk_swap[role][:], tab[:, 2 * g + role, 1, :], ALU.mult).then_inc(a.rot2, 1)
        eng.wait_ge(a.rot1, at(k, kp, i))
        eng.wait_ge(a.rot2, at(k, kp, i))
        nc.gpsimd.tensor_tensor(qk_rope[role][:], rope_1[:], rope_2[:], ALU.add).then_inc(a.rope, 1)
        eng.wait_ge(a.rope, at(k, kp, i))

    def pool_event(eng, st, what, pr, per, i):
        return

    NEXT = RING

    def out_bank(m):
        return bank((m + 1) % 3, m // 3 * TOK) if m < NEXT else bank(SS + 1 + m - NEXT)

    OUT_C0 = (A_OUT, B_OUT, C_OUT)
    OUT_EARLY = (
        {0: ((0, 0, 6),), 1: ((1, 0, 6),), 2: ((2, 0, 6), (3, 0, 6)), 5: ((4, 0, 6),),
         6: tuple((m, 6, 7) for m in range(5)) + ((5, 0, 4),), 9: ((5, 4, 6),)},
        {0: ((0, 0, 5), (3, 0, 5)), 1: ((1, 0, 5),), 2: ((2, 0, 5), (4, 0, 5)), 3: tuple((m, 5, 6) for m in range(5)),
         5: tuple((m, 6, 7) for m in range(5)), 6: ((5, 0, 4),)},
        {},
    )

    def out_part(eng, st, m, k0, k1):
        c = OUT_C0[st] + m
        s = c % RING
        if k0 == 0:
            eng.wait_ge(w_lo_done, c + 1)
        if st < 2:
            eng.wait_ge(att[st].olo, k1)
        else:
            eng.wait_ge(att[st].olo, PAIRS_C)
            eng.wait_ge(side_lo, 4)
        for k in range(k0, k1):
            wh, wl = w_hi[s][:, k * P:(k + 1) * P], w_lo[s][:, k * P:(k + 1) * P]
            nc.tensor.matmul(out_bank(m), wh, mix_hi[:, k, :], start=False, stop=False, skip_group_check=True)
            nc.tensor.matmul(out_bank(m), wh, mix_lo[:, k, :], start=False, stop=False, skip_group_check=True)
            last = nc.tensor.matmul(out_bank(m), wl, mix_hi[:, k, :], start=False, stop=(k == KT - 1), skip_group_check=True)
        if k1 == KT:
            last.then_inc(tiles, 1)

    def out_early(eng, st):
        def after(k):
            if k < 3:
                eng.wait_ge(att[st].auxr, 3 * STAGES[st]["nd"] * STAGES[st]["pairs"] + k - 2)
                out_zero(eng, ((k + 1) % 3,))
            for part in OUT_EARLY[st].get(k, ()):
                out_part(eng, st, *part)
        return after

    def out_zero(eng, banks):
        eng.wait_ge(zeroed, 1)
        for bk in banks:
            nc.tensor.matmul(bank(bk, 0, 512), zero[:, 0:P], zero[:, 0:512], start=True, stop=True, skip_group_check=True)

    def out_pe(eng, st):
        done = {}
        for parts in OUT_EARLY[st].values():
            for m, k0, k1 in parts:
                done[m] = k1
        if not done:
            eng.wait_ge(side_lo, 4)
            out_zero(eng, range(3))
        out_zero(eng, (SS + 1, SS + 2))
        for m in range(KT):
            out_part(eng, st, m, done.get(m, 0), KT)

    def out_act(eng, c0, e):
        for m in range(KT):
            if m < KT + AHEAD_HI - RING:
                split_hi(eng, c0 + m + RING - AHEAD_HI, 0, None)
            resid_act(eng, e, m)

    def out_dve(eng, c0, e):
        for m in range(KT):
            resid_dve_add(eng, m, out_bank(m), c0 + (m + 3 if m < 3 else m))
            if m < KT + AHEAD - RING:
                split_lo(eng, c0 + m + RING - AHEAD, 0, None)
            if m >= 1:
                resid_dve_lo(eng, e, m - 1)
        resid_dve_lo(eng, e, KT - 1)

    FFN_C0 = (A_FFN, B_FFN, C_FFN)

    def acc(m):
        return bank(4 + m // 2, (m % 2) * TOK)

    def ffn_chunk(f, j):
        return FFN_C0[f] + (2 * j if j < 2 else 4 + 3 * (j - 2) if j < FT else 3 * FT - 2 + j - FT)

    def ffn_stage(eng, f, step):
        first = 4
        turns = (FT - first) // 2 - (f == 2)
        for j in range(first):
            step(eng, j, 0, None)
        with eng.Fori(0, turns) as i:
            for u in range(2):
                step(eng, first + u, 2, i)
        for j in range(first + 2 * turns, FT + 2):
            step(eng, j, 0, None)

    def ffn_pe(f):
        e = 2 * f + 1

        def step(eng, j, per, i):
            F, b, c, cp = ffn[f], j % 2, ffn_chunk(f, j), 3 * per
            if i is not None or j < FT:
                if i is None and j == 0:
                    eng.wait_ge(x_new, KT * (e - 1) + NEXT)
                if i is None and j == 1:
                    eng.wait_ge(x_r, e + 1)
                past(eng, F.up, 2 * (j - 1), 2 * per, i)
                project(eng, c, cp, i, bank(b), xg_hi, xg_lo, e if j == 0 and i is None else None)
                project(eng, c + 1, cp, i, bank(2 + b), xg_hi, xg_lo)
                c += 2
            if i is None and j == 1:
                eng.wait_ge(x_new, KT * e)
                out_zero(eng, range(4, 8))
            if i is not None or j >= 2:
                s = c % RING
                eng.wait_ge(w_lo_done, at(c + 1, cp, i))
                eng.wait_ge(F.glo, at(j - 1, per, i))
                for m in range(KT):
                    wh, wl = w_hi[s][:, m * P:(m + 1) * P], w_lo[s][:, m * P:(m + 1) * P]
                    nc.tensor.matmul(acc(m), wh, g_hi[b][:], start=False, stop=False, skip_group_check=True)
                    nc.tensor.matmul(acc(m), wh, g_lo[b][:], start=False, stop=False, skip_group_check=True)
                    last = nc.tensor.matmul(acc(m), wl, g_hi[b][:], start=False, stop=True, skip_group_check=True)
                    if m == KT - 1:
                        last.then_inc(tiles, 1)
                    elif i is None and j == FT + 1:
                        last.then_inc(acc_done, 1)
        return step

    def par_col(f, j, per, i, k):
        return par[:, ds(at(PAR_FFN + 8 * (f * FT + j) + k, 8 * per, i), 1)]

    def ffn_act(f):
        def step(eng, j, per, i):
            F, c, cp = ffn[f], ffn_chunk(f, j), 3 * per
            n = 3 if 2 <= j < FT else 2 if j < 2 else 1
            split_hi(eng, c, cp, i)
            if j == 1:
                resid_act_r(eng, 2 * f + 1)
                nc.scalar.preload_act_table_set("silu_and_others")
                eng.wait_ge(rest_in, 32)
            t = j - 2
            if i is not None or 0 <= t < FT:
                if i is not None or t >= 2:
                    eng.wait_ge(tiles, at(ffn_chunk(f, t) + 3, cp, i))
                eng.wait_ge(F.gated, at(t + 1, per, i))
                nc.scalar.activation(g_hi[t % 2][:], gated[:], ACT.Copy).then_inc(F.ghi, 1)
            t = j - 1
            work = i is not None or 0 <= t < FT
            if work:
                for s in range(2):
                    eng.wait_ge(F.up, at(2 * t + 1 + s, 2 * per, i))
                    nc.scalar.activation(cv_s[t % 2][s][:], up_s[t % 2][s][:], ACT.Identity,
                                         scale=par_col(f, t, per, i, 4 * s + 2),
                                         bias=par_col(f, t, per, i, 4 * s + 3)).then_inc(F.tap0, 1)
            for q in range(1, n):
                split_hi(eng, c + q, cp, i)
            if work:
                eng.wait_ge(F.conv, at(2 * t + 1, 2 * per, i))
                nc.scalar.activation(gate_s[:], cv_s[t % 2][0][:], ACT.Silu).then_inc(F.silu, 1)
        return step

    def ffn_dve(f):
        def step(eng, j, per, i):
            F, c, cp = ffn[f], ffn_chunk(f, j), 3 * per
            n = 3 if 2 <= j < FT else 2 if j < 2 else 1
            t = j - 1
            b = t % 2
            work = i is not None or 0 <= t < FT
            split_lo(eng, c, cp, i)
            if work:
                if i is None and t == 0:
                    eng.wait_ge(x_r, 2 * f + 2)
                for s in range(2):
                    eng.wait_ge(tiles, at(ffn_chunk(f, t) + 1 + s, cp, i))
                    nc.vector.tensor_tensor(up_s[b][s][:], bank(2 * s + b), rms_r[:], ALU.mult).then_inc(F.up, 1)
            if n > 1:
                split_lo(eng, c + 1, cp, i)
            if i is not None or j >= 2:
                eng.wait_ge(F.ghi, at(j - 1, per, i))
                nc.vector.tensor_tensor(g_lo[j % 2][:], gated[:], g_hi[j % 2][:].bitcast(F32),
                                        ALU.subtract).then_inc(F.glo, 1)
            if work:
                for k in range(1, 3):
                    for s in range(2):
                        if k == 1:
                            eng.wait_ge(F.tap0, at(2 * t + 1 + s, 2 * per, i))
                        else:
                            eng.wait_ge(F.tap1, at(2 * t + 1 + s, 2 * per, i))
                        nc.vector.scalar_tensor_tensor(cv_s[b][s][:, k:TOK], up_s[b][s][:, 0:TOK - k],
                                                       par_col(f, t, per, i, 4 * s + 2 - k), cv_s[b][s][:, k:TOK],
                                                       ALU.mult, ALU.add).then_inc(F.tap1 if k == 1 else F.conv, 1)
            if n > 2:
                split_lo(eng, c + 2, cp, i)
        return step

    def ffn_pool(f):
        def step(eng, j, per, i):
            F, t = ffn[f], j - 1
            if i is None and not 0 <= t < FT:
                return
            eng.wait_ge(F.silu, at(t + 1, per, i))
            eng.wait_ge(F.conv, at(2 * t + 2, 2 * per, i))
            past(eng, F.glo, t, per, i)
            nc.gpsimd.tensor_tensor(gated[:], gate_s[:], cv_s[t % 2][1][:], ALU.mult).then_inc(F.gated, 1)
        return step

    def ffn_end_act(eng, e):
        for m in range(KT):
            resid_act(eng, e, m)

    def ffn_end_dve(eng, f):
        for m in range(KT):
            if m < KT - 2:
                eng.wait_ge(acc_done, f * (KT - 1) + (m | 1) + 1)
            else:
                eng.wait_ge(tiles, FFN_C0[f] + 3 * FT)
            nc.vector.tensor_tensor(xT[:, m, :], acc(m), xT[:, m, :], ALU.add).then_inc(x_new, 1)
            if m >= 1 and f < 2:
                resid_dve_lo(eng, 2 * f + 2, m - 1)
        if f < 2:
            resid_dve_lo(eng, 2 * f + 2, KT - 1)

    PRE_OUT = [fg[0], cv_a[0][:], cv_b[0][:], cv_a[1][:], cv_b[1][:],
               pl[0][0][:, POOL_PAD:POOL_PAD + TOK], pl[1][0][:, POOL_PAD:POOL_PAD + TOK]]

    def pre_pe(eng):
        for n in range(N_PRE):
            past(eng, pre_out, n - 2, 0, None)
            project(eng, C_PRE + n, 0, None, bank(n % 3), xg_hi, xg_lo, 4 if n == 0 else None)

    def pre_act_f(eng):
        for n in range(N_PRE):
            split_hi(eng, C_PRE + n, 0, None)
            if n == 1:
                resid_act_r(eng, 4)
            if n == 2:
                eng.wait_ge(pre_out, 1)
                nc.scalar.activation(fg[1], fg[0], ACT.Identity, bias=par[0:HEADS_C, PAR_BF:PAR_BF + 1]).then_inc(pre_act, 1)
                eng.wait_ge(pre_dve, 1)
                nc.scalar.activation(fg[3], fg[2], ACT.Exp, scale=-1.0).then_inc(pre_act, 1)
                eng.wait_ge(pre_act, 2)
                nc.scalar.activation(fg[4], fg[3], ACT.Ln, bias=1.0).then_inc(pre_act, 1)
            if n in (4, 6):
                t = n // 2 - 2
                eng.wait_ge(pre_out, 2 * t + 3)
                if t == 0:
                    nc.scalar.preload_act_table_set("sigmoid_and_others")
                nc.scalar.activation(cv_e[t][:], cv_b[t][:], ACT.Sigmoid).then_inc(pre_act, 1)
        nc.scalar.preload_act_table_set("natural_log_exp_and_others")

    def pre_dve_f(eng):
        def glu(t):
            eng.wait_ge(pre_act, 4 + t)
            eng.wait_ge(zeroed, 3)
            nc.vector.tensor_tensor(cv_h[t][:, PADC:PADC + TOK], cv_a[t][:], cv_e[t][:], ALU.mult).then_inc(pre_dve, 1)

        def out(n):
            if n == 0:
                eng.wait_ge(x_r, 5)
            if n == 5:
                eng.wait_ge(pl_zeroed, 6)
            eng.wait_ge(tiles, C_PRE + n + 1)
            src = bank(n % 3)[0:HEADS_C, :] if n == 0 else bank(n % 3)
            r = rms_r[0:HEADS_C, :] if n == 0 else rms_r[:]
            nc.vector.tensor_tensor(PRE_OUT[n], src, r, ALU.mult).then_inc(pre_out, 1)

        for n in range(N_PRE):
            split_lo(eng, C_PRE + n, 0, None)
            if n >= 1:
                out(n - 1)
            if n == 2:
                eng.wait_ge(pre_act, 1)
                nc.vector.scalar_tensor_tensor(fg[2], fg[1], -1.0, fg[1], ALU.mult, ALU.max).then_inc(pre_dve, 1)
            if n == 3:
                eng.wait_ge(pre_act, 3)
                nc.vector.scalar_tensor_tensor(fg[5], fg[1], 0.0, fg[4], ALU.min, ALU.subtract).then_inc(pre_dve, 1)
                eng.wait_ge(pre_dve, 2)
                nc.vector.tensor_tensor_scan(fg[2], con[0:HEADS_C, CON_ONES:CON_ONES + 1].to_broadcast([HEADS_C, TOK]),
                                             fg[5], 0.0, ALU.mult, ALU.add).then_inc(pre_dve, 1)
                eng.wait_ge(pre_dve, 3)
                for h in range(HEADS_C):
                    last = nc.vector.tensor_scalar(bias_k[:, h * TOK:(h + 1) * TOK], fg[2],
                                                   con[0:HEADS_C, CON_ID + h:CON_ID + h + 1], -1.0, ALU.mult, ALU.mult)
                last.then_inc(bias_in, 1)
            if n == 6:
                glu(0)
        out(N_PRE - 1)
        glu(1)

    def pre_pool_f(eng):
        n = 0
        for t in range(2):
            for b in pl[t]:
                nc.gpsimd.memset(b, 0.0).then_inc(pl_zeroed, 1)
        for t in range(2):
            eng.wait_ge(pre_out, 6 + t)
            src, k = 0, 1
            steps = ((1, 0, P), (2, HD, P)) if t == 0 else ((1, 0, P), (2, 0, P), (4, 0, P), (8, HD, P))
            for s, p0, p1 in steps:
                dst = 1 if src != 1 else 2
                if p0:
                    nc.gpsimd.tensor_copy(pl[t][dst][0:HD, POOL_PAD:], pl[t][src][0:HD, POOL_PAD:]).then_inc(pre_pool, 1)
                    n += 1
                nc.gpsimd.tensor_tensor(pl[t][dst][p0:p1, s:], pl[t][src][p0:p1, s:],
                                        pl[t][src][p0:p1, 0:POOL_PAD + TOK - s], ALU.add).then_inc(pre_pool, 1)
                n += 1
                eng.wait_ge(pre_pool, n)
                src = dst
            inv = con[:, CON_INV + t * TOK:CON_INV + (t + 1) * TOK]
            s0 = pl[t][src][:, POOL_PAD:]
            nc.gpsimd.tensor_tensor(s0, s0, inv, ALU.mult).then_inc(pre_pool, 1)
            n += 1
            eng.wait_ge(pre_pool, n)
            nc.gpsimd.tensor_tensor(pl[t][3 - src][:, POOL_PAD:], s0, pl[t][0][:, POOL_PAD:], ALU.subtract).then_inc(pre_pool, 1)
            n += 1
            eng.wait_ge(pre_pool, n)
        return n

    POOL_D = [pl[0][1], pl[1][1]]
    N_POOL_STEPS = 3 + 2 + 5 + 2

    TAPS_PER = 4
    POOL_TAPS = CONV_C // 2
    DVE_TAPS = [(0, j) for j in range(CONV_C)] + [(1, j) for j in range(CONV_C - POOL_TAPS)]
    part, prods = rope_1, qk_swap

    def conv_w(t, j):
        return par[:, PAR_DW + t * CONV_C + j:PAR_DW + t * CONV_C + j + 1]

    def conv_taps(eng, n):
        for q in range(TAPS_PER * n, min(TAPS_PER * (n + 1), len(DVE_TAPS) + 1)):
            if q == len(DVE_TAPS):
                eng.wait_ge(tap_pool, 2 * POOL_TAPS - 1)
                eng.wait_ge(tap, q)
                nc.vector.tensor_tensor(cv_acc[1][:], cv_acc[1][:], part[:], ALU.add).then_inc(tap, 1)
                continue
            t, j = DVE_TAPS[q]
            src = cv_h[t][:, j:j + TOK]
            if j == 0:
                if t == 0:
                    eng.wait_ge(pre_dve, 5)
                nc.vector.tensor_scalar(cv_acc[t][:], src, conv_w(t, j), par[:, PAR_DWB + t:PAR_DWB + t + 1],
                                        ALU.mult, ALU.add).then_inc(tap, 1)
            else:
                eng.wait_ge(tap, q)
                nc.vector.scalar_tensor_tensor(cv_acc[t][:], src, conv_w(t, j), cv_acc[t][:],
                                               ALU.mult, ALU.add).then_inc(tap, 1)

    def conv_pool(eng):
        eng.wait_ge(pre_dve, 5)
        for q in range(POOL_TAPS):
            j = CONV_C - POOL_TAPS + q
            to = part if q == 0 else prods[q % 2]
            nc.gpsimd.tensor_scalar(to[:], cv_h[1][:, j:j + TOK], conv_w(1, j), None, ALU.mult).then_inc(tap_pool, 1)
            if q > 0:
                eng.wait_ge(tap_pool, 2 * q)
                nc.gpsimd.tensor_tensor(part[:], part[:], prods[q % 2][:], ALU.add).then_inc(tap_pool, 1)

    def side_pe(eng):
        ones = con[:, CON_ONES:CON_ONES + P]

        def after(k):
            if k == 2:
                eng.wait_ge(att[2].auxr, 3 * PAIRS_C)
                eng.wait_ge(tap, len(DVE_TAPS) + 1)
                for t in range(2):
                    last = nc.tensor.matmul(bank(0), ones, cv_acc[t][:], start=(t == 0), stop=(t == 1))
                last.then_inc(ln_pe, 1)
                eng.wait_ge(pre_pool, N_POOL_STEPS)
                for t in range(2):
                    for g in range(2):
                        p0, p1 = HD * g, HD * g + HD
                        last = nc.tensor.matmul(bank(1, t * TOK)[p0:p1, :],
                                                par[p0:p1, PAR_POOLW + t * HD:PAR_POOLW + (t + 1) * HD],
                                                POOL_D[t][p0:p1, POOL_PAD:], start=True, stop=True)
                last.then_inc(ln_pe, 1)
            elif k == 3:
                eng.wait_ge(ln_act, 4)
                for t in range(2):
                    last = nc.tensor.matmul(bank(2), ones, cv_e[t][:], start=(t == 0), stop=(t == 1))
                last.then_inc(ln_pe, 1)
            elif k == 5:
                eng.wait_ge(ln_act, 8)
                for o in range(2):
                    for t in range(2):
                        w = PAR_PW + t * 2 * P + o * P
                        last = nc.tensor.matmul(bank(2 * o, TOK), par[:, w:w + P], cv_a[t][:], start=(t == 0), stop=(t == 1))
                last.then_inc(ln_pe, 1)
        return after

    def side_act(eng):
        def after(k):
            if k == 2:
                eng.wait_ge(ln_pe, 2)
                for t in range(2):
                    nc.scalar.activation(mix_hi[:, 6 + t, :], bank(1, t * TOK), ACT.Copy,
                                         scale=par[:, PAR_PSC + t:PAR_PSC + t + 1]).then_inc(ln_act, 1)
                for t in range(2):
                    eng.wait_ge(ln_dve, t + 1)
                    nc.scalar.activation(cv_e[t][:], cv_b[t][:], ACT.Square).then_inc(ln_act, 1)
            elif k == 3:
                eng.wait_ge(ln_pe, 3)
                nc.scalar.activation(ln_x[:], bank(2), ACT.Ln, scale=1.0 / (2 * P),
                                     bias=con[:, CON_EPS:CON_EPS + 1]).then_inc(ln_act, 1)
                eng.wait_ge(ln_act, 5)
                nc.scalar.activation(ln_x[:], ln_x[:], ACT.Exp, scale=-0.5).then_inc(ln_act, 1)
            elif k == 4:
                nc.scalar.preload_act_table_set("silu_and_others")
                for t in range(2):
                    eng.wait_ge(ln_dve, 3 + t)
                    nc.scalar.activation(cv_a[t][:], cv_b[t][:], ACT.Silu, scale=par[:, PAR_LNG + t:PAR_LNG + t + 1],
                                         bias=par[:, PAR_LNB + t:PAR_LNB + t + 1]).then_inc(ln_act, 1)
                nc.scalar.preload_act_table_set("natural_log_exp_and_others")
            elif k == 6:
                eng.wait_ge(ln_pe, 4)
                for o in range(2):
                    nc.scalar.activation(mix_hi[:, 4 + o, :], bank(2 * o, TOK), ACT.Copy).then_inc(ln_act, 1)
        return after

    def side_dve(eng):
        def after(k):
            if k == 2:
                eng.wait_ge(ln_pe, 1)
                for t in range(2):
                    nc.vector.scalar_tensor_tensor(cv_b[t][:], bank(0), -1.0 / (2 * P), cv_acc[t][:],
                                                   ALU.mult, ALU.add).then_inc(ln_dve, 1)
                for t in range(2):
                    eng.wait_ge(ln_act, 2)
                    nc.vector.scalar_tensor_tensor(mix_lo[:, 6 + t, :], bank(1, t * TOK), par[:, PAR_PSC + t:PAR_PSC + t + 1],
                                                   mix_hi[:, 6 + t, :].bitcast(F32), ALU.mult, ALU.subtract).then_inc(side_lo, 1)
            elif k == 3:
                eng.wait_ge(ln_act, 6)
                for t in range(2):
                    nc.vector.tensor_tensor(cv_b[t][:], cv_b[t][:], ln_x[:], ALU.mult).then_inc(ln_dve, 1)
            elif k == 6:
                for o in range(2):
                    eng.wait_ge(ln_act, 9 + o)
                    nc.vector.tensor_tensor(mix_lo[:, 4 + o, :], bank(2 * o, TOK), mix_hi[:, 4 + o, :].bitcast(F32),
                                            ALU.subtract).then_inc(side_lo, 1)
        return after

    with nc.Block() as block:

        @block.sync
        def _(sp):
            def load(s, c):
                sp.dma_start(w_raw[s][:], stream_d[ds(c, 1)].rearrange("o p n -> (o p) n")).then_inc(w_loaded[s], 16)

            half = KT // 2
            sp.dma_start(par[:, 0:PAR_FFN], par_d[:, 0:PAR_FFN]).then_inc(par_in, 16)
            sp.dma_start(xT[:, 0:half], x_d[0:half].rearrange("k p t -> p k t")).then_inc(x_in, 16)
            load(0, 0)
            sp.dma_start(con[:, 0:CON_COS], con_d[:, 0:CON_COS]).then_inc(con_in, 16)
            sp.dma_start(xT[:, half:KT], x_d[half:KT].rearrange("k p t -> p k t")).then_inc(x_in, 16)
            for s in range(1, AHEAD):
                load(s, s)
            sp.dma_start(con[:, CON_COS:], con_d[:, CON_COS:]).then_inc(rest_in, 16)
            load(AHEAD, AHEAD)
            sp.dma_start(par[:, PAR_FFN:], par_d[:, PAR_FFN:]).then_inc(rest_in, 16)
            for s in range(AHEAD + 1, RING):
                load(s, s)
            turns = N_CHUNKS // RING
            with sp.Fori(1, turns) as i:
                for s in range(RING):
                    sp.wait_ge(w_lo_done, i * RING + (s - RING + 1))
                    load(s, i * RING + s)
            for c in range(turns * RING, N_CHUNKS):
                sp.wait_ge(w_lo_done, c - RING + 1)
                load(c % RING, c)
            for m in range(KT):
                sp.wait_ge(x_new, 5 * KT + m + 1)
                sp.dma_start(out_d[m], xT[:, m, :]).then_inc(stored, 16)
            sp.wait_ge(stored, 16 * KT)

        @block.tensor
        def _(pe):
            pe.wait_ge(con_in, 16)
            for st in range(3):
                if st == 2:
                    pre_pe(pe)
                    pe.wait_ge(pre_out, N_PRE)
                    pe.wait_ge(rest_in, 32)
                att_stage(pe, "pe", st, pe_tile, pe_event, side_pe(pe) if st == 2 else out_early(pe, st))
                out_pe(pe, st)
                ffn_stage(pe, st, ffn_pe(st))

        @block.scalar
        def _(act):
            nc.scalar.preload_act_table_set("natural_log_exp_and_others")
            split_hi(act, -AHEAD_HI, 0, None)
            for m in range(KT):
                resid_act(act, 0, m)
            for c in range(1, AHEAD_HI):
                split_hi(act, c - AHEAD_HI, 0, None)
            for st in range(3):
                if st == 2:
                    pre_act_f(act)
                att_stage(act, "act", st, act_tile, act_event, side_act(act) if st == 2 else None)
                out_act(act, OUT_C0[st], 2 * st + 1)
                ffn_stage(act, st, ffn_act(st))
                if st < 2:
                    nc.scalar.preload_act_table_set("natural_log_exp_and_others")
                    ffn_end_act(act, 2 * st + 2)

        @block.vector
        def _(dve):
            dve.wait_ge(par_in, 16)
            split_lo(dve, -AHEAD, 0, None)
            for m in range(KT):
                resid_dve_lo(dve, 0, m)
            for c in range(1, AHEAD):
                split_lo(dve, c - AHEAD, 0, None)
            for st in range(3):
                if st == 2:
                    pre_dve_f(dve)
                att_stage(dve, "dve", st, dve_tile, dve_event, side_dve(dve) if st == 2 else None)
                out_dve(dve, OUT_C0[st], 2 * st + 1)
                ffn_stage(dve, st, ffn_dve(st))
                ffn_end_dve(dve, st)

        @block.gpsimd
        def _(pool):
            nc.gpsimd.memset(zero[:], 0.0).then_inc(zeroed, 1)
            nc.gpsimd.memset(cv_h[0][:], 0.0).then_inc(zeroed, 1)
            nc.gpsimd.memset(cv_h[1][:], 0.0).then_inc(zeroed, 1)
            pool.wait_ge(par_in, 16)
            pool.wait_ge(rest_in, 32)
            for tab, n0, n in ((rope_t, 0, 2 * NDIL), (rope_b, 2 * NDIL, 2)):
                for k in range(n):
                    for w, (src, col) in enumerate(((CON_COS, PAR_GAIN), (CON_SIN, PAR_SWAP))):
                        c = col + n0 + k
                        nc.gpsimd.tensor_scalar(tab[:, k, w, :], con[:, src:src + TOK], par[:, c:c + 1], None,
                                                ALU.mult).then_inc(tables, 1)
            pool.wait_ge(tables, 4 * NDIL + 4)
            pool.wait_ge(zeroed, 3)
            att_stage(pool, "pool", 0, pool_tile, pool_event)
            ffn_stage(pool, 0, ffn_pool(0))
            att_stage(pool, "pool", 1, pool_tile, pool_event)
            ffn_stage(pool, 1, ffn_pool(1))
            pre_pool_f(pool)
            conv_pool(pool)
            ffn_stage(pool, 2, ffn_pool(2))


def weight_stream(w):
    def tile(m):
        return m.reshape(KT, P, P).transpose(1, 0, 2).reshape(P, CHUNK)

    chunks = []

    def qkv(m, nd, pairs, cols):
        for pr in range(pairs):
            for g in range(nd):
                for role in range(3):
                    c = cols(role, g, pr)
                    chunks.append(tile(m[:, c:c + P]))

    def outs(m):
        for n in range(KT):
            chunks.append(tile(m[:, n * P:(n + 1) * P]))

    def mlp(up, down):
        for j in range(FT + 2):
            if j < FT:
                chunks.append(tile(up[:, j * P:(j + 1) * P]))
                chunks.append(tile(up[:, D_FF + j * P:D_FF + (j + 1) * P]))
            if j >= 2:
                chunks.append(down[(j - 2) * P:(j - 1) * P, :])

    qkv(w["a_w_qkv"][0], NDIL, PAIRS_AB, lambda r, g, pr: (r * NDIL + g) * D + pr * P)
    outs(w["a_w_o"][0])
    mlp(w["ffn_w_up"][0], w["ffn_w_down"][0])
    qkv(w["b_w_qkv"][0], 1, PAIRS_AB, lambda r, g, pr: r * D + pr * P)
    outs(w["b_w_o"][0])
    mlp(w["ffn_w_up"][1], w["ffn_w_down"][1])
    w_in = w["w_in_2"][0]
    att = HEADS_C * HD
    forget = np.zeros((D, P), np.float32)
    forget[:, 0:HEADS_C] = w_in[:, 3 * att:3 * att + HEADS_C]
    chunks.append(tile(forget))
    conv = 3 * att + HEADS_C
    for t in range(2):
        for half in range(2):
            c = conv + half * 2 * P + t * P
            chunks.append(tile(w_in[:, c:c + P]))
    for t in range(2):
        c = conv + 4 * P + t * P
        chunks.append(tile(w_in[:, c:c + P]))
    qkv(w_in, 1, PAIRS_C, lambda r, g, pr: r * att + pr * P)
    outs(w["w_out_2"][0])
    mlp(w["w_up_2"][0], w["w_down_2"][0])
    return np.stack(chunks)


def parameters(w):
    par = np.zeros((P, N_PAR), np.float32)

    def cols(at, v):
        n = v.shape[0] // P
        par[:, at:at + n] = v.reshape(n, P).T

    norms = (w["attn_norm"][0], w["ffn_norm"][0], w["attn_norm"][1], w["ffn_norm"][1], w["norm1_g_2"][0], w["norm2_g_2"][0])
    for e, v in enumerate(norms):
        cols(PAR_NORM + KT * e, v)
    gains = []
    for g in range(NDIL):
        gains += [w["a_q_norm"][0, g], w["a_k_norm"][0, g]]
    gains += [w["b_q_norm"][0], w["b_k_norm"][0], w["q_norm_g_2"][0], w["k_norm_g_2"][0]]
    half = ROPE_DIM // 2
    for n, v in enumerate(gains):
        par[:, PAR_GAIN + n] = np.concatenate([v, v])
        if n < 2 * NDIL + 2:
            sw = np.concatenate([v[half:ROPE_DIM], v[0:half], v[ROPE_DIM:]])
            par[:, PAR_SWAP + n] = np.concatenate([sw, sw])
    convs = ((w["ffn_conv_w"][0], w["ffn_conv_b"][0]), (w["ffn_conv_w"][1], w["ffn_conv_b"][1]), (w["ffn_dw_w_2"][0], None))
    for f, (cw, cb) in enumerate(convs):
        for j in range(FT):
            for s in range(2):
                c = PAR_FFN + 8 * (f * FT + j) + 4 * s
                rows = slice(s * D_FF + j * P, s * D_FF + (j + 1) * P)
                for k in range(3):
                    par[:, c + k] = cw[k, rows]
                if cb is not None:
                    par[:, c + 3] = cb[rows]
    for t in range(2):
        par[:, PAR_DW + t * CONV_C:PAR_DW + (t + 1) * CONV_C] = w["conv_dw_w_2"][0][:, t * P:(t + 1) * P].T
    cols(PAR_DWB, w["conv_dw_b_2"][0])
    cols(PAR_LNG, w["conv_ln_g_2"][0])
    cols(PAR_LNB, w["conv_ln_b_2"][0])
    cols(PAR_PSC, w["pool_scale_2"][0])
    par[0:HEADS_C, PAR_BF] = w["b_f_2"][0]
    for g in range(4):
        par[HD * (g % 2):HD * (g % 2) + HD, PAR_POOLW + (g // 2) * HD:PAR_POOLW + (g // 2 + 1) * HD] = w["pool_w_2"][0, g]
    for t in range(2):
        par[:, PAR_PW + t * 2 * P:PAR_PW + (t + 1) * 2 * P] = w["conv_pw_w_2"][0][t * P:(t + 1) * P, :]
    return par


def kernel(**inputs):
    import concourse.bacc as bacc
    from concourse.bass_utils import run_bass_kernel_spmd

    w = {k: np.asarray(v) for k, v in inputs.items()}
    con = shape_constants()
    arrays = {
        "x_t": np.ascontiguousarray(w["x"][0].T).reshape(KT, P, TOK),
        "w_stream": weight_stream(w),
        "params": parameters(w),
        "consts": con,
    }
    nc = bacc.Bacc("TRN2", target_bir_lowering=False, num_devices=1)
    f32 = mybir.dt.float32
    args = [nc.dram_tensor(n, a.shape, f32, kind="ExternalInput").ap() for n, a in arrays.items()]
    out = nc.dram_tensor("y_t", (KT, P, TOK), f32, kind="ExternalOutput").ap()
    build(nc, *args, out)
    r = run_bass_kernel_spmd(nc, [arrays], core_ids=[0])
    return r.results[0]["y_t"].reshape(D, TOK).T.reshape(1, TOK, D)
```

```python
import itertools

import numpy as np

import concourse.bass as bass
from concourse import mybir
from concourse.alu_op_type import AluOpType as ALU

P = 128
D = 1024
TOK = 256
KT = D // P
HEADS_A = 16
HD = 64
NDIL = 3
DILATED_PAIRS = ((128, 1), (512, 4), (2048, 16))
ROPE_DIM = HD // 4
ROPE_THETA = 500000.0
PAIRS_AB = HEADS_A // 2
HEADS_C = 8
PAIRS_C = HEADS_C // 2
D_FF = 2816
FT = D_FF // P
CONV_C = 31
PADC = CONV_C - 1
POOL_PAD = 16
POOL_WINDOWS = (2, 4, 8, 16)
EPS = 1e-6
NEG = -1e30
RING = 6
AHEAD = 3
AHEAD_HI = AHEAD + 1
CHUNK = KT * P

A_QKV = 0
A_OUT = A_QKV + 3 * NDIL * PAIRS_AB
A_FFN = A_OUT + KT
B_QKV = A_FFN + 3 * FT
B_OUT = B_QKV + 3 * PAIRS_AB
B_FFN = B_OUT + KT
C_PRE = B_FFN + 3 * FT
N_PRE = 7
C_QKV = C_PRE + N_PRE
C_OUT = C_QKV + 3 * PAIRS_C
C_FFN = C_OUT + KT
N_CHUNKS = C_FFN + 3 * FT

PAR_NORM = 0
PAR_GAIN = PAR_NORM + 6 * KT
PAR_SWAP = PAR_GAIN + 2 * NDIL + 4
PAR_FFN = PAR_SWAP + 2 * NDIL + 2
PAR_DW = PAR_FFN + 3 * FT * 8
PAR_DWB = PAR_DW + 2 * CONV_C
PAR_LNG = PAR_DWB + 2
PAR_LNB = PAR_LNG + 2
PAR_PSC = PAR_LNB + 2
PAR_BF = PAR_PSC + 2
PAR_POOLW = PAR_BF + 1
PAR_PW = PAR_POOLW + 2 * HD
N_PAR = PAR_PW + 2 * 2 * P

CON_ID = 0
CON_ONES = CON_ID + P
CON_BLK = CON_ONES + P
CON_EPS = CON_BLK + P
CON_COS = CON_EPS + 2
CON_SIN = CON_COS + TOK
CON_MASKA = CON_SIN + TOK
CON_MASK1 = CON_MASKA + 3 * NDIL * P
CON_INV = CON_MASK1 + 3 * P
N_CON = CON_INV + 2 * TOK


def shape_constants():
    con = np.zeros((P, N_CON), np.float32)
    pos = np.arange(TOK, dtype=np.float32)
    inv_freq = np.float32(ROPE_THETA) ** (-np.arange(0, ROPE_DIM, 2, dtype=np.float32) / np.float32(ROPE_DIM))
    ang = (pos[:, None] * inv_freq[None, :]).astype(np.float32)
    cos, sin = np.cos(ang).T, np.sin(ang).T
    half = ROPE_DIM // 2
    con[:, CON_COS:CON_COS + TOK] = 1.0
    for b in (0, HD):
        con[b:b + half, CON_COS:CON_COS + TOK] = cos
        con[b + half:b + ROPE_DIM, CON_COS:CON_COS + TOK] = cos
        con[b:b + half, CON_SIN:CON_SIN + TOK] = -sin
        con[b + half:b + ROPE_DIM, CON_SIN:CON_SIN + TOK] = sin

    def mask(window, dil, qt, keys):
        d = (qt * P + np.arange(P))[:, None] - np.arange(keys)[None, :]
        ok = (d >= 0) & (d <= window) & (d % dil == 0)
        return np.where(ok, 0.0, NEG)

    o = CON_MASKA
    for qt in range(2):
        for w, d in DILATED_PAIRS:
            con[:, o:o + (qt + 1) * P] = mask(w, d, qt, (qt + 1) * P)
            o += (qt + 1) * P
    o = CON_MASK1
    for qt in range(2):
        con[:, o:o + (qt + 1) * P] = mask(TOK, 1, qt, (qt + 1) * P)
        o += (qt + 1) * P
    con[:, CON_ID:CON_ID + P] = np.eye(P)
    con[:, CON_ONES:CON_ONES + P] = 1.0
    for b in (0, HD):
        con[b:b + HD, CON_BLK + b:CON_BLK + b + HD] = 1.0
    for g, w in enumerate(POOL_WINDOWS):
        b = HD * (g % 2)
        con[b:b + HD, CON_INV + (g // 2) * TOK:CON_INV + (g // 2 + 1) * TOK] = 1.0 / np.minimum(pos + 1, w)
    con[:, CON_EPS] = EPS
    con[:, CON_EPS + 1] = HD * EPS
    return con


def build(nc, x_d, stream_d, par_d, con_d, out_d):
    F32 = mybir.dt.float32
    F32R = mybir.dt.float32r
    BF16 = mybir.dt.bfloat16
    ACT = mybir.ActivationFunctionType
    ds = bass.ds

    def sb(name, shape, dt=F32):
        return nc.alloc_sbuf_tensor(name, shape, dt)

    def sem(name):
        return nc.alloc_semaphore(name)

    w_raw = [sb(f"w_raw{s}", [P, CHUNK]) for s in range(RING)]
    w_hi = [sb(f"w_hi{s}", [P, CHUNK], F32R) for s in range(RING)]
    w_lo = [sb(f"w_lo{s}", [P, CHUNK], F32R) for s in range(RING)]
    xT = sb("xT", [P, KT, TOK])
    xg_hi = sb("xg_hi", [P, KT, TOK], F32R)
    xg_lo = sb("xg_lo", [P, KT, TOK], F32R)
    mix_hi = sb("mix_hi", [P, KT, TOK], F32R)
    mix_lo = sb("mix_lo", [P, KT, TOK], F32R)
    par = sb("par", [P, N_PAR])
    con = sb("con", [P, N_CON])
    zero = sb("zero", [P, 512], BF16)
    ln_x = sb("ln_x", [P, TOK])
    rms_r = sb("rms_r", [P, TOK])
    rope_t = sb("rope_t", [P, 2 * NDIL, 2, TOK])
    rope_b = sb("rope_b", [P, 2, 2, TOK])
    qk_raw = [sb(f"qk_raw{r}", [P, TOK]) for r in range(2)]
    qk_sq = [sb(f"qk_sq{r}", [P, TOK], F32R) for r in range(2)]
    sq_all = sb("sq_all", [P, TOK])
    sq_lo = [sb(f"sq_lo{r}", [P, TOK], F32R) for r in range(2)]
    blk = sb("blk", [P, P], F32R)
    qk_swap = [sb(f"qk_swap{r}", [P, TOK]) for r in range(2)]
    qk_rope = [sb(f"qk_rope{r}", [P, TOK]) for r in range(2)]
    qk_r = [sb(f"qk_r{r}", [P, TOK]) for r in range(2)]
    rope_1 = sb("rope_1", [P, TOK])
    rope_2 = sb("rope_2", [P, TOK])
    v_t = sb("v_t", [P, TOK])
    sqx = [sq_all, v_t] + qk_swap + qk_rope + [rope_1, rope_2]
    qk_n = [[[sb(f"qk_n{b}{g}{r}", [P, TOK]) for r in range(2)] for g in range(NDIL)] for b in range(2)]
    v_n = [[sb(f"v_n{b}{g}", [P, 2, P]) for g in range(NDIL)] for b in range(2)]
    prob = [sb(f"prob{h}", [P, 3 * NDIL * P]) for h in range(2)]
    prob_t = [sb(f"prob_t{h}", [P, NDIL, 3 * P]) for h in range(2)]
    smax = [sb(f"smax{h}", [P, 2]) for h in range(2)]
    nmax = [sb(f"nmax{h}", [P, 2]) for h in range(2)]
    ssum = [sb(f"ssum{h}", [P, 2]) for h in range(2)]
    rsum = [sb(f"rsum{h}", [P, 2]) for h in range(2)]
    scratch = sb("scratch", [P, 64])
    scratch_col = itertools.count()
    up_s = [[qk_n[b][1][s] for s in range(2)] for b in range(2)]
    cv_s = [[qk_n[b][2][s] for s in range(2)] for b in range(2)]
    gate_s, gated = qk_raw
    g_hi = [sb(f"g_hi{b}", [P, TOK], F32R) for b in range(2)]
    g_lo = [sb(f"g_lo{b}", [P, TOK], F32R) for b in range(2)]
    bias_k = rope_t[0:HEADS_C, 0:4].rearrange("p a b t -> p (a b t)")
    fg = [rope_t[0:HEADS_C, 4 + n // 2, n % 2, :] for n in range(4)] + [rope_b[0:HEADS_C, 0, n, :] for n in range(2)]
    cv_a = [qk_n[0][1][i] for i in range(2)]
    cv_b = [qk_n[0][2][i] for i in range(2)]
    cv_e = [qk_n[1][1][i] for i in range(2)]
    cv_acc = [qk_n[1][2][i] for i in range(2)]
    cv_h = [sb(f"cv_h{i}", [P, PADC + TOK]) for i in range(2)]
    W_PL = POOL_PAD + TOK
    prob_t_flat = [prob_t[h][:].rearrange("p g c -> p (g c)") for h in range(2)]
    pl = [[prob[i][:, 3 * P:3 * P + W_PL], prob[i][:, 3 * P + W_PL:3 * P + 2 * W_PL],
           prob_t_flat[i][:, 3 * P:3 * P + W_PL]] for i in range(2)]

    ps = nc.alloc_psum_tensor("ps", [P, 8 * 512], F32)

    def bank(b, lo=0, n=TOK):
        return ps[:, b * 512 + lo:b * 512 + lo + n]

    SS = 3

    w_loaded = [sem(f"w_loaded{s}") for s in range(RING)]
    w_hi_done = sem("w_hi_done")
    w_lo_done = sem("w_lo_done")
    tiles = sem("tiles")
    x_in = [sem(f"x_in{h}") for h in range(2)]
    par_in = sem("par_in")
    con_in = sem("con_in")
    rope_in = sem("rope_in")
    rest_in = sem("rest_in")
    pl_zeroed = sem("pl_zeroed")
    zeroed = sem("zeroed")
    acc_done = sem("acc_done")
    x_new = sem("x_new")
    x_sq = sem("x_sq")
    x_hi = sem("x_hi")
    x_lo = sem("x_lo")
    x_add = sem("x_add")
    x_ss = sem("x_ss")
    x_ln = sem("x_ln")
    x_r = sem("x_r")
    tables = sem("tables")
    blk_in = sem("blk_in")
    stored = sem("stored")

    class Att:

        def __init__(self, n):
            self.raw = sem(f"{n}_raw")
            self.sq = sem(f"{n}_sq")
            self.sqall = sem(f"{n}_sqall")
            self.sqlo = sem(f"{n}_sqlo")
            self.swap = sem(f"{n}_swap")
            self.rot1 = sem(f"{n}_rot1")
            self.rot2 = sem(f"{n}_rot2")
            self.rope = sem(f"{n}_rope")
            self.aux = sem(f"{n}_aux")
            self.auxr = sem(f"{n}_auxr")
            self.r = sem(f"{n}_r")
            self.qn = sem(f"{n}_qn")
            self.score = sem(f"{n}_score")
            self.mx = sem(f"{n}_mx")
            self.masked = sem(f"{n}_masked")
            self.expd = sem(f"{n}_expd")
            self.rs = sem(f"{n}_rs")
            self.pn = sem(f"{n}_pn")
            self.pt = sem(f"{n}_pt")
            self.ptr = sem(f"{n}_ptr")
            self.pv = sem(f"{n}_pv")
            self.ohi = sem(f"{n}_ohi")
            self.olo = sem(f"{n}_olo")

    class Ffn:

        def __init__(self, n):
            self.up = sem(f"{n}_up")
            self.tap0 = sem(f"{n}_tap0")
            self.tap1 = sem(f"{n}_tap1")
            self.conv = sem(f"{n}_conv")
            self.silu = sem(f"{n}_silu")
            self.gated = sem(f"{n}_gated")
            self.ghi = sem(f"{n}_ghi")
            self.glo = sem(f"{n}_glo")

    att = [Att("aA"), Att("aB"), Att("aC")]
    ffn = [Ffn("fA"), Ffn("fB"), Ffn("fC")]
    pre_out = sem("pre_out")
    pre_act = sem("pre_act")
    pre_dve = sem("pre_dve")
    pre_pool = sem("pre_pool")
    tap = sem("tap")
    tap_pool = sem("tap_pool")
    bias_in = sem("bias_in")
    ln_pe = sem("ln_pe")
    ln_dve = sem("ln_dve")
    ln_act = sem("ln_act")
    side_lo = sem("side_lo")

    def at(base, per, i):
        return base if i is None else base + per * i

    def past(eng, s, base, per, i):
        if i is not None or base > 0:
            eng.wait_ge(s, at(base, per, i))

    def own_wait(i):
        if i is not None:
            n = next(scratch_col) % 64
            nc.vector.memset(scratch[:, n:n + 1], 0.0)

    def split_hi(eng, c, per, i):
        c = c + AHEAD_HI
        if i is None and c >= N_CHUNKS:
            return
        s = c % RING
        eng.wait_ge(w_loaded[s], at(16 * (c // RING + 1), 16 * per // RING, i))
        past(eng, tiles, c - RING + 1, per, i)
        nc.scalar.activation(w_hi[s][:], w_raw[s][:], ACT.Copy).then_inc(w_hi_done, 1)

    def split_lo(eng, c, per, i):
        c = c + AHEAD
        if i is None and c >= N_CHUNKS:
            return
        s = c % RING
        eng.wait_ge(w_hi_done, at(c + 1, per, i))
        nc.vector.tensor_tensor(w_lo[s][:], w_raw[s][:], w_hi[s][:].bitcast(F32),
                                ALU.subtract).then_inc(w_lo_done, 1)

    def project_k(eng, c, out, hi, lo, k):
        s = c % RING
        wh, wl = w_hi[s][:, k * P:(k + 1) * P], w_lo[s][:, k * P:(k + 1) * P]
        nc.tensor.matmul(out, wh, hi[:, k, :], start=(k == 0), stop=False)
        nc.tensor.matmul(out, wh, lo[:, k, :], start=False, stop=False)
        last = nc.tensor.matmul(out, wl, hi[:, k, :], start=False, stop=(k == KT - 1))
        if k == KT - 1:
            last.then_inc(tiles, 1)

    def project(eng, c, per, i, out, hi, lo):
        eng.wait_ge(w_lo_done, at(c + 1, per, i))
        for k in range(KT):
            project_k(eng, c, out, hi, lo, k)

    def project_first(eng, c, out0, out1, e, lag):
        for k in range(KT + lag):
            if k < KT:
                if k == 0:
                    eng.wait_ge(w_lo_done, c + 1)
                eng.wait_ge(x_lo, KT * e + k + 1)
                project_k(eng, c, out0, xg_hi, xg_lo, k)
            if k >= lag:
                if k == lag:
                    eng.wait_ge(w_lo_done, c + 2)
                project_k(eng, c + 1, out1, xg_hi, xg_lo, k - lag)
            if k == KT - 1 and e > 0:
                resid_pe(eng, e, 0)
        if e == 0:
            resid_pe(eng, e, 0)
        resid_pe(eng, e, 1)

    def resid_dve_add(eng, m, src, c):
        eng.wait_ge(tiles, c + 1)
        nc.vector.tensor_tensor(xT[:, m, :], src, xT[:, m, :], ALU.add).then_inc(x_new, 1)

    def resid_act(eng, e, m):
        if e == 0:
            eng.wait_ge(x_in[m // (KT // 2)], 16)
            eng.wait_ge(par_in, 16)
        else:
            eng.wait_ge(x_new, KT * (e - 1) + m + 1)
        g = PAR_NORM + KT * e + m
        nc.scalar.activation(xg_hi[:, m, :], xT[:, m, :], ACT.Copy, scale=par[:, g:g + 1]).then_inc(x_hi, 1)
        if e > 0:
            nc.scalar.activation(sqx[m][:], xT[:, m, :], ACT.Square).then_inc(x_sq, 1)

    def resid_dve_lo(eng, e, m):
        eng.wait_ge(x_hi, KT * e + m + 1)
        if e == 0:
            eng.wait_ge(x_in[m // (KT // 2)], 16)
        g = PAR_NORM + KT * e + m
        nc.vector.scalar_tensor_tensor(xg_lo[:, m, :], xT[:, m, :], par[:, g:g + 1], xg_hi[:, m, :].bitcast(F32),
                                       ALU.mult, ALU.subtract).then_inc(x_lo, 1)

    def resid_pool(eng, e):
        if e == 0:
            for m in range(KT):
                eng.wait_ge(x_in[m // (KT // 2)], 16)
                nc.gpsimd.tensor_tensor(sqx[m][:], xT[:, m, :], xT[:, m, :], ALU.mult).then_inc(x_sq, 1)
        for n, (to, other) in enumerate(((0, 1), (2, 3), (0, 2), (4, 5), (6, 7), (4, 6))):
            if n % 3 < 2:
                eng.wait_ge(x_sq, KT * e + other + 1)
            else:
                eng.wait_ge(x_add, 6 * e + n)
            nc.gpsimd.tensor_tensor(sqx[to][:], sqx[to][:], sqx[other][:], ALU.add).then_inc(x_add, 1)

    def resid_pe(eng, e, h):
        eng.wait_ge(x_add, 6 * e + 3 * h + 3)
        if e == 0:
            eng.wait_ge(con_in, 16)
        nc.tensor.matmul(bank(SS), con[:, CON_ONES:CON_ONES + P], sqx[4 * h][:], start=(h == 0), stop=(h == 1)).then_inc(x_ss, 1)

    def resid_act_r(eng, e):
        eng.wait_ge(x_ss, 2 * (e + 1))
        eng.wait_ge(con_in, 16)
        nc.scalar.activation(ln_x[:], bank(SS), ACT.Ln, scale=1.0 / D, bias=con[:, CON_EPS:CON_EPS + 1]).then_inc(x_ln, 1)
        eng.wait_ge(x_ln, e + 1)
        nc.scalar.activation(rms_r[:], ln_x[:], ACT.Exp, scale=-0.5).then_inc(x_r, 1)

    EVENTS3 = dict(
        pe=(("S0", 2), ("T0", 5), ("S1", 6), ("T1", 9), ("PV", 10)),
        dve=(("S0", 3), ("N0", 5), ("S1", 7), ("N1", 9), ("X", 12)),
        act=(("S0", 4), ("E0", 6), ("S1", 8), ("E1", 10), ("X", 11)),
        pool=())
    EVENTS1 = dict(
        pe=(("S0", 2), ("S1", 2), ("T0", 5), ("T1", 5), ("PV", 6)),
        dve=(("S0", 3), ("S1", 3), ("N0", 5), ("N1", 5), ("X", 8)),
        act=(("S0", 4), ("S1", 4), ("E0", 6), ("E1", 6), ("X", 7)),
        pool=())
    STAGES = [
        dict(c0=A_QKV, nd=NDIL, pairs=PAIRS_AB, events=EVENTS3, norm=0, rope=rope_t, gain=PAR_GAIN, mask=CON_MASKA),
        dict(c0=B_QKV, nd=1, pairs=PAIRS_AB, events=EVENTS1, norm=2, rope=rope_b, gain=PAR_GAIN + 2 * NDIL, mask=CON_MASK1),
        dict(c0=C_QKV, nd=1, pairs=PAIRS_C, events=EVENTS1, norm=4, rope=None, gain=PAR_GAIN + 2 * NDIL + 2, mask=CON_MASK1),
    ]

    def att_stage(eng, who, st, tile, event, after=None):
        S = STAGES[st]
        T, pairs = 3 * S["nd"], S["pairs"]
        every = [o for evs in S["events"].values() for _, o in evs]
        reach = 1 + max(every) // T

        def window(w, per, i):
            for t in range(T):
                tile(eng, st, w * T + t, per * T, i)
                here = sorted((-(o // T), x) for x, (_, o) in enumerate(S["events"][who]) if o % T == t)
                for late, x in here:
                    pr = w - 1 + late
                    if 0 <= pr < pairs:
                        event(eng, st, S["events"][who][x][0], pr, per, i)
                if after is not None and w >= pairs:
                    after((w - pairs) * T + t)

        for w in range(reach):
            window(w, 0, None)
        turns = (pairs - reach) // 2
        if turns:
            with eng.Fori(0, turns) as i:
                for u in range(2):
                    window(reach + u, 2, i)
        for w in range(reach + 2 * turns, pairs + reach):
            window(w, 0, None)

    def kind(S, n):
        T = 3 * S["nd"]
        return n % 3, (n % T) // 3, (n // T) % 2, n - n // 3 if n % 3 < 2 else None

    def qk_no(n):
        return 2 * (n // 3) + n % 3

    def score_out(S, h, qt, g):
        if S["nd"] == 1:
            o = (3 + h) * 512 + (0, P)[qt]
        else:
            o = 3 * 512 + (g * P if qt == 0 else 512 + g * 2 * P)
        return ps[:, o:o + (qt + 1) * P]

    def score_all(S, h, qt):
        w = S["nd"] * P * (qt + 1)
        o = (3 + h) * 512 + (0, P)[qt] if S["nd"] == 1 else (3 + qt) * 512
        return ps[:, o:o + w]

    def prob_cols(S, qt):
        w = S["nd"] * P
        return (0, w) if qt == 0 else (w, 3 * w)

    def pt_bank(S, h, g):
        return 5 + h if S["nd"] == 1 else 3 + g

    def pv_out(S, b):
        return (7 * 512 + b * TOK) if S["nd"] == 1 else (6 + b) * 512

    def aux_out(m, lo=0, n=TOK):
        return bank((m + 1) % 3, TOK + lo, n)

    def pe_tile(eng, st, n, per, i):
        S, a = STAGES[st], att[st]
        N = 3 * S["nd"] * S["pairs"]
        if i is None and st < 2 and n < 2:
            if n == 0:
                project_first(eng, S["c0"], bank(0), bank(1), S["norm"], 1 if st else 4)
        elif i is not None or n < N:
            past(eng, a.raw, n - 2, per, i)
            past(eng, a.auxr, n - 3, per, i)
            project(eng, S["c0"] + n, per, i, bank(n % 3), xg_hi, xg_lo)
        m = n - 2
        if i is None and (m < 0 or m >= N):
            return
        role = m % 3
        if st == 0 and m == 0 and i is None:
            eng.wait_ge(blk_in, 1)
        eng.wait_ge(a.raw, at(m + 2 if i is not None else min(m + 2, N), per, i))
        if role < 2:
            eng.wait_ge(a.sq, at(qk_no(m) + 1, per * 2 // 3, i))
            if S["rope"] is None:
                nc.tensor.matmul(aux_out(m), con[:, CON_BLK:CON_BLK + P], qk_rope[role][:],
                                 start=True, stop=True).then_inc(a.aux, 1)
            else:
                eng.wait_ge(a.sqlo, at(qk_no(m) + 1, per * 2 // 3, i))
                nc.tensor.matmul(aux_out(m), blk[:], qk_sq[role][:], start=True, stop=False)
                nc.tensor.matmul(aux_out(m), blk[:], sq_lo[role][:], start=False, stop=True).then_inc(a.aux, 1)
        else:
            for tt in range(2):
                last = nc.tensor.transpose(aux_out(m, tt * P, P), v_t[:, tt * P:(tt + 1) * P],
                                           con[:, CON_ID:CON_ID + P])
            last.then_inc(a.aux, 1)

    def pe_event(eng, st, what, pr, per, i):
        S, a = STAGES[st], att[st]
        nd, T, b = S["nd"], 3 * S["nd"], pr % 2
        if what[0] == "S":
            h = int(what[1])
            lo, hi = HD * h, HD * h + HD
            eng.wait_ge(a.qn, at(2 * nd * (pr + 1), 2 * nd * per, i))
            if nd > 1 and h == 1:
                eng.wait_ge(a.ptr, at(2 * pr + 1, 2 * per, i))
            if st == 2:
                eng.wait_ge(bias_in, 1)
            for qt in range(2):
                for g in range(nd):
                    q, k = qk_n[b][g]
                    out = score_out(S, h, qt, g)
                    last = nc.tensor.matmul(out, q[lo:hi, qt * P:(qt + 1) * P], k[lo:hi, 0:(qt + 1) * P],
                                            start=True, stop=(st < 2))
                    if st == 2:
                        last = nc.tensor.matmul(out, con[0:HEADS_C, CON_ONES:CON_ONES + P],
                                                bias_k[:, ds(at((2 * pr + h) * TOK, 2 * per * TOK, i), (qt + 1) * P)],
                                                start=False, stop=True)
            last.then_inc(a.score, 1)
        elif what[0] == "T":
            h = int(what[1])
            eng.wait_ge(a.pn, at(2 * pr + h + 1, 2 * per, i))
            w = nd * P
            for g in range(nd):
                bk = pt_bank(S, h, g)
                for n, o in enumerate((g * P, w + g * 2 * P, w + g * 2 * P + P)):
                    last = nc.tensor.transpose(bank(bk, n * P, P), prob[h][:, o:o + P], con[:, CON_ID:CON_ID + P])
            last.then_inc(a.pt, 1)
        elif what == "PV":
            eng.wait_ge(a.ptr, at(2 * pr + 2, 2 * per, i))
            eng.wait_ge(a.auxr, at(T * pr + T, T * per, i))
            if nd == 1:
                past(eng, a.olo, pr, per, i)
            for g in range(nd):
                for kt, q0 in ((0, 0), (1, P)):
                    for h in range(2):
                        lo, hi = HD * h, HD * h + HD
                        last = nc.tensor.matmul(ps[lo:hi, pv_out(S, b) + q0:pv_out(S, b) + TOK],
                                                v_n[b][g][:, kt, lo:hi],
                                                prob_t[h][:, g, 2 * P * kt:2 * P * kt + TOK - q0],
                                                start=(g == 0 and kt == 0), stop=(g == nd - 1 and kt == 1),
                                                skip_group_check=True)
            last.then_inc(a.pv, 1)

    def rope_tables(tab, g, gains):
        for k in range(2 * g, 2 * g + 2):
            for w, (src, col) in enumerate(((CON_COS, PAR_GAIN), (CON_SIN, PAR_SWAP))):
                c = col + gains + k
                nc.scalar.activation(tab[:, k, w, :], con[:, src:src + TOK], ACT.Copy,
                                     scale=par[:, c:c + 1]).then_inc(tables, 1)

    def act_tile(eng, st, n, per, i):
        S, a = STAGES[st], att[st]
        N = 3 * S["nd"] * S["pairs"]
        if i is not None or n < N + RING - AHEAD_HI:
            split_hi(eng, S["c0"] + n, per, i)
        if n == 1 and st < 2:
            resid_act_r(eng, S["norm"])
        if st == 0 and n in (2, 3, 4):
            rope_tables(*((rope_t, 1, 0), (rope_t, 2, 0), (rope_b, 0, 2 * NDIL))[n - 2])
        m = n - 1
        if (i is not None or 0 <= m < N) and m % 3 < 2:
            eng.wait_ge(a.raw, at(m + 1, per, i))
            sq = (qk_rope if S["rope"] is None else qk_sq)[m % 3][:]
            nc.scalar.activation(sq, qk_raw[m % 3][:], ACT.Square).then_inc(a.sq, 1)
        m = n - 3
        if i is None and (m < 0 or m >= N):
            return
        role, g, b, _ = kind(S, m)
        eng.wait_ge(a.aux, at(m + 1, per, i))
        if role < 2:
            e = CON_EPS + 1 - role
            nc.scalar.activation(qk_r[role][:], aux_out(m), ACT.Ln, scale=(1.0, 1.0 / HD)[role],
                                 bias=con[:, e:e + 1]).then_inc(a.auxr, 1)
            eng.wait_ge(a.auxr, at(m + 1, per, i))
            nc.scalar.activation(qk_r[role][:], qk_r[role][:], ACT.Exp, scale=-0.5).then_inc(a.r, 1)
        else:
            nc.scalar.activation(v_n[b][g][:], aux_out(m).rearrange("p (t c) -> p t c", t=2),
                                 ACT.Copy).then_inc(a.auxr, 1)

    def act_event(eng, st, what, pr, per, i):
        S, a = STAGES[st], att[st]
        nd, b = S["nd"], pr % 2
        if what[0] == "S":
            h = int(what[1])
            eng.wait_ge(a.masked, at(2 * pr + h + 1, 2 * per, i))
            for qt in range(2):
                o0, o1 = prob_cols(S, qt)
                last = nc.scalar.activation(prob[h][:, o0:o1], prob[h][:, o0:o1], ACT.Exp, bias=nmax[h][:, qt:qt + 1],
                                            accum_out=ssum[h][:, qt:qt + 1])
            last.then_inc(a.expd, 1)
        elif what[0] == "E":
            h = int(what[1])
            eng.wait_ge(a.pt, at(2 * pr + h + 1, 2 * per, i))
            b0 = pt_bank(S, h, 0) * 512
            nc.scalar.activation(prob_t[h][:, 0:nd, :],
                                 ps[:, b0:b0 + nd * 512].rearrange("p (g c) -> p g c", c=512)[:, :, 0:3 * P],
                                 ACT.Copy).then_inc(a.ptr, 1)
        elif what == "X":
            eng.wait_ge(a.pv, at(pr + 1, per, i))
            nc.scalar.activation(mix_hi[:, ds(at(pr, per, i), 1), :], ps[:, pv_out(S, b):pv_out(S, b) + TOK].rearrange("p (o t) -> p o t", o=1),
                                 ACT.Copy).then_inc(a.ohi, 1)

    SWAP = [p + ROPE_DIM // 2 if p < ROPE_DIM // 2 else p - ROPE_DIM // 2 if p < ROPE_DIM else p for p in range(32)]

    def dve_tile(eng, st, n, per, i):
        S, a = STAGES[st], att[st]
        N = 3 * S["nd"] * S["pairs"]
        if i is not None or n < N + RING - AHEAD:
            split_lo(eng, S["c0"] + n, per, i)
        m = n - 4
        if (i is not None or 0 <= m < N) and m % 3 < 2:
            role, g, b, _ = kind(S, m)
            eng.wait_ge(a.r, at(qk_no(m) + 1, per * 2 // 3, i))
            if S["rope"] is not None:
                eng.wait_ge(a.rope, at(qk_no(m) + 1, per * 2 // 3, i))
                nc.vector.tensor_tensor(qk_n[b][g][role][:], qk_rope[role][:], qk_r[role][:], ALU.mult).then_inc(a.qn, 1)
            else:
                c = S["gain"] + role
                nc.vector.scalar_tensor_tensor(qk_n[b][g][role][:], qk_raw[role][:], par[:, c:c + 1], qk_r[role][:],
                                               ALU.mult, ALU.mult).then_inc(a.qn, 1)
        m = n - 1
        if i is not None or 0 <= m < N:
            role = m % 3
            eng.wait_ge(tiles, at(S["c0"] + m + 1, per, i))
            if m == 0 and i is None:
                eng.wait_ge(x_r, S["norm"] + 1)
            if S["rope"] is None and role < 2 and m >= 3:
                eng.wait_ge(a.qn, at(qk_no(m - 3) + 1, per * 2 // 3, i))
            nc.vector.tensor_tensor((qk_raw + [v_t])[role][:], bank(m % 3), rms_r[:], ALU.mult).then_inc(a.raw, 1)
            if role < 2 and S["rope"] is not None:
                eng.wait_ge(a.raw, at(m + 1, per, i))
                own_wait(i)
                nc.vector.stream_shuffle(qk_swap[role][:], qk_raw[role][:], SWAP).then_inc(a.swap, 1)
        if st == 2:
            if n == 1:
                forget_bias(eng)
            conv_taps(eng, n + 2)

    def dve_event(eng, st, what, pr, per, i):
        S, a = STAGES[st], att[st]
        b = pr % 2
        if what[0] == "S":
            h = int(what[1])
            eng.wait_ge(a.score, at(2 * pr + h + 1, 2 * per, i))
            own_wait(i)
            mo = S["mask"]
            if st == 0 and i is None and pr == 0:
                eng.wait_ge(rest_in, 32)
            for qt in range(2):
                o0, o1 = prob_cols(S, qt)
                last = nc.vector.tensor_tensor_reduce(prob[h][:, o0:o1], score_all(S, h, qt), con[:, mo + o0:mo + o1],
                                                      1.0, NEG, ALU.add, ALU.max, smax[h][:, qt:qt + 1])
            last.then_inc(a.mx, 1)
            eng.wait_ge(a.mx, at(2 * pr + h + 1, 2 * per, i))
            nc.vector.tensor_scalar(nmax[h][:], smax[h][:], -1.0, None, ALU.mult).then_inc(a.masked, 1)
        elif what[0] == "N":
            h = int(what[1])
            eng.wait_ge(a.expd, at(2 * pr + h + 1, 2 * per, i))
            nc.vector.reciprocal(rsum[h][:], ssum[h][:]).then_inc(a.rs, 1)
            eng.wait_ge(a.rs, at(2 * pr + h + 1, 2 * per, i))
            for qt in range(2):
                o0, o1 = prob_cols(S, qt)
                last = nc.vector.tensor_scalar(prob[h][:, o0:o1], prob[h][:, o0:o1], rsum[h][:, qt:qt + 1], None, ALU.mult)
            last.then_inc(a.pn, 1)
        elif what == "X":
            eng.wait_ge(a.ohi, at(pr + 1, per, i))
            nc.vector.tensor_tensor(mix_lo[:, ds(at(pr, per, i), 1), :], ps[:, pv_out(S, b):pv_out(S, b) + TOK].rearrange("p (o t) -> p o t", o=1),
                                    mix_hi[:, ds(at(pr, per, i), 1), :].bitcast(F32), ALU.subtract).then_inc(a.olo, 1)

    def pool_tile(eng, st, n, per, i):
        S, a = STAGES[st], att[st]
        N = 3 * S["nd"] * S["pairs"]
        m = n - 1
        if (i is None and not 0 <= m < N) or m % 3 == 2:
            return
        role, g, _, _ = kind(S, m)
        k, kp = qk_no(m) + 1, per * 2 // 3
        tab = S["rope"]
        if st == 0 and m < 3 * NDIL:
            eng.wait_ge(tables, 4 * (g + 1))
        if st == 1 and m == 0:
            eng.wait_ge(tables, 4 * NDIL + 4)
        eng.wait_ge(a.raw, at(m + 1, per, i))
        nc.gpsimd.tensor_tensor(sq_all[:], qk_raw[role][:], qk_raw[role][:], ALU.mult).then_inc(a.sqall, 1)
        nc.gpsimd.tensor_tensor(rope_1[:], qk_raw[role][:], tab[:, 2 * g + role, 0, :], ALU.mult).then_inc(a.rot1, 1)
        eng.wait_ge(a.sq, at(k, kp, i))
        eng.wait_ge(a.sqall, at(k, kp, i))
        nc.gpsimd.tensor_tensor(sq_lo[role][:], sq_all[:], qk_sq[role][:].bitcast(F32), ALU.subtract).then_inc(a.sqlo, 1)
        eng.wait_ge(a.swap, at(k, kp, i))
        nc.gpsimd.tensor_tensor(rope_2[:], qk_swap[role][:], tab[:, 2 * g + role, 1, :], ALU.mult).then_inc(a.rot2, 1)
        eng.wait_ge(a.rot1, at(k, kp, i))
        eng.wait_ge(a.rot2, at(k, kp, i))
        nc.gpsimd.tensor_tensor(qk_rope[role][:], rope_1[:], rope_2[:], ALU.add).then_inc(a.rope, 1)
        eng.wait_ge(a.rope, at(k, kp, i))
        eng.wait_ge(a.sqlo, at(k, kp, i))

    def pool_event(eng, st, what, pr, per, i):
        return

    NEXT = RING

    def out_bank(m):
        return bank((m + 1) % 3, m // 3 * TOK) if m < NEXT else bank(SS + 1 + m - NEXT)

    OUT_C0 = (A_OUT, B_OUT, C_OUT)
    FIVE, FOUR = range(5), (0, 3, 1, 4)
    OUT_EARLY = (
        {0: [(0, range(6))], 1: [(1, range(6))], 2: [(2, range(6)), (3, range(6))], 5: [(4, range(6))],
         6: [(m, (6,)) for m in FIVE] + [(5, range(4))], 9: [(5, (4, 5))]},
        {0: [(0, range(5)), (3, range(5))], 1: [(1, range(5))], 2: [(2, range(5)), (4, range(5))],
         3: [(m, (5,)) for m in FIVE], 5: [(m, (6,)) for m in FIVE], 6: [(5, range(4))]},
        {0: [(0, (0,)), (3, (0,))], 1: [(1, (0,)), (0, (1,)), (3, (1,)), (1, (1,)), (4, (0, 1))],
         4: [(m, (6, 7)) for m in FOUR] + [(m, (2,)) for m in FOUR], 6: [(m, (4, 5)) for m in FOUR]},
    )

    def out_part(eng, st, m, ks, last):
        c = OUT_C0[st] + m
        s = c % RING
        eng.wait_ge(w_lo_done, c + 1)
        pairs = [k for k in ks if k < STAGES[st]["pairs"]]
        if pairs:
            eng.wait_ge(att[st].olo, max(pairs) + 1)
        if len(pairs) < len(ks):
            eng.wait_ge(side_lo, 4 if 4 in ks or 5 in ks else 2)
        for k in ks:
            wh, wl = w_hi[s][:, k * P:(k + 1) * P], w_lo[s][:, k * P:(k + 1) * P]
            end = last and k == ks[-1]
            nc.tensor.matmul(out_bank(m), wh, mix_hi[:, k, :], start=False, stop=False, skip_group_check=True)
            nc.tensor.matmul(out_bank(m), wh, mix_lo[:, k, :], start=False, stop=False, skip_group_check=True)
            mm = nc.tensor.matmul(out_bank(m), wl, mix_hi[:, k, :], start=False, stop=end, skip_group_check=True)
        if last:
            mm.then_inc(tiles, 1)

    def out_early(eng, st):
        def after(k):
            if k < (3 if st < 2 else 2):
                eng.wait_ge(att[st].auxr, 3 * STAGES[st]["nd"] * STAGES[st]["pairs"] + k - 2)
                out_zero(eng, ((k + 1) % 3,))
            for part in OUT_EARLY[st].get(k, ()):
                out_part(eng, st, *part, False)
        return after

    def out_zero(eng, banks):
        eng.wait_ge(zeroed, 1)
        for bk in banks:
            nc.tensor.matmul(bank(bk, 0, 512), zero[:, 0:P], zero[:, 0:512], start=True, stop=True, skip_group_check=True)

    def out_pe(eng, st):
        done = [k for parts in OUT_EARLY[st].values() for m, ks in parts for k in [(m, k) for k in ks]]
        if st == 2:
            eng.wait_ge(side_lo, 4)
            out_zero(eng, (0,))
        out_zero(eng, (SS + 1, SS + 2))
        for m in range(KT):
            out_part(eng, st, m, [k for k in range(KT) if (m, k) not in done], True)

    def out_act(eng, c0, e):
        for m in range(KT):
            if m in (0, 1, 2, 4):
                split_hi(eng, c0 + RING - AHEAD_HI + (0, 1, 2, 4).index(m), 0, None)
            resid_act(eng, e, m)
        for m in range(4, KT + AHEAD_HI - RING):
            split_hi(eng, c0 + RING - AHEAD_HI + m, 0, None)

    def out_dve(eng, c0, e):
        def add(m):
            resid_dve_add(eng, m, out_bank(m), c0 + (m + 3 if m < 3 else m))

        for m in range(NEXT):
            add(m)
            if m in (0, 2, 5):
                split_lo(eng, c0 + RING - AHEAD + (0, 2, 5).index(m), 0, None)
        for m in range(KT):
            if m >= NEXT:
                add(m)
            resid_dve_lo(eng, e, m)
            if m == 3:
                split_lo(eng, c0 + RING - AHEAD + m, 0, None)
        for m in range(4, KT + AHEAD - RING):
            split_lo(eng, c0 + RING - AHEAD + m, 0, None)

    FFN_C0 = (A_FFN, B_FFN, C_FFN)

    def acc(m):
        return bank(4 + m // 2, (m % 2) * TOK)

    def ffn_chunk(f, j):
        return FFN_C0[f] + (2 * j if j < 2 else 4 + 3 * (j - 2) if j < FT else 3 * FT - 2 + j - FT)

    def ffn_stage(eng, f, step):
        first = 4
        turns = (FT - first) // 2 - (f == 2)
        for j in range(first):
            step(eng, j, 0, None)
        with eng.Fori(0, turns) as i:
            for u in range(2):
                step(eng, first + u, 2, i)
        for j in range(first + 2 * turns, FT + 2):
            step(eng, j, 0, None)

    def ffn_pe(f):
        e = 2 * f + 1

        def step(eng, j, per, i):
            F, b, c, cp = ffn[f], j % 2, ffn_chunk(f, j), 3 * per
            if i is not None or j < FT:
                if i is None and j == 0:
                    eng.wait_ge(x_new, KT * (e - 1) + NEXT)
                past(eng, F.up, 2 * (j - 1), 2 * per, i)
                if i is None and j == 0:
                    project_first(eng, c, bank(0), bank(2), e, 3)
                else:
                    project(eng, c, cp, i, bank(b), xg_hi, xg_lo)
                    if i is None and j == 1:
                        eng.wait_ge(x_r, e + 1)
                    project(eng, c + 1, cp, i, bank(2 + b), xg_hi, xg_lo)
                c += 2
            if i is None and j == 1:
                eng.wait_ge(x_new, KT * e)
                out_zero(eng, range(4, 8))
            if i is not None or j >= 2:
                s = c % RING
                eng.wait_ge(w_lo_done, at(c + 1, cp, i))
                eng.wait_ge(F.glo, at(j - 1, per, i))
                for m in range(KT):
                    wh, wl = w_hi[s][:, m * P:(m + 1) * P], w_lo[s][:, m * P:(m + 1) * P]
                    nc.tensor.matmul(acc(m), wh, g_hi[b][:], start=False, stop=False, skip_group_check=True)
                    nc.tensor.matmul(acc(m), wh, g_lo[b][:], start=False, stop=False, skip_group_check=True)
                    last = nc.tensor.matmul(acc(m), wl, g_hi[b][:], start=False, stop=True, skip_group_check=True)
                    if m == KT - 1:
                        last.then_inc(tiles, 1)
                    elif i is None and j == FT + 1:
                        last.then_inc(acc_done, 1)
        return step

    def par_col(f, j, per, i, k):
        return par[:, ds(at(PAR_FFN + 8 * (f * FT + j) + k, 8 * per, i), 1)]

    def ffn_act(f):
        def step(eng, j, per, i):
            F, c, cp = ffn[f], ffn_chunk(f, j), 3 * per
            n = 3 if 2 <= j < FT else 2 if j < 2 else 1
            split_hi(eng, c, cp, i)
            if j == 1:
                resid_act_r(eng, 2 * f + 1)
                nc.scalar.preload_act_table_set("silu_and_others")
                eng.wait_ge(rest_in, 32)
            t = j - 2
            if i is not None or 0 <= t < FT:
                if i is not None or t >= 2:
                    eng.wait_ge(tiles, at(ffn_chunk(f, t) + 3, cp, i))
                eng.wait_ge(F.gated, at(t + 1, per, i))
                nc.scalar.activation(g_hi[t % 2][:], gated[:], ACT.Copy).then_inc(F.ghi, 1)
            t = j - 1
            work = i is not None or 0 <= t < FT
            if work:
                for s in range(2):
                    eng.wait_ge(F.up, at(2 * t + 1 + s, 2 * per, i))
                    nc.scalar.activation(cv_s[t % 2][s][:], up_s[t % 2][s][:], ACT.Identity,
                                         scale=par_col(f, t, per, i, 4 * s + 2),
                                         bias=par_col(f, t, per, i, 4 * s + 3)).then_inc(F.tap0, 1)
            for q in range(1, n):
                split_hi(eng, c + q, cp, i)
            if work:
                eng.wait_ge(F.conv, at(2 * t + 1, 2 * per, i))
                nc.scalar.activation(gate_s[:], cv_s[t % 2][0][:], ACT.Silu).then_inc(F.silu, 1)
        return step

    def ffn_dve(f):
        def step(eng, j, per, i):
            F, c, cp = ffn[f], ffn_chunk(f, j), 3 * per
            n = 3 if 2 <= j < FT else 2 if j < 2 else 1
            t = j - 1
            b = t % 2
            work = i is not None or 0 <= t < FT
            split_lo(eng, c, cp, i)
            if work:
                if i is None and t == 0:
                    eng.wait_ge(x_r, 2 * f + 2)
                for s in range(2):
                    eng.wait_ge(tiles, at(ffn_chunk(f, t) + 1 + s, cp, i))
                    nc.vector.tensor_tensor(up_s[b][s][:], bank(2 * s + b), rms_r[:], ALU.mult).then_inc(F.up, 1)
            if n > 1:
                split_lo(eng, c + 1, cp, i)
            if i is not None or j >= 2:
                eng.wait_ge(F.ghi, at(j - 1, per, i))
                nc.vector.tensor_tensor(g_lo[j % 2][:], gated[:], g_hi[j % 2][:].bitcast(F32),
                                        ALU.subtract).then_inc(F.glo, 1)
            if work:
                for k in range(1, 3):
                    for s in range(2):
                        if k == 1:
                            eng.wait_ge(F.tap0, at(2 * t + 1 + s, 2 * per, i))
                        else:
                            eng.wait_ge(F.tap1, at(2 * t + 1 + s, 2 * per, i))
                        nc.vector.scalar_tensor_tensor(cv_s[b][s][:, k:TOK], up_s[b][s][:, 0:TOK - k],
                                                       par_col(f, t, per, i, 4 * s + 2 - k), cv_s[b][s][:, k:TOK],
                                                       ALU.mult, ALU.add).then_inc(F.tap1 if k == 1 else F.conv, 1)
            if n > 2:
                split_lo(eng, c + 2, cp, i)
        return step

    def ffn_pool(f):
        def step(eng, j, per, i):
            F, t = ffn[f], j - 1
            if i is None and not 0 <= t < FT:
                return
            eng.wait_ge(F.silu, at(t + 1, per, i))
            eng.wait_ge(F.conv, at(2 * t + 2, 2 * per, i))
            past(eng, F.glo, t, per, i)
            nc.gpsimd.tensor_tensor(gated[:], gate_s[:], cv_s[t % 2][1][:], ALU.mult).then_inc(F.gated, 1)
        return step

    def ffn_end_act(eng, e):
        for m in range(KT):
            resid_act(eng, e, m)

    def ffn_end_dve(eng, f):
        for m in range(KT):
            if m < KT - 2:
                eng.wait_ge(acc_done, f * (KT - 1) + (m | 1) + 1)
            else:
                eng.wait_ge(tiles, FFN_C0[f] + 3 * FT)
            nc.vector.tensor_tensor(xT[:, m, :], acc(m), xT[:, m, :], ALU.add).then_inc(x_new, 1)
            if m >= 1 and f < 2:
                resid_dve_lo(eng, 2 * f + 2, m - 1)
        if f < 2:
            resid_dve_lo(eng, 2 * f + 2, KT - 1)

    FORGET = 4
    PRE_OUT = [cv_a[0][:], cv_b[0][:], cv_a[1][:], cv_b[1][:], fg[0],
               pl[0][0][:, POOL_PAD:POOL_PAD + TOK], pl[1][0][:, POOL_PAD:POOL_PAD + TOK]]

    def pre_pe(eng):
        project_first(eng, C_PRE, bank(0), bank(1), 4, 1)
        for n in range(2, N_PRE):
            past(eng, pre_out, n - 2, 0, None)
            project(eng, C_PRE + n, 0, None, bank(n % 3), xg_hi, xg_lo)

    def pre_act_f(eng):
        for n in range(N_PRE):
            split_hi(eng, C_PRE + n, 0, None)
            if n == 1:
                resid_act_r(eng, 4)
            if n in (3, 5):
                t = n // 2 - 1
                eng.wait_ge(pre_out, 2 * t + 2)
                if t == 0:
                    nc.scalar.preload_act_table_set("sigmoid_and_others")
                nc.scalar.activation(cv_e[t][:], cv_b[t][:], ACT.Sigmoid).then_inc(pre_act, 1)
        nc.scalar.preload_act_table_set("natural_log_exp_and_others")
        eng.wait_ge(pre_out, FORGET + 1)
        nc.scalar.activation(fg[1], fg[0], ACT.Identity, bias=par[0:HEADS_C, PAR_BF:PAR_BF + 1]).then_inc(pre_act, 1)
        eng.wait_ge(pre_dve, 2)
        nc.scalar.activation(fg[3], fg[2], ACT.Exp, scale=-1.0).then_inc(pre_act, 1)
        eng.wait_ge(pre_act, 4)
        nc.scalar.activation(fg[4], fg[3], ACT.Ln, bias=1.0).then_inc(pre_act, 1)

    def pre_dve_f(eng):
        def glu(t):
            eng.wait_ge(pre_act, 1 + t)
            eng.wait_ge(zeroed, 3)
            nc.vector.tensor_tensor(cv_h[t][:, PADC:PADC + TOK], cv_a[t][:], cv_e[t][:], ALU.mult).then_inc(pre_dve, 1)

        def out(n):
            if n == 0:
                eng.wait_ge(x_r, 5)
            if n == 5:
                eng.wait_ge(pl_zeroed, 6)
            eng.wait_ge(tiles, C_PRE + n + 1)
            src = bank(n % 3)[0:HEADS_C, :] if n == FORGET else bank(n % 3)
            r = rms_r[0:HEADS_C, :] if n == FORGET else rms_r[:]
            nc.vector.tensor_tensor(PRE_OUT[n], src, r, ALU.mult).then_inc(pre_out, 1)

        for n in range(N_PRE):
            split_lo(eng, C_PRE + n, 0, None)
            if n >= 1:
                out(n - 1)
            if n == 4:
                glu(0)
            if n >= 5:
                conv_taps(eng, n - 5)
        out(N_PRE - 1)
        eng.wait_ge(pre_act, 3)
        nc.vector.scalar_tensor_tensor(fg[2], fg[1], -1.0, fg[1], ALU.mult, ALU.max).then_inc(pre_dve, 1)
        glu(1)
        eng.wait_ge(pre_act, 5)
        nc.vector.scalar_tensor_tensor(fg[5], fg[1], 0.0, fg[4], ALU.min, ALU.subtract).then_inc(pre_dve, 1)
        eng.wait_ge(pre_dve, 4)
        nc.vector.tensor_tensor_scan(fg[2], con[0:HEADS_C, CON_ONES:CON_ONES + 1].to_broadcast([HEADS_C, TOK]),
                                     fg[5], 0.0, ALU.mult, ALU.add).then_inc(pre_dve, 1)

    def forget_bias(eng):
        eng.wait_ge(pre_dve, 5)
        for h in range(HEADS_C):
            last = nc.vector.tensor_scalar(bias_k[:, h * TOK:(h + 1) * TOK], fg[2],
                                           con[0:HEADS_C, CON_ID + h:CON_ID + h + 1], -1.0, ALU.mult, ALU.mult)
        last.then_inc(bias_in, 1)

    def pool_zeroes(eng):
        for t in range(2):
            for b in pl[t]:
                nc.gpsimd.memset(b, 0.0).then_inc(pl_zeroed, 1)

    def pre_pool_f(eng):
        n = 0
        for t in range(2):
            eng.wait_ge(pre_out, 6 + t)
            src, k = 0, 1
            steps = ((1, 0, P), (2, HD, P)) if t == 0 else ((1, 0, P), (2, 0, P), (4, 0, P), (8, HD, P))
            for s, p0, p1 in steps:
                dst = 1 if src != 1 else 2
                if p0:
                    nc.gpsimd.tensor_copy(pl[t][dst][0:HD, POOL_PAD:], pl[t][src][0:HD, POOL_PAD:]).then_inc(pre_pool, 1)
                    n += 1
                nc.gpsimd.tensor_tensor(pl[t][dst][p0:p1, s:], pl[t][src][p0:p1, s:],
                                        pl[t][src][p0:p1, 0:POOL_PAD + TOK - s], ALU.add).then_inc(pre_pool, 1)
                n += 1
                eng.wait_ge(pre_pool, n)
                src = dst
            inv = con[:, CON_INV + t * TOK:CON_INV + (t + 1) * TOK]
            s0 = pl[t][src][:, POOL_PAD:]
            nc.gpsimd.tensor_tensor(s0, s0, inv, ALU.mult).then_inc(pre_pool, 1)
            n += 1
            eng.wait_ge(pre_pool, n)
            nc.gpsimd.tensor_tensor(pl[t][3 - src][:, POOL_PAD:], s0, pl[t][0][:, POOL_PAD:], ALU.subtract).then_inc(pre_pool, 1)
            n += 1
            eng.wait_ge(pre_pool, n)
        return n

    POOL_D = [pl[0][1], pl[1][1]]
    N_POOL_STEPS = 3 + 2 + 5 + 2

    TAPS_PER = 3
    POOL_TAPS = CONV_C // 2
    DVE_TAPS = [(0, j) for j in range(CONV_C)] + [(1, j) for j in range(CONV_C - POOL_TAPS)]
    part, prods = rope_1, qk_swap

    def conv_w(t, j):
        return par[:, PAR_DW + t * CONV_C + j:PAR_DW + t * CONV_C + j + 1]

    def conv_taps(eng, n):
        for q in range(TAPS_PER * n, min(TAPS_PER * (n + 1), len(DVE_TAPS) + 1)):
            if q == len(DVE_TAPS):
                eng.wait_ge(tap_pool, 2 * POOL_TAPS - 1)
                eng.wait_ge(tap, q)
                nc.vector.tensor_tensor(cv_acc[1][:], cv_acc[1][:], part[:], ALU.add).then_inc(tap, 1)
                continue
            t, j = DVE_TAPS[q]
            src = cv_h[t][:, j:j + TOK]
            if j == 0:
                eng.wait_ge(pre_dve, (1, 3)[t])
                nc.vector.tensor_scalar(cv_acc[t][:], src, conv_w(t, j), par[:, PAR_DWB + t:PAR_DWB + t + 1],
                                        ALU.mult, ALU.add).then_inc(tap, 1)
            else:
                eng.wait_ge(tap, q)
                nc.vector.scalar_tensor_tensor(cv_acc[t][:], src, conv_w(t, j), cv_acc[t][:],
                                               ALU.mult, ALU.add).then_inc(tap, 1)

    def conv_pool(eng):
        eng.wait_ge(pre_dve, 3)
        for q in range(POOL_TAPS):
            j = CONV_C - POOL_TAPS + q
            to = part if q == 0 else prods[q % 2]
            nc.gpsimd.tensor_scalar(to[:], cv_h[1][:, j:j + TOK], conv_w(1, j), None, ALU.mult).then_inc(tap_pool, 1)
            if q > 0:
                eng.wait_ge(tap_pool, 2 * q)
                nc.gpsimd.tensor_tensor(part[:], part[:], prods[q % 2][:], ALU.add).then_inc(tap_pool, 1)

    def side_pe(eng):
        ones = con[:, CON_ONES:CON_ONES + P]

        early = out_early(eng, 2)

        def after(k):
            if k == 2:
                eng.wait_ge(att[2].auxr, 3 * PAIRS_C)
                eng.wait_ge(tap, len(DVE_TAPS) + 1)
                for t in range(2):
                    last = nc.tensor.matmul(bank(0), ones, cv_acc[t][:], start=(t == 0), stop=(t == 1))
                last.then_inc(ln_pe, 1)
            elif k == 3:
                eng.wait_ge(att[2].masked, HEADS_C)
                eng.wait_ge(ln_act, 2)
                for t in range(2):
                    last = nc.tensor.matmul(bank(4), ones, cv_e[t][:], start=(t == 0), stop=(t == 1))
                last.then_inc(ln_pe, 1)
                eng.wait_ge(pre_pool, N_POOL_STEPS)
                for t in range(2):
                    for g in range(2):
                        p0, p1 = HD * g, HD * g + HD
                        last = nc.tensor.matmul(bank(3, t * TOK)[p0:p1, :],
                                                par[p0:p1, PAR_POOLW + t * HD:PAR_POOLW + (t + 1) * HD],
                                                POOL_D[t][p0:p1, POOL_PAD:], start=True, stop=True)
                last.then_inc(ln_pe, 1)
            elif k == 5:
                eng.wait_ge(ln_act, 8)
                for o in range(2):
                    for t in range(2):
                        w = PAR_PW + t * 2 * P + o * P
                        last = nc.tensor.matmul(bank(4 * o, TOK), par[:, w:w + P], cv_a[t][:], start=(t == 0), stop=(t == 1))
                last.then_inc(ln_pe, 1)
            early(k)
        return after

    def side_act(eng):
        def after(k):
            if k == 2:
                for t in range(2):
                    eng.wait_ge(ln_dve, t + 1)
                    nc.scalar.activation(cv_e[t][:], cv_b[t][:], ACT.Square).then_inc(ln_act, 1)
            elif k == 3:
                eng.wait_ge(ln_pe, 2)
                nc.scalar.activation(ln_x[:], bank(4), ACT.Ln, scale=1.0 / (2 * P),
                                     bias=con[:, CON_EPS:CON_EPS + 1]).then_inc(ln_act, 1)
                eng.wait_ge(ln_act, 3)
                nc.scalar.activation(ln_x[:], ln_x[:], ACT.Exp, scale=-0.5).then_inc(ln_act, 1)
                eng.wait_ge(ln_pe, 3)
                for t in range(2):
                    nc.scalar.activation(mix_hi[:, 6 + t, :], bank(3, t * TOK), ACT.Copy,
                                         scale=par[:, PAR_PSC + t:PAR_PSC + t + 1]).then_inc(ln_act, 1)
            elif k == 4:
                nc.scalar.preload_act_table_set("silu_and_others")
                for t in range(2):
                    eng.wait_ge(ln_dve, 3 + t)
                    nc.scalar.activation(cv_a[t][:], cv_b[t][:], ACT.Silu, scale=par[:, PAR_LNG + t:PAR_LNG + t + 1],
                                         bias=par[:, PAR_LNB + t:PAR_LNB + t + 1]).then_inc(ln_act, 1)
                nc.scalar.preload_act_table_set("natural_log_exp_and_others")
            elif k == 6:
                eng.wait_ge(ln_pe, 4)
                for o in range(2):
                    nc.scalar.activation(mix_hi[:, 4 + o, :], bank(4 * o, TOK), ACT.Copy).then_inc(ln_act, 1)
        return after

    def side_dve(eng):
        def after(k):
            if k == 2:
                eng.wait_ge(ln_pe, 1)
                for t in range(2):
                    nc.vector.scalar_tensor_tensor(cv_b[t][:], bank(0), -1.0 / (2 * P), cv_acc[t][:],
                                                   ALU.mult, ALU.add).then_inc(ln_dve, 1)
            elif k == 3:
                eng.wait_ge(ln_act, 4)
                for t in range(2):
                    nc.vector.tensor_tensor(cv_b[t][:], cv_b[t][:], ln_x[:], ALU.mult).then_inc(ln_dve, 1)
                eng.wait_ge(ln_act, 6)
                for t in range(2):
                    nc.vector.scalar_tensor_tensor(mix_lo[:, 6 + t, :], bank(3, t * TOK), par[:, PAR_PSC + t:PAR_PSC + t + 1],
                                                   mix_hi[:, 6 + t, :].bitcast(F32), ALU.mult, ALU.subtract).then_inc(side_lo, 1)
            elif k == 6:
                for o in range(2):
                    eng.wait_ge(ln_act, 9 + o)
                    nc.vector.tensor_tensor(mix_lo[:, 4 + o, :], bank(4 * o, TOK), mix_hi[:, 4 + o, :].bitcast(F32),
                                            ALU.subtract).then_inc(side_lo, 1)
        return after

    with nc.Block() as block:

        @block.sync
        def _(sp):
            def load(s, c):
                sp.dma_start(w_raw[s][:], stream_d[ds(c, 1)].rearrange("o p n -> (o p) n")).then_inc(w_loaded[s], 16)

            half = KT // 2
            sp.dma_start(par[:, 0:PAR_FFN], par_d[:, 0:PAR_FFN]).then_inc(par_in, 16)
            sp.dma_start(xT[:, 0:half], x_d[0:half].rearrange("k p t -> p k t")).then_inc(x_in[0], 16)
            load(0, 0)
            sp.dma_start(con[:, 0:CON_COS], con_d[:, 0:CON_COS]).then_inc(con_in, 16)
            sp.dma_start(xT[:, half:KT], x_d[half:KT].rearrange("k p t -> p k t")).then_inc(x_in[1], 16)
            sp.dma_start(con[:, CON_COS:CON_MASKA], con_d[:, CON_COS:CON_MASKA]).then_inc(rope_in, 16)
            for s in range(1, AHEAD):
                load(s, s)
            sp.dma_start(con[:, CON_MASKA:], con_d[:, CON_MASKA:]).then_inc(rest_in, 16)
            load(AHEAD, AHEAD)
            sp.dma_start(par[:, PAR_FFN:], par_d[:, PAR_FFN:]).then_inc(rest_in, 16)
            for s in range(AHEAD + 1, RING):
                load(s, s)
            turns = N_CHUNKS // RING
            with sp.Fori(1, turns) as i:
                for s in range(RING):
                    sp.wait_ge(w_lo_done, i * RING + (s - RING + 1))
                    load(s, i * RING + s)
            for c in range(turns * RING, N_CHUNKS):
                sp.wait_ge(w_lo_done, c - RING + 1)
                load(c % RING, c)
            for m in range(KT):
                sp.wait_ge(x_new, 5 * KT + m + 1)
                sp.dma_start(out_d[m], xT[:, m, :]).then_inc(stored, 16)
            sp.wait_ge(stored, 16 * KT)

        @block.tensor
        def _(pe):
            for st in range(3):
                if st == 2:
                    pre_pe(pe)
                    pe.wait_ge(pre_out, N_PRE)
                    pe.wait_ge(rest_in, 32)
                att_stage(pe, "pe", st, pe_tile, pe_event, side_pe(pe) if st == 2 else out_early(pe, st))
                out_pe(pe, st)
                ffn_stage(pe, st, ffn_pe(st))

        @block.scalar
        def _(act):
            nc.scalar.preload_act_table_set("natural_log_exp_and_others")
            split_hi(act, -AHEAD_HI, 0, None)
            for m in range(KT):
                resid_act(act, 0, m)
                if m == 3:
                    split_hi(act, 1 - AHEAD_HI, 0, None)
            for c in range(2, AHEAD_HI - 1):
                split_hi(act, c - AHEAD_HI, 0, None)
            act.wait_ge(con_in, 16)
            nc.scalar.activation(blk[:], con[:, CON_BLK:CON_BLK + P], ACT.Copy).then_inc(blk_in, 1)
            act.wait_ge(rope_in, 16)
            rope_tables(rope_t, 0, 0)
            split_hi(act, AHEAD_HI - 1 - AHEAD_HI, 0, None)
            for st in range(3):
                if st == 2:
                    pre_act_f(act)
                att_stage(act, "act", st, act_tile, act_event, side_act(act) if st == 2 else None)
                out_act(act, OUT_C0[st], 2 * st + 1)
                ffn_stage(act, st, ffn_act(st))
                if st < 2:
                    nc.scalar.preload_act_table_set("natural_log_exp_and_others")
                    ffn_end_act(act, 2 * st + 2)

        @block.vector
        def _(dve):
            dve.wait_ge(par_in, 16)
            split_lo(dve, -AHEAD, 0, None)
            for m in range(KT):
                resid_dve_lo(dve, 0, m)
                if m == 3:
                    split_lo(dve, 1 - AHEAD, 0, None)
            for c in range(2, AHEAD):
                split_lo(dve, c - AHEAD, 0, None)
            for st in range(3):
                if st == 2:
                    pre_dve_f(dve)
                att_stage(dve, "dve", st, dve_tile, dve_event, side_dve(dve) if st == 2 else None)
                out_dve(dve, OUT_C0[st], 2 * st + 1)
                ffn_stage(dve, st, ffn_dve(st))
                ffn_end_dve(dve, st)

        @block.gpsimd
        def _(pool):
            nc.gpsimd.memset(zero[:], 0.0).then_inc(zeroed, 1)
            nc.gpsimd.memset(cv_h[0][:], 0.0).then_inc(zeroed, 1)
            nc.gpsimd.memset(cv_h[1][:], 0.0).then_inc(zeroed, 1)
            resid_pool(pool, 0)
            pool.wait_ge(zeroed, 3)
            for st in range(3):
                if st > 0:
                    resid_pool(pool, 2 * st)
                if st < 2:
                    att_stage(pool, "pool", st, pool_tile, pool_event)
                else:
                    pool_zeroes(pool)
                    conv_pool(pool)
                    pre_pool_f(pool)
                resid_pool(pool, 2 * st + 1)
                ffn_stage(pool, st, ffn_pool(st))


def weight_stream(w):
    def tile(m):
        return m.reshape(KT, P, P).transpose(1, 0, 2).reshape(P, CHUNK)

    chunks = []

    def qkv(m, nd, pairs, cols):
        for pr in range(pairs):
            for g in range(nd):
                for role in range(3):
                    c = cols(role, g, pr)
                    chunks.append(tile(m[:, c:c + P]))

    def outs(m):
        for n in range(KT):
            chunks.append(tile(m[:, n * P:(n + 1) * P]))

    def mlp(up, down):
        for j in range(FT + 2):
            if j < FT:
                chunks.append(tile(up[:, j * P:(j + 1) * P]))
                chunks.append(tile(up[:, D_FF + j * P:D_FF + (j + 1) * P]))
            if j >= 2:
                chunks.append(down[(j - 2) * P:(j - 1) * P, :])

    qkv(w["a_w_qkv"][0], NDIL, PAIRS_AB, lambda r, g, pr: (r * NDIL + g) * D + pr * P)
    outs(w["a_w_o"][0])
    mlp(w["ffn_w_up"][0], w["ffn_w_down"][0])
    qkv(w["b_w_qkv"][0], 1, PAIRS_AB, lambda r, g, pr: r * D + pr * P)
    outs(w["b_w_o"][0])
    mlp(w["ffn_w_up"][1], w["ffn_w_down"][1])
    w_in = w["w_in_2"][0]
    att = HEADS_C * HD
    forget = np.zeros((D, P), np.float32)
    forget[:, 0:HEADS_C] = w_in[:, 3 * att:3 * att + HEADS_C]
    conv = 3 * att + HEADS_C
    for t in range(2):
        for half in range(2):
            c = conv + half * 2 * P + t * P
            chunks.append(tile(w_in[:, c:c + P]))
    chunks.append(tile(forget))
    for t in range(2):
        c = conv + 4 * P + t * P
        chunks.append(tile(w_in[:, c:c + P]))
    qkv(w_in, 1, PAIRS_C, lambda r, g, pr: r * att + pr * P)
    outs(w["w_out_2"][0])
    mlp(w["w_up_2"][0], w["w_down_2"][0])
    return np.stack(chunks)


def parameters(w):
    par = np.zeros((P, N_PAR), np.float32)

    def cols(at, v):
        n = v.shape[0] // P
        par[:, at:at + n] = v.reshape(n, P).T

    norms = (w["attn_norm"][0], w["ffn_norm"][0], w["attn_norm"][1], w["ffn_norm"][1], w["norm1_g_2"][0], w["norm2_g_2"][0])
    for e, v in enumerate(norms):
        cols(PAR_NORM + KT * e, v)
    gains = []
    for g in range(NDIL):
        gains += [w["a_q_norm"][0, g], w["a_k_norm"][0, g]]
    gains += [w["b_q_norm"][0], w["b_k_norm"][0], w["q_norm_g_2"][0], w["k_norm_g_2"][0]]
    half = ROPE_DIM // 2
    for n, v in enumerate(gains):
        par[:, PAR_GAIN + n] = np.concatenate([v, v])
        if n < 2 * NDIL + 2:
            sw = np.concatenate([v[half:ROPE_DIM], v[0:half], v[ROPE_DIM:]])
            par[:, PAR_SWAP + n] = np.concatenate([sw, sw])
    convs = ((w["ffn_conv_w"][0], w["ffn_conv_b"][0]), (w["ffn_conv_w"][1], w["ffn_conv_b"][1]), (w["ffn_dw_w_2"][0], None))
    for f, (cw, cb) in enumerate(convs):
        for j in range(FT):
            for s in range(2):
                c = PAR_FFN + 8 * (f * FT + j) + 4 * s
                rows = slice(s * D_FF + j * P, s * D_FF + (j + 1) * P)
                for k in range(3):
                    par[:, c + k] = cw[k, rows]
                if cb is not None:
                    par[:, c + 3] = cb[rows]
    for t in range(2):
        par[:, PAR_DW + t * CONV_C:PAR_DW + (t + 1) * CONV_C] = w["conv_dw_w_2"][0][:, t * P:(t + 1) * P].T
    cols(PAR_DWB, w["conv_dw_b_2"][0])
    cols(PAR_LNG, w["conv_ln_g_2"][0])
    cols(PAR_LNB, w["conv_ln_b_2"][0])
    cols(PAR_PSC, w["pool_scale_2"][0])
    par[0:HEADS_C, PAR_BF] = w["b_f_2"][0]
    for g in range(4):
        par[HD * (g % 2):HD * (g % 2) + HD, PAR_POOLW + (g // 2) * HD:PAR_POOLW + (g // 2 + 1) * HD] = w["pool_w_2"][0, g]
    for t in range(2):
        par[:, PAR_PW + t * 2 * P:PAR_PW + (t + 1) * 2 * P] = w["conv_pw_w_2"][0][t * P:(t + 1) * P, :]
    return par


def kernel(**inputs):
    import concourse.bacc as bacc
    from concourse.bass_utils import run_bass_kernel_spmd

    w = {k: np.asarray(v) for k, v in inputs.items()}
    con = shape_constants()
    arrays = {
        "x_t": np.ascontiguousarray(w["x"][0].T).reshape(KT, P, TOK),
        "w_stream": weight_stream(w),
        "params": parameters(w),
        "consts": con,
    }
    nc = bacc.Bacc("TRN2", target_bir_lowering=False, num_devices=1)
    f32 = mybir.dt.float32
    args = [nc.dram_tensor(n, a.shape, f32, kind="ExternalInput").ap() for n, a in arrays.items()]
    out = nc.dram_tensor("y_t", (KT, P, TOK), f32, kind="ExternalOutput").ap()
    build(nc, *args, out)
    r = run_bass_kernel_spmd(nc, [arrays], core_ids=[0])
    return r.results[0]["y_t"].reshape(D, TOK).T.reshape(1, TOK, D)
```

```python
import itertools

import numpy as np

import concourse.bass as bass
from concourse import mybir
from concourse.alu_op_type import AluOpType as ALU

P = 128
D = 1024
TOK = 256
KT = D // P
HEADS_A = 16
HD = 64
NDIL = 3
DILATED_PAIRS = ((128, 1), (512, 4), (2048, 16))
ROPE_DIM = HD // 4
ROPE_THETA = 500000.0
PAIRS_AB = HEADS_A // 2
HEADS_C = 8
PAIRS_C = HEADS_C // 2
D_FF = 2816
FT = D_FF // P
CONV_C = 31
PADC = CONV_C - 1
POOL_PAD = 16
POOL_WINDOWS = (2, 4, 8, 16)
EPS = 1e-6
NEG = -1e30
RING = 6
AHEAD = 3
AHEAD_HI = AHEAD + 1
X_SQ_POOL = KT // 2
WARM_UP = 20
CHUNK = KT * P

A_QKV = 0
A_OUT = A_QKV + 3 * NDIL * PAIRS_AB
A_FFN = A_OUT + KT
B_QKV = A_FFN + 3 * FT
B_OUT = B_QKV + 3 * PAIRS_AB
B_FFN = B_OUT + KT
C_PRE = B_FFN + 3 * FT
N_PRE = 7
C_QKV = C_PRE + N_PRE
C_OUT = C_QKV + 3 * PAIRS_C
C_FFN = C_OUT + KT
N_CHUNKS = C_FFN + 3 * FT

PAR_NORM = 0
PAR_GAIN = PAR_NORM + 6 * KT
PAR_SWAP = PAR_GAIN + 2 * NDIL + 4
PAR_FFN = PAR_SWAP + 2 * NDIL + 2
PAR_DW = PAR_FFN + 3 * FT * 8
PAR_DWB = PAR_DW + 2 * CONV_C
PAR_LNG = PAR_DWB + 2
PAR_LNB = PAR_LNG + 2
PAR_PSC = PAR_LNB + 2
PAR_BF = PAR_PSC + 2
PAR_POOLW = PAR_BF + 1
PAR_PW = PAR_POOLW + 2 * HD
N_PAR = PAR_PW + 2 * 2 * P

CON_ID = 0
CON_ONES = CON_ID + P
CON_BLK = CON_ONES + P
CON_EPS = CON_BLK + P
CON_NEG = CON_EPS + 2
CON_COS = CON_NEG + HEADS_C
CON_SIN = CON_COS + TOK
CON_MASKA = CON_SIN + TOK
CON_MASK1 = CON_MASKA + 3 * NDIL * P
CON_INV = CON_MASK1 + 3 * P
N_CON = CON_INV + 2 * TOK


def shape_constants():
    con = np.zeros((P, N_CON), np.float32)
    pos = np.arange(TOK, dtype=np.float32)
    inv_freq = np.float32(ROPE_THETA) ** (-np.arange(0, ROPE_DIM, 2, dtype=np.float32) / np.float32(ROPE_DIM))
    ang = (pos[:, None] * inv_freq[None, :]).astype(np.float32)
    cos, sin = np.cos(ang).T, np.sin(ang).T
    half = ROPE_DIM // 2
    con[:, CON_COS:CON_COS + TOK] = 1.0
    for b in (0, HD):
        con[b:b + half, CON_COS:CON_COS + TOK] = cos
        con[b + half:b + ROPE_DIM, CON_COS:CON_COS + TOK] = cos
        con[b:b + half, CON_SIN:CON_SIN + TOK] = -sin
        con[b + half:b + ROPE_DIM, CON_SIN:CON_SIN + TOK] = sin

    def mask(window, dil, qt, keys):
        d = (qt * P + np.arange(P))[:, None] - np.arange(keys)[None, :]
        ok = (d >= 0) & (d <= window) & (d % dil == 0)
        return np.where(ok, 0.0, NEG)

    o = CON_MASKA
    for qt in range(2):
        for w, d in DILATED_PAIRS:
            con[:, o:o + (qt + 1) * P] = mask(w, d, qt, (qt + 1) * P)
            o += (qt + 1) * P
    o = CON_MASK1
    for qt in range(2):
        con[:, o:o + (qt + 1) * P] = mask(TOK, 1, qt, (qt + 1) * P)
        o += (qt + 1) * P
    con[:, CON_ID:CON_ID + P] = np.eye(P)
    con[:, CON_ONES:CON_ONES + P] = 1.0
    for b in (0, HD):
        con[b:b + HD, CON_BLK + b:CON_BLK + b + HD] = 1.0
    for g, w in enumerate(POOL_WINDOWS):
        b = HD * (g % 2)
        con[b:b + HD, CON_INV + (g // 2) * TOK:CON_INV + (g // 2 + 1) * TOK] = 1.0 / np.minimum(pos + 1, w)
    con[0:HEADS_C, CON_NEG:CON_NEG + HEADS_C] = -np.eye(HEADS_C)
    con[:, CON_EPS] = EPS
    con[:, CON_EPS + 1] = HD * EPS
    return con


def build(nc, x_d, stream_d, par_d, con_d, out_d):
    F32 = mybir.dt.float32
    F32R = mybir.dt.float32r
    BF16 = mybir.dt.bfloat16
    ACT = mybir.ActivationFunctionType
    ds = bass.ds

    def sb(name, shape, dt=F32):
        return nc.alloc_sbuf_tensor(name, shape, dt)

    def sem(name):
        return nc.alloc_semaphore(name)

    w_raw = [sb(f"w_raw{s}", [P, CHUNK]) for s in range(RING)]
    w_hi = [sb(f"w_hi{s}", [P, CHUNK], F32R) for s in range(RING)]
    w_lo = [sb(f"w_lo{s}", [P, CHUNK], F32R) for s in range(RING)]
    xT = sb("xT", [P, KT, TOK])
    xg = sb("xg", [P, KT, 2, TOK], F32R)
    xg_hi, xg_lo = xg[:, :, 0, :], xg[:, :, 1, :]
    mix_hi = sb("mix_hi", [P, KT, TOK], F32R)
    mix_lo = sb("mix_lo", [P, KT, TOK], F32R)
    par = sb("par", [P, N_PAR])
    con = sb("con", [P, N_CON])
    zero = sb("zero", [P, 512], BF16)
    ln_x = sb("ln_x", [P, TOK])
    rms_r = sb("rms_r", [P, TOK])
    rope_t = sb("rope_t", [P, 2 * NDIL, 2, TOK])
    rope_b = sb("rope_b", [P, 2, 2, TOK])
    qk_raw = [sb(f"qk_raw{r}", [P, TOK]) for r in range(2)]
    qk_sq = [sb(f"qk_sq{r}", [P, TOK], F32R) for r in range(2)]
    sq_all = sb("sq_all", [P, TOK])
    sq_lo = [sb(f"sq_lo{r}", [P, TOK], F32R) for r in range(2)]
    blk = sb("blk", [P, P], F32R)
    qk_swap = [sb(f"qk_swap{r}", [P, TOK]) for r in range(2)]
    qk_rope = [sb(f"qk_rope{r}", [P, TOK]) for r in range(2)]
    qk_r = [sb(f"qk_r{r}", [P, TOK]) for r in range(2)]
    rope_1 = sb("rope_1", [P, TOK])
    rope_2 = sb("rope_2", [P, TOK])
    v_t = sb("v_t", [P, TOK])
    sqx = [sq_all, v_t] + qk_swap + qk_rope + [rope_1, rope_2]
    qk_n = [[[sb(f"qk_n{b}{g}{r}", [P, TOK]) for r in range(2)] for g in range(NDIL)] for b in range(2)]
    v_n = [[sb(f"v_n{b}{g}", [P, 2, P]) for g in range(NDIL)] for b in range(2)]
    prob = [sb(f"prob{h}", [P, 3 * NDIL * P]) for h in range(2)]
    prob_t = [sb(f"prob_t{h}", [P, NDIL, 3 * P]) for h in range(2)]
    smax = [sb(f"smax{h}", [P, 2]) for h in range(2)]
    nmax = [sb(f"nmax{h}", [P, 2]) for h in range(2)]
    ssum = [sb(f"ssum{h}", [P, 2]) for h in range(2)]
    rsum = [sb(f"rsum{h}", [P, 2]) for h in range(2)]
    scratch = sb("scratch", [P, 64])
    scratch_col = itertools.count()
    up_s = [[qk_n[b][1][s] for s in range(2)] for b in range(2)]
    cv_s = [[qk_n[b][2][s] for s in range(2)] for b in range(2)]
    gate_s, gated = qk_raw
    up_sum = [prob[s][:, 0:TOK] for s in range(2)]
    g_hi = [sb(f"g_hi{b}", [P, TOK], F32R) for b in range(2)]
    g_lo = [sb(f"g_lo{b}", [P, TOK], F32R) for b in range(2)]
    fg = [rope_t[0:HEADS_C, 4 + n // 2, n % 2, :] for n in range(4)] + [rope_b[0:HEADS_C, 0, n, :] for n in range(2)]
    pick = [(qk_sq + sq_lo)[h // 2][0:HEADS_C, h % 2 * P:(h % 2 + 1) * P] for h in range(HEADS_C)]
    cum_hi, cum_lo = g_hi[0][0:HEADS_C, :], g_lo[0][0:HEADS_C, :]
    cv_a = [qk_n[0][1][i] for i in range(2)]
    cv_b = [qk_n[0][2][i] for i in range(2)]
    cv_e = [qk_n[1][1][i] for i in range(2)]
    cv_acc = [qk_n[1][2][i] for i in range(2)]
    cv_h = [sb(f"cv_h{i}", [P, PADC + TOK]) for i in range(2)]
    W_PL = POOL_PAD + TOK
    prob_t_flat = [prob_t[h][:].rearrange("p g c -> p (g c)") for h in range(2)]
    pl = [[prob[i][:, 3 * P:3 * P + W_PL], prob[i][:, 3 * P + W_PL:3 * P + 2 * W_PL],
           prob_t_flat[i][:, 3 * P:3 * P + W_PL]] for i in range(2)]

    ps = nc.alloc_psum_tensor("ps", [P, 8 * 512], F32)

    def bank(b, lo=0, n=TOK):
        return ps[:, b * 512 + lo:b * 512 + lo + n]

    SS = 3

    w_loaded = [sem(f"w_loaded{s}") for s in range(RING)]
    w_hi_done = sem("w_hi_done")
    w_lo_done = sem("w_lo_done")
    tiles = sem("tiles")
    x_in = [sem(f"x_in{h}") for h in range(2)]
    par_in = sem("par_in")
    con_in = sem("con_in")
    rope_in = sem("rope_in")
    rest_in = sem("rest_in")
    pl_zeroed = sem("pl_zeroed")
    zeroed = sem("zeroed")
    acc_done = sem("acc_done")
    x_new = sem("x_new")
    x_sq = sem("x_sq")
    x_sq_pool = sem("x_sq_pool")
    x_hi = sem("x_hi")
    x_lo = sem("x_lo")
    x_add = sem("x_add")
    x_ss = sem("x_ss")
    x_ln = sem("x_ln")
    x_r = sem("x_r")
    tables_first = sem("tables_first")
    tables = sem("tables")
    blk_in = sem("blk_in")
    stored = sem("stored")

    class Att:

        def __init__(self, n):
            self.raw = sem(f"{n}_raw")
            self.sq = sem(f"{n}_sq")
            self.sqall = sem(f"{n}_sqall")
            self.sqlo = sem(f"{n}_sqlo")
            self.swap = sem(f"{n}_swap")
            self.rot1 = sem(f"{n}_rot1")
            self.rot2 = sem(f"{n}_rot2")
            self.rope = sem(f"{n}_rope")
            self.aux = sem(f"{n}_aux")
            self.auxr = sem(f"{n}_auxr")
            self.r = sem(f"{n}_r")
            self.qn = sem(f"{n}_qn")
            self.score = sem(f"{n}_score")
            self.mx = sem(f"{n}_mx")
            self.masked = sem(f"{n}_masked")
            self.expd = sem(f"{n}_expd")
            self.rs = sem(f"{n}_rs")
            self.pn = sem(f"{n}_pn")
            self.pt = sem(f"{n}_pt")
            self.ptr = sem(f"{n}_ptr")
            self.pv = sem(f"{n}_pv")
            self.ohi = sem(f"{n}_ohi")
            self.olo = sem(f"{n}_olo")

    class Ffn:

        def __init__(self, n):
            self.sum = sem(f"{n}_sum")
            self.up = sem(f"{n}_up")
            self.tap0 = sem(f"{n}_tap0")
            self.tap1 = sem(f"{n}_tap1")
            self.conv = sem(f"{n}_conv")
            self.silu = sem(f"{n}_silu")
            self.gated = sem(f"{n}_gated")
            self.ghi = sem(f"{n}_ghi")
            self.glo = sem(f"{n}_glo")

    att = [Att("aA"), Att("aB"), Att("aC")]
    ffn = [Ffn("fA"), Ffn("fB"), Ffn("fC")]
    pre_out = sem("pre_out")
    pre_act = sem("pre_act")
    pre_dve = sem("pre_dve")
    pre_pool = sem("pre_pool")
    tap = sem("tap")
    tap_prod = sem("tap_prod")
    tap_pool = sem("tap_pool")
    pick_in = sem("pick_in")
    cum_hi_done = sem("cum_hi_done")
    cum_lo_done = sem("cum_lo_done")
    ln_pe = sem("ln_pe")
    ln_dve = sem("ln_dve")
    ln_act = sem("ln_act")
    side_lo = sem("side_lo")

    def at(base, per, i):
        return base if i is None else base + per * i

    def past(eng, s, base, per, i):
        if i is not None or base > 0:
            eng.wait_ge(s, at(base, per, i))

    def own_wait(i):
        if i is not None:
            n = next(scratch_col) % 64
            nc.vector.memset(scratch[:, n:n + 1], 0.0)

    def split_hi(eng, c, per, i):
        c = c + AHEAD_HI
        if i is None and c >= N_CHUNKS:
            return
        s = c % RING
        eng.wait_ge(w_loaded[s], at(16 * (c // RING + 1), 16 * per // RING, i))
        past(eng, tiles, c - RING + 1, per, i)
        nc.scalar.activation(w_hi[s][:], w_raw[s][:], ACT.Copy).then_inc(w_hi_done, 1)

    def split_lo(eng, c, per, i):
        c = c + AHEAD
        if i is None and c >= N_CHUNKS:
            return
        s = c % RING
        eng.wait_ge(w_hi_done, at(c + 1, per, i))
        nc.vector.tensor_tensor(w_lo[s][:], w_raw[s][:], w_hi[s][:].bitcast(F32),
                                ALU.subtract).then_inc(w_lo_done, 1)

    def project_k(eng, c, out, hi, lo, k):
        s = c % RING
        wh, wl = w_hi[s][:, k * P:(k + 1) * P], w_lo[s][:, k * P:(k + 1) * P]
        nc.tensor.matmul(out, wh, hi[:, k, :], start=(k == 0), stop=False)
        nc.tensor.matmul(out, wh, lo[:, k, :], start=False, stop=False)
        last = nc.tensor.matmul(out, wl, hi[:, k, :], start=False, stop=(k == KT - 1))
        if k == KT - 1:
            last.then_inc(tiles, 1)

    def project(eng, c, per, i, out, hi, lo):
        eng.wait_ge(w_lo_done, at(c + 1, per, i))
        for k in range(KT):
            project_k(eng, c, out, hi, lo, k)

    def project2_k(eng, c, b, k):
        s = c % RING
        nc.tensor.matmul(bank(b, 0, 2 * TOK), w_hi[s][:, k * P:(k + 1) * P], xg[:, k, :, :].rearrange("p h t -> p (h t)"),
                         start=(k == 0), stop=False, skip_group_check=True)
        last = nc.tensor.matmul(bank(b), w_lo[s][:, k * P:(k + 1) * P], xg_hi[:, k, :], start=False,
                                stop=(k == KT - 1), skip_group_check=True)
        if k == KT - 1:
            last.then_inc(tiles, 1)

    def project2(eng, c, per, i, b):
        eng.wait_ge(w_lo_done, at(c + 1, per, i))
        for k in range(KT):
            project2_k(eng, c, b, k)

    def project_first(eng, c, b0, b1, e, lag):
        for k in range(KT + lag):
            if k < KT:
                if k == 0:
                    eng.wait_ge(w_lo_done, c + 1)
                eng.wait_ge(x_lo, KT * e + k + 1)
                project2_k(eng, c, b0, k) if e % 2 else project_k(eng, c, bank(b0), xg_hi, xg_lo, k)
            if k >= lag:
                if k == lag:
                    eng.wait_ge(w_lo_done, c + 2)
                project2_k(eng, c + 1, b1, k - lag) if e % 2 else project_k(eng, c + 1, bank(b1), xg_hi, xg_lo, k - lag)
            if k == KT - 1 and e > 0:
                resid_pe(eng, e, 0)
            if k == KT + lag // 2 and e == 0:
                resid_pe(eng, e, 0)
                resid_pe(eng, e, 1)
        if e > 0:
            resid_pe(eng, e, 1)

    def resid_dve_add(eng, m, src, c):
        eng.wait_ge(tiles, c + 1)
        nc.vector.tensor_tensor(xT[:, m, :], src, xT[:, m, :], ALU.add).then_inc(x_new, 1)

    def resid_act(eng, e, m):
        if e == 0:
            eng.wait_ge(x_in[m // (KT // 2)], 16)
            eng.wait_ge(par_in, 16)
        else:
            eng.wait_ge(x_new, KT * (e - 1) + m + 1)
        g = PAR_NORM + KT * e + m
        nc.scalar.activation(xg_hi[:, m, :], xT[:, m, :], ACT.Copy, scale=par[:, g:g + 1]).then_inc(x_hi, 1)
        if e > 0:
            resid_act_sq(eng, m)

    def resid_act_sq(eng, m):
        nc.scalar.activation(sqx[m][:], xT[:, m, :], ACT.Square).then_inc(x_sq, 1)

    def resid_dve_lo(eng, e, m):
        eng.wait_ge(x_hi, KT * e + m + 1)
        if e == 0:
            eng.wait_ge(x_in[m // (KT // 2)], 16)
        g = PAR_NORM + KT * e + m
        nc.vector.scalar_tensor_tensor(xg_lo[:, m, :], xT[:, m, :], par[:, g:g + 1], xg_hi[:, m, :].bitcast(F32),
                                       ALU.mult, ALU.subtract).then_inc(x_lo, 1)

    def resid_pool(eng, e):
        if e == 0:
            eng.wait_ge(x_in[0], 16)
            for m in range(X_SQ_POOL):
                nc.gpsimd.tensor_tensor(sqx[m][:], xT[:, m, :], xT[:, m, :], ALU.mult).then_inc(x_sq_pool, 1)
        for n, (to, other) in enumerate(((0, 1), (2, 3), (0, 2), (4, 5), (6, 7), (4, 6))):
            if n % 3 < 2:
                if e == 0 and other < X_SQ_POOL:
                    eng.wait_ge(x_sq_pool, other + 1)
                else:
                    eng.wait_ge(x_sq, KT * e + other + 1 - X_SQ_POOL)
            else:
                eng.wait_ge(x_add, 6 * e + n)
            nc.gpsimd.tensor_tensor(sqx[to][:], sqx[to][:], sqx[other][:], ALU.add).then_inc(x_add, 1)

    def resid_pe(eng, e, h):
        eng.wait_ge(x_add, 6 * e + 3 * h + 3)
        if e == 0:
            eng.wait_ge(con_in, 16)
        nc.tensor.matmul(bank(SS), con[:, CON_ONES:CON_ONES + P], sqx[4 * h][:], start=(h == 0), stop=(h == 1)).then_inc(x_ss, 1)

    def resid_act_r(eng, e):
        eng.wait_ge(x_ss, 2 * (e + 1))
        eng.wait_ge(con_in, 16)
        nc.scalar.activation(ln_x[:], bank(SS), ACT.Ln, scale=1.0 / D, bias=con[:, CON_EPS:CON_EPS + 1]).then_inc(x_ln, 1)
        eng.wait_ge(x_ln, e + 1)
        nc.scalar.activation(rms_r[:], ln_x[:], ACT.Exp, scale=-0.5).then_inc(x_r, 1)

    EVENTS3 = dict(
        pe=(("S0", 2), ("T0", 5), ("S1", 6), ("T1", 9), ("PV", 10)),
        dve=(("S0", 3), ("N0", 5), ("S1", 7), ("N1", 9), ("X", 12)),
        act=(("S0", 4), ("E0", 6), ("S1", 8), ("E1", 10), ("X", 11)),
        pool=())
    EVENTS1 = dict(
        pe=(("S0", 2), ("S1", 2), ("T0", 5), ("T1", 5), ("PV", 6)),
        dve=(("S0", 3), ("S1", 3), ("N0", 5), ("N1", 5), ("X", 8)),
        act=(("S0", 4), ("S1", 4), ("E0", 6), ("E1", 6), ("X", 7)),
        pool=())
    EVENTS_C = dict(EVENTS1, dve=(("S0", 3), ("S1", 3), ("N0", 5), ("N1", 5), ("X", 7)))
    STAGES = [
        dict(c0=A_QKV, nd=NDIL, pairs=PAIRS_AB, events=EVENTS3, norm=0, rope=rope_t, gain=PAR_GAIN, mask=CON_MASKA),
        dict(c0=B_QKV, nd=1, pairs=PAIRS_AB, events=EVENTS1, norm=2, rope=rope_b, gain=PAR_GAIN + 2 * NDIL, mask=CON_MASK1),
        dict(c0=C_QKV, nd=1, pairs=PAIRS_C, events=EVENTS_C, norm=4, rope=None, gain=PAR_GAIN + 2 * NDIL + 2, mask=CON_MASK1),
    ]

    def att_stage(eng, who, st, tile, event, after=None):
        S = STAGES[st]
        T, pairs = 3 * S["nd"], S["pairs"]
        every = [o for evs in S["events"].values() for _, o in evs]
        reach = 1 + max(every) // T

        def window(w, per, i):
            for t in range(T):
                tile(eng, st, w * T + t, per * T, i)
                here = sorted((-(o // T), x) for x, (_, o) in enumerate(S["events"][who]) if o % T == t)
                for late, x in here:
                    pr = w - 1 + late
                    if 0 <= pr < pairs:
                        event(eng, st, S["events"][who][x][0], pr, per, i)
                if after is not None and w >= pairs:
                    after((w - pairs) * T + t)

        for w in range(reach):
            window(w, 0, None)
        turns = (pairs - reach) // 2
        if turns:
            with eng.Fori(0, turns) as i:
                for u in range(2):
                    window(reach + u, 2, i)
        for w in range(reach + 2 * turns, pairs + reach):
            window(w, 0, None)

    def kind(S, n):
        T = 3 * S["nd"]
        return n % 3, (n % T) // 3, (n // T) % 2, n - n // 3 if n % 3 < 2 else None

    def qk_no(n):
        return 2 * (n // 3) + n % 3

    def score_out(S, h, qt, g):
        if S["nd"] == 1:
            o = (3 + h) * 512 + (0, P)[qt]
        else:
            o = 3 * 512 + (g * P if qt == 0 else 512 + g * 2 * P)
        return ps[:, o:o + (qt + 1) * P]

    def score_all(S, h, qt):
        w = S["nd"] * P * (qt + 1)
        o = (3 + h) * 512 + (0, P)[qt] if S["nd"] == 1 else (3 + qt) * 512
        return ps[:, o:o + w]

    def prob_cols(S, qt):
        w = S["nd"] * P
        return (0, w) if qt == 0 else (w, 3 * w)

    def pt_bank(S, h, g):
        return 5 + h if S["nd"] == 1 else 3 + g

    def pv_out(S, b):
        return (7 * 512 + b * TOK) if S["nd"] == 1 else (6 + b) * 512

    def aux_out(m, lo=0, n=TOK):
        return bank((m + 1) % 3, TOK + lo, n)

    def pe_tile(eng, st, n, per, i):
        S, a = STAGES[st], att[st]
        N = 3 * S["nd"] * S["pairs"]
        if i is None and st < 2 and n < 2:
            if n == 0:
                project_first(eng, S["c0"], 0, 1, S["norm"], 1 if st else KT)
        elif i is not None or n < N:
            if st == 2 and n < 3:
                eng.wait_ge(pre_out, N_PRE - 2 + n)
            past(eng, a.raw, n - 2, per, i)
            past(eng, a.auxr, n - 3, per, i)
            project(eng, S["c0"] + n, per, i, bank(n % 3), xg_hi, xg_lo)
        m = n - 2
        if i is None and (m < 0 or m >= N):
            return
        role = m % 3
        if st == 0 and m == 0 and i is None:
            eng.wait_ge(blk_in, 1)
        eng.wait_ge(a.raw, at(m + 2 if i is not None else min(m + 2, N), per, i))
        if role < 2:
            eng.wait_ge(a.sq, at(qk_no(m) + 1, per * 2 // 3, i))
            if S["rope"] is None:
                nc.tensor.matmul(aux_out(m), con[:, CON_BLK:CON_BLK + P], qk_rope[role][:],
                                 start=True, stop=True).then_inc(a.aux, 1)
            else:
                eng.wait_ge(a.sqlo, at(qk_no(m) + 1, per * 2 // 3, i))
                nc.tensor.matmul(aux_out(m), blk[:], qk_sq[role][:], start=True, stop=False)
                nc.tensor.matmul(aux_out(m), blk[:], sq_lo[role][:], start=False, stop=True).then_inc(a.aux, 1)
        else:
            for tt in range(2):
                last = nc.tensor.transpose(aux_out(m, tt * P, P), v_t[:, tt * P:(tt + 1) * P],
                                           con[:, CON_ID:CON_ID + P])
            last.then_inc(a.aux, 1)

    def pe_event(eng, st, what, pr, per, i):
        S, a = STAGES[st], att[st]
        nd, T, b = S["nd"], 3 * S["nd"], pr % 2
        if what[0] == "S":
            h = int(what[1])
            lo, hi = HD * h, HD * h + HD
            eng.wait_ge(a.qn, at(2 * nd * (pr + 1), 2 * nd * per, i))
            if nd > 1 and h == 1:
                eng.wait_ge(a.ptr, at(2 * pr + 1, 2 * per, i))
            if st == 2:
                eng.wait_ge(pick_in, HEADS_C)
                eng.wait_ge(cum_lo_done, 1)
                if pr == PAIRS_C - 1 and h == 0:
                    eng.wait_ge(side_lo, 2)
            for qt in range(2):
                for g in range(nd):
                    q, k = qk_n[b][g]
                    out = score_out(S, h, qt, g)
                    last = nc.tensor.matmul(out, q[lo:hi, qt * P:(qt + 1) * P], k[lo:hi, 0:(qt + 1) * P],
                                            start=True, stop=(st < 2))
                    if st == 2:
                        for part in (cum_hi, cum_lo):
                            last = nc.tensor.matmul(out, pick[2 * pr + h], part[:, 0:(qt + 1) * P],
                                                    start=False, stop=(part is cum_lo))
            last.then_inc(a.score, 1)
        elif what[0] == "T":
            h = int(what[1])
            eng.wait_ge(a.pn, at(2 * pr + h + 1, 2 * per, i))
            w = nd * P
            for g in range(nd):
                bk = pt_bank(S, h, g)
                for n, o in enumerate((g * P, w + g * 2 * P, w + g * 2 * P + P)):
                    last = nc.tensor.transpose(bank(bk, n * P, P), prob[h][:, o:o + P], con[:, CON_ID:CON_ID + P])
            last.then_inc(a.pt, 1)
        elif what == "PV":
            eng.wait_ge(a.ptr, at(2 * pr + 2, 2 * per, i))
            eng.wait_ge(a.auxr, at(T * pr + T, T * per, i))
            if nd == 1:
                past(eng, a.olo, pr, per, i)
            for g in range(nd):
                for kt, q0 in ((0, 0), (1, P)):
                    for h in range(2):
                        lo, hi = HD * h, HD * h + HD
                        last = nc.tensor.matmul(ps[lo:hi, pv_out(S, b) + q0:pv_out(S, b) + TOK],
                                                v_n[b][g][:, kt, lo:hi],
                                                prob_t[h][:, g, 2 * P * kt:2 * P * kt + TOK - q0],
                                                start=(g == 0 and kt == 0), stop=(g == nd - 1 and kt == 1),
                                                skip_group_check=True)
            last.then_inc(a.pv, 1)

    def rope_tables(tab, g, gains):
        for k in range(2 * g, 2 * g + 2):
            for w, (src, col) in enumerate(((CON_COS, PAR_GAIN), (CON_SIN, PAR_SWAP))):
                c = col + gains + k
                nc.scalar.activation(tab[:, k, w, :], con[:, src:src + TOK], ACT.Copy,
                                     scale=par[:, c:c + 1]).then_inc(tables, 1)

    def rope_tables_dve(g):
        for k in range(2 * g, 2 * g + 2):
            for w, (src, col) in enumerate(((CON_COS, PAR_GAIN), (CON_SIN, PAR_SWAP))):
                nc.vector.tensor_scalar(rope_t[:, k, w, :], con[:, src:src + TOK], par[:, col + k:col + k + 1], None,
                                        ALU.mult).then_inc(tables_first, 1)

    TABLES_2, TABLES_B = 5, 8

    def act_square(eng, st, m, per, i):
        S, a = STAGES[st], att[st]
        eng.wait_ge(a.raw, at(m + 1, per, i))
        sq = (qk_rope if S["rope"] is None else qk_sq)[m % 3][:]
        nc.scalar.activation(sq, qk_raw[m % 3][:], ACT.Square).then_inc(a.sq, 1)

    def act_tile(eng, st, n, per, i):
        S, a = STAGES[st], att[st]
        N = 3 * S["nd"] * S["pairs"]
        first = i is None and n in (1, 2)
        if n == 1 and st == 1:
            resid_act_r(eng, S["norm"])
        if first:
            act_square(eng, st, n - 1, per, i)
        if i is not None or n < N + RING - AHEAD_HI:
            split_hi(eng, S["c0"] + n, per, i)
        if st == 2 and n in (1, 2):
            forget_pick(range(4 * n - 4, 4 * n))
            if n == 1:
                eng.wait_ge(pre_dve, 5)
                nc.scalar.activation(cum_hi, fg[2], ACT.Copy).then_inc(cum_hi_done, 1)
        if st == 0 and n == TABLES_2:
            rope_tables(rope_t, 2, 0)
        if st == 0 and n == TABLES_B:
            rope_tables(rope_b, 0, 2 * NDIL)
        m = n - 1
        if (i is not None or 0 <= m < N) and m % 3 < 2 and not first:
            act_square(eng, st, m, per, i)
        m = n - 3
        if i is None and (m < 0 or m >= N):
            return
        role, g, b, _ = kind(S, m)
        eng.wait_ge(a.aux, at(m + 1, per, i))
        if role < 2:
            e = CON_EPS + 1 - role
            nc.scalar.activation(qk_r[role][:], aux_out(m), ACT.Ln, scale=(1.0, 1.0 / HD)[role],
                                 bias=con[:, e:e + 1]).then_inc(a.auxr, 1)
            eng.wait_ge(a.auxr, at(m + 1, per, i))
            nc.scalar.activation(qk_r[role][:], qk_r[role][:], ACT.Exp, scale=-0.5).then_inc(a.r, 1)
        else:
            nc.scalar.activation(v_n[b][g][:], aux_out(m).rearrange("p (t c) -> p t c", t=2),
                                 ACT.Copy).then_inc(a.auxr, 1)

    def act_tile_c(eng, st, n, per, i):
        if st == 2:
            conv_prods(eng, n - 1)
        act_tile(eng, st, n, per, i)

    def act_event(eng, st, what, pr, per, i):
        S, a = STAGES[st], att[st]
        nd, b = S["nd"], pr % 2
        if what[0] == "S":
            h = int(what[1])
            eng.wait_ge(a.masked, at(2 * pr + h + 1, 2 * per, i))
            for qt in range(2):
                o0, o1 = prob_cols(S, qt)
                last = nc.scalar.activation(prob[h][:, o0:o1], prob[h][:, o0:o1], ACT.Exp, bias=nmax[h][:, qt:qt + 1],
                                            accum_out=ssum[h][:, qt:qt + 1])
            last.then_inc(a.expd, 1)
        elif what[0] == "E":
            h = int(what[1])
            eng.wait_ge(a.pt, at(2 * pr + h + 1, 2 * per, i))
            b0 = pt_bank(S, h, 0) * 512
            nc.scalar.activation(prob_t[h][:, 0:nd, :],
                                 ps[:, b0:b0 + nd * 512].rearrange("p (g c) -> p g c", c=512)[:, :, 0:3 * P],
                                 ACT.Copy).then_inc(a.ptr, 1)
        elif what == "X":
            eng.wait_ge(a.pv, at(pr + 1, per, i))
            nc.scalar.activation(mix_hi[:, ds(at(pr, per, i), 1), :], ps[:, pv_out(S, b):pv_out(S, b) + TOK].rearrange("p (o t) -> p o t", o=1),
                                 ACT.Copy).then_inc(a.ohi, 1)

    SWAP = [p + ROPE_DIM // 2 if p < ROPE_DIM // 2 else p - ROPE_DIM // 2 if p < ROPE_DIM else p for p in range(32)]

    def dve_tile(eng, st, n, per, i):
        S, a = STAGES[st], att[st]
        N = 3 * S["nd"] * S["pairs"]
        if st == 2 and n > 1:
            conv_taps(eng, n)
        first = i is None and n in (1, 2, 3)
        if (i is not None or n < N + RING - AHEAD) and not first:
            split_lo(eng, S["c0"] + n, per, i)
        m = n - 4
        if (i is not None or 0 <= m < N) and m % 3 < 2:
            role, g, b, _ = kind(S, m)
            eng.wait_ge(a.r, at(qk_no(m) + 1, per * 2 // 3, i))
            if S["rope"] is not None:
                eng.wait_ge(a.rope, at(qk_no(m) + 1, per * 2 // 3, i))
                nc.vector.tensor_tensor(qk_n[b][g][role][:], qk_rope[role][:], qk_r[role][:], ALU.mult).then_inc(a.qn, 1)
            else:
                c = S["gain"] + role
                nc.vector.scalar_tensor_tensor(qk_n[b][g][role][:], qk_raw[role][:], par[:, c:c + 1], qk_r[role][:],
                                               ALU.mult, ALU.mult).then_inc(a.qn, 1)
        m = n - 1
        if i is not None or 0 <= m < N:
            role = m % 3
            eng.wait_ge(tiles, at(S["c0"] + m + 1, per, i))
            if m == 0 and i is None:
                eng.wait_ge(x_r, S["norm"] + 1)
            if S["rope"] is None and role < 2 and m >= 3:
                eng.wait_ge(a.qn, at(qk_no(m - 3) + 1, per * 2 // 3, i))
            nc.vector.tensor_tensor((qk_raw + [v_t])[role][:], bank(m % 3), rms_r[:], ALU.mult).then_inc(a.raw, 1)
            if role < 2 and S["rope"] is not None:
                eng.wait_ge(a.raw, at(m + 1, per, i))
                own_wait(i)
                nc.vector.stream_shuffle(qk_swap[role][:], qk_raw[role][:], SWAP).then_inc(a.swap, 1)
        if st == 0 and first and n == 2:
            rope_tables_dve(1)
        if first:
            for c in ((), (1,), (2, 3))[n - 1]:
                split_lo(eng, S["c0"] + c, per, i)

    def dve_event(eng, st, what, pr, per, i):
        S, a = STAGES[st], att[st]
        b = pr % 2
        if what[0] == "S":
            h = int(what[1])
            eng.wait_ge(a.score, at(2 * pr + h + 1, 2 * per, i))
            own_wait(i)
            mo = S["mask"]
            if st == 0 and i is None and pr == 0:
                eng.wait_ge(rest_in, 32)
            for qt in range(2):
                o0, o1 = prob_cols(S, qt)
                last = nc.vector.tensor_tensor_reduce(prob[h][:, o0:o1], score_all(S, h, qt), con[:, mo + o0:mo + o1],
                                                      1.0, NEG, ALU.add, ALU.max, smax[h][:, qt:qt + 1])
            last.then_inc(a.mx, 1)
            eng.wait_ge(a.mx, at(2 * pr + h + 1, 2 * per, i))
            nc.vector.tensor_scalar(nmax[h][:], smax[h][:], -1.0, None, ALU.mult).then_inc(a.masked, 1)
        elif what[0] == "N":
            h = int(what[1])
            eng.wait_ge(a.expd, at(2 * pr + h + 1, 2 * per, i))
            nc.vector.reciprocal(rsum[h][:], ssum[h][:]).then_inc(a.rs, 1)
            eng.wait_ge(a.rs, at(2 * pr + h + 1, 2 * per, i))
            for qt in range(2):
                o0, o1 = prob_cols(S, qt)
                last = nc.vector.tensor_scalar(prob[h][:, o0:o1], prob[h][:, o0:o1], rsum[h][:, qt:qt + 1], None, ALU.mult)
            last.then_inc(a.pn, 1)
        elif what == "X":
            eng.wait_ge(a.ohi, at(pr + 1, per, i))
            nc.vector.tensor_tensor(mix_lo[:, ds(at(pr, per, i), 1), :], ps[:, pv_out(S, b):pv_out(S, b) + TOK].rearrange("p (o t) -> p o t", o=1),
                                    mix_hi[:, ds(at(pr, per, i), 1), :].bitcast(F32), ALU.subtract).then_inc(a.olo, 1)

    def pool_squares(eng, st, m, per, i):
        a, role, k, kp = att[st], m % 3, qk_no(m) + 1, per * 2 // 3
        eng.wait_ge(a.raw, at(m + 1, per, i))
        nc.gpsimd.tensor_tensor(sq_all[:], qk_raw[role][:], qk_raw[role][:], ALU.mult).then_inc(a.sqall, 1)
        eng.wait_ge(a.sq, at(k, kp, i))
        eng.wait_ge(a.sqall, at(k, kp, i))
        nc.gpsimd.tensor_tensor(sq_lo[role][:], sq_all[:], qk_sq[role][:].bitcast(F32), ALU.subtract).then_inc(a.sqlo, 1)

    def pool_rotate(eng, st, m, per, i):
        S, a = STAGES[st], att[st]
        role, g, _, _ = kind(S, m)
        k, kp, tab = qk_no(m) + 1, per * 2 // 3, S["rope"]
        if i is None and st == 0 and g < 2:
            eng.wait_ge(tables_first, 4 * (g + 1))
        elif i is None:
            eng.wait_ge(tables, 4 * (st + 1))
        nc.gpsimd.tensor_tensor(rope_1[:], qk_raw[role][:], tab[:, 2 * g + role, 0, :], ALU.mult).then_inc(a.rot1, 1)
        eng.wait_ge(a.swap, at(k, kp, i))
        nc.gpsimd.tensor_tensor(rope_2[:], qk_swap[role][:], tab[:, 2 * g + role, 1, :], ALU.mult).then_inc(a.rot2, 1)
        eng.wait_ge(a.rot1, at(k, kp, i))
        eng.wait_ge(a.rot2, at(k, kp, i))
        nc.gpsimd.tensor_tensor(qk_rope[role][:], rope_1[:], rope_2[:], ALU.add).then_inc(a.rope, 1)
        eng.wait_ge(a.rope, at(k, kp, i))

    def pool_tile(eng, st, n, per, i):
        S, a = STAGES[st], att[st]
        N = 3 * S["nd"] * S["pairs"]
        m = n - 1
        if (i is None and not 0 <= m < N) or m % 3 == 2:
            return
        if i is not None or m != 1:
            pool_squares(eng, st, m, per, i)
        if i is None and m == 0:
            eng.wait_ge(a.sqlo, 1)
            pool_squares(eng, st, 1, per, i)
        pool_rotate(eng, st, m, per, i)
        eng.wait_ge(a.sqlo, at(qk_no(m) + 1 if i is not None or m > 1 else 2, per * 2 // 3, i))

    def pool_event(eng, st, what, pr, per, i):
        return

    NEXT = RING

    def out_bank(m):
        return bank((m + 1) % 3, m // 3 * TOK) if m < NEXT else bank(SS + 1 + m - NEXT)

    OUT_C0 = (A_OUT, B_OUT, C_OUT)
    FIVE, FOUR = range(5), (0, 3, 1, 4)
    OUT_EARLY = (
        {0: [(0, range(6))], 2: [(1, range(6)), (2, range(6))], 5: [(3, range(6))],
         6: [(4, range(6))] + [(m, (6,)) for m in FIVE] + [(5, range(2))], 9: [(5, range(2, 5))], 10: [(5, (5, 6))]},
        {0: [(0, range(5)), (3, range(5))], 1: [(1, range(5))], 2: [(2, range(5)), (4, range(5))],
         3: [(m, (5,)) for m in FIVE], 5: [(m, (6,)) for m in FIVE], 6: [(5, range(4))]},
        {0: [(0, (0,)), (3, (0,))], 1: [(1, (0,)), (4, (0,))] + [(m, (1,)) for m in FOUR],
         3: [(m, (6, 7)) for m in FOUR], 4: [(m, (2,)) for m in FOUR], 6: [(m, (4, 5)) for m in FOUR]},
    )

    def out_part(eng, st, m, ks, last):
        c = OUT_C0[st] + m
        s = c % RING
        eng.wait_ge(w_lo_done, c + 1)
        pairs = [k for k in ks if k < STAGES[st]["pairs"]]
        if pairs:
            eng.wait_ge(att[st].olo, max(pairs) + 1)
        if len(pairs) < len(ks):
            eng.wait_ge(side_lo, 4 if 4 in ks or 5 in ks else 2)
        for k in ks:
            wh, wl = w_hi[s][:, k * P:(k + 1) * P], w_lo[s][:, k * P:(k + 1) * P]
            end = last and k == ks[-1]
            nc.tensor.matmul(out_bank(m), wh, mix_hi[:, k, :], start=False, stop=False, skip_group_check=True)
            nc.tensor.matmul(out_bank(m), wh, mix_lo[:, k, :], start=False, stop=False, skip_group_check=True)
            mm = nc.tensor.matmul(out_bank(m), wl, mix_hi[:, k, :], start=False, stop=end, skip_group_check=True)
        if last:
            mm.then_inc(tiles, 1)

    def out_early(eng, st):
        def after(k):
            if k < (3 if st < 2 else 2):
                eng.wait_ge(att[st].auxr, 3 * STAGES[st]["nd"] * STAGES[st]["pairs"] + k - 2)
                out_zero(eng, ((k + 1) % 3,))
            for part in OUT_EARLY[st].get(k, ()):
                out_part(eng, st, *part, False)
        return after

    def out_zero(eng, banks):
        eng.wait_ge(zeroed, 1)
        for bk in banks:
            nc.tensor.matmul(bank(bk, 0, 512), zero[:, 0:P], zero[:, 0:512], start=True, stop=True, skip_group_check=True)

    def out_pe(eng, st):
        done = [k for parts in OUT_EARLY[st].values() for m, ks in parts for k in [(m, k) for k in ks]]
        if st == 2:
            eng.wait_ge(side_lo, 4)
            out_zero(eng, (0,))
        out_zero(eng, (SS + 1, SS + 2))
        for m in range(KT):
            out_part(eng, st, m, [k for k in range(KT) if (m, k) not in done], True)

    def out_act(eng, c0, e):
        def split(n):
            split_hi(eng, c0 + RING - AHEAD_HI + n, 0, None)

        split(0)
        for m in range(KT):
            if m in (0, 2, 4):
                split(1 + m // 2)
            resid_act(eng, e, m)
        for n in range(4, KT + AHEAD_HI - RING):
            split(n)

    def out_dve(eng, c0, e):
        def add(m):
            resid_dve_add(eng, m, out_bank(m), c0 + (m + 3 if m < 3 else m))

        def split(n):
            split_lo(eng, c0 + RING - AHEAD + n, 0, None)

        for n in range(3):
            split(n)
            for m in ((0, 1, 2), (3, 4, 5), (6,))[n]:
                add(m)
        for m in range(KT):
            if m == 4:
                add(7)
                split(3)
            resid_dve_lo(eng, e, m)
        for n in range(4, KT + AHEAD - RING):
            split(n)

    FFN_C0 = (A_FFN, B_FFN, C_FFN)

    def acc(m):
        return bank(4 + m // 2, (m % 2) * TOK)

    def ffn_chunk(f, j):
        return FFN_C0[f] + (2 * j if j < 2 else 4 + 3 * (j - 2) if j < FT else 3 * FT - 2 + j - FT)

    def ffn_stage(eng, f, step):
        first = 4
        turns = (FT - first) // 2 - (f == 2)
        for j in range(first):
            step(eng, j, 0, None)
        with eng.Fori(0, turns) as i:
            for u in range(2):
                step(eng, first + u, 2, i)
        for j in range(first + 2 * turns, FT + 2):
            step(eng, j, 0, None)

    def ffn_pe(f):
        e = 2 * f + 1

        def step(eng, j, per, i):
            F, b, c, cp = ffn[f], j % 2, ffn_chunk(f, j), 3 * per
            if i is not None or j < FT:
                if i is None and j == 0:
                    eng.wait_ge(x_new, KT * (e - 1) + NEXT)
                past(eng, F.sum, 2 * (j - 1), 2 * per, i)
                if i is None and j == 0:
                    project_first(eng, c, 0, 2, e, 3)
                else:
                    project2(eng, c, cp, i, b)
                    if i is None and j == 1:
                        eng.wait_ge(x_r, e + 1)
                    project2(eng, c + 1, cp, i, 2 + b)
                c += 2
            if i is None and j == 1:
                eng.wait_ge(x_new, KT * e)
                out_zero(eng, range(4, 8))
            if i is not None or j >= 2:
                s = c % RING
                eng.wait_ge(w_lo_done, at(c + 1, cp, i))
                eng.wait_ge(F.glo, at(j - 1, per, i))
                for m in range(KT):
                    wh, wl = w_hi[s][:, m * P:(m + 1) * P], w_lo[s][:, m * P:(m + 1) * P]
                    nc.tensor.matmul(acc(m), wh, g_hi[b][:], start=False, stop=False, skip_group_check=True)
                    nc.tensor.matmul(acc(m), wh, g_lo[b][:], start=False, stop=False, skip_group_check=True)
                    last = nc.tensor.matmul(acc(m), wl, g_hi[b][:], start=False, stop=True, skip_group_check=True)
                    if m == KT - 1:
                        last.then_inc(tiles, 1)
                    elif i is None and j == FT + 1:
                        last.then_inc(acc_done, 1)
        return step

    def par_col(f, j, per, i, k):
        return par[:, ds(at(PAR_FFN + 8 * (f * FT + j) + k, 8 * per, i), 1)]

    def ffn_act(f):
        def step(eng, j, per, i):
            F, c, cp = ffn[f], ffn_chunk(f, j), 3 * per
            n = 3 if 2 <= j < FT else 2 if j < 2 else 1
            split_hi(eng, c, cp, i)
            if j == 1:
                resid_act_r(eng, 2 * f + 1)
                nc.scalar.preload_act_table_set("silu_and_others")
                eng.wait_ge(rest_in, 32)
            t = j - 2
            if i is not None or 0 <= t < FT:
                if i is not None or t >= 2:
                    eng.wait_ge(tiles, at(ffn_chunk(f, t) + 3, cp, i))
                eng.wait_ge(F.gated, at(t + 1, per, i))
                nc.scalar.activation(g_hi[t % 2][:], gated[:], ACT.Copy).then_inc(F.ghi, 1)
            t = j - 1
            work = i is not None or 0 <= t < FT
            if work:
                for s in range(2):
                    eng.wait_ge(F.up, at(2 * t + 1 + s, 2 * per, i))
                    nc.scalar.activation(cv_s[t % 2][s][:], up_s[t % 2][s][:], ACT.Identity,
                                         scale=par_col(f, t, per, i, 4 * s + 2),
                                         bias=par_col(f, t, per, i, 4 * s + 3)).then_inc(F.tap0, 1)
            for q in range(1, n):
                split_hi(eng, c + q, cp, i)
            if work:
                eng.wait_ge(F.conv, at(2 * t + 1, 2 * per, i))
                nc.scalar.activation(gate_s[:], cv_s[t % 2][0][:], ACT.Silu).then_inc(F.silu, 1)
        return step

    def ffn_dve(f):
        def step(eng, j, per, i):
            F, c, cp = ffn[f], ffn_chunk(f, j), 3 * per
            n = 3 if 2 <= j < FT else 2 if j < 2 else 1
            t = j - 1
            b = t % 2
            work = i is not None or 0 <= t < FT

            def add(s):
                eng.wait_ge(tiles, at(ffn_chunk(f, t) + 1 + s, cp, i))
                past(eng, F.up, 2 * t + s - 1, 2 * per, i)
                nc.vector.tensor_reduce(up_sum[s], bank(2 * s + b, 0, 2 * TOK).rearrange("p (h t) -> p t h", h=2),
                                        mybir.AxisListType.X, ALU.add).then_inc(F.sum, 1)

            last = i is None and j == FT
            if last:
                add(0)
            split_lo(eng, c, cp, i)
            if work:
                if not last:
                    add(0)
                add(1)
            if n > 1:
                split_lo(eng, c + 1, cp, i)
            if i is not None or j >= 2:
                eng.wait_ge(F.ghi, at(j - 1, per, i))
                nc.vector.tensor_tensor(g_lo[j % 2][:], gated[:], g_hi[j % 2][:].bitcast(F32),
                                        ALU.subtract).then_inc(F.glo, 1)
            if work:
                for k in range(1, 3):
                    for s in range(2):
                        if k == 1:
                            eng.wait_ge(F.tap0, at(2 * t + 1 + s, 2 * per, i))
                        else:
                            eng.wait_ge(F.tap1, at(2 * t + 1 + s, 2 * per, i))
                        nc.vector.scalar_tensor_tensor(cv_s[b][s][:, k:TOK], up_s[b][s][:, 0:TOK - k],
                                                       par_col(f, t, per, i, 4 * s + 2 - k), cv_s[b][s][:, k:TOK],
                                                       ALU.mult, ALU.add).then_inc(F.tap1 if k == 1 else F.conv, 1)
            if n > 2:
                split_lo(eng, c + 2, cp, i)
        return step

    def ffn_pool(f):
        def step(eng, j, per, i):
            F, t = ffn[f], j - 1
            if i is None and not 0 <= t < FT:
                return
            if i is None and t == 0:
                eng.wait_ge(x_r, 2 * f + 2)
            for s in range(2):
                eng.wait_ge(F.sum, at(2 * t + 1 + s, 2 * per, i))
                nc.gpsimd.tensor_tensor(up_s[t % 2][s][:], up_sum[s], rms_r[:], ALU.mult).then_inc(F.up, 1)
            eng.wait_ge(F.silu, at(t + 1, per, i))
            eng.wait_ge(F.conv, at(2 * t + 2, 2 * per, i))
            past(eng, F.glo, t, per, i)
            nc.gpsimd.tensor_tensor(gated[:], gate_s[:], cv_s[t % 2][1][:], ALU.mult).then_inc(F.gated, 1)
        return step

    def ffn_end_act(eng, e):
        for m in range(KT):
            resid_act(eng, e, m)

    def ffn_end_dve(eng, f):
        for m in range(KT):
            if m < KT - 2:
                eng.wait_ge(acc_done, f * (KT - 1) + (m | 1) + 1)
            else:
                eng.wait_ge(tiles, FFN_C0[f] + 3 * FT)
            nc.vector.tensor_tensor(xT[:, m, :], acc(m), xT[:, m, :], ALU.add).then_inc(x_new, 1)
            if m >= 1 and f < 2:
                resid_dve_lo(eng, 2 * f + 2, m - 1)
        if f < 2:
            resid_dve_lo(eng, 2 * f + 2, KT - 1)

    FORGET = 4
    PRE_OUT = [cv_a[0][:], cv_b[0][:], cv_a[1][:], cv_b[1][:], fg[0],
               pl[0][0][:, POOL_PAD:POOL_PAD + TOK], pl[1][0][:, POOL_PAD:POOL_PAD + TOK]]

    def pre_bank(n):
        return (n + 2) % 3

    def pre_pe(eng):
        project_first(eng, C_PRE, pre_bank(0), pre_bank(1), 4, 1)
        for n in range(2, N_PRE):
            past(eng, pre_out, n - 2, 0, None)
            project(eng, C_PRE + n, 0, None, bank(pre_bank(n)), xg_hi, xg_lo)

    def pre_act_f(eng):
        for n in range(N_PRE):
            split_hi(eng, C_PRE + n, 0, None)
            if n == 1:
                resid_act_r(eng, 4)
            if n in (3, 5):
                t = n // 2 - 1
                eng.wait_ge(pre_out, 2 * t + 2)
                if t == 0:
                    nc.scalar.preload_act_table_set("sigmoid_and_others")
                nc.scalar.activation(cv_e[t][:], cv_b[t][:], ACT.Sigmoid).then_inc(pre_act, 1)
        nc.scalar.preload_act_table_set("natural_log_exp_and_others")
        eng.wait_ge(pre_out, FORGET + 1)
        nc.scalar.activation(fg[1], fg[0], ACT.Identity, bias=par[0:HEADS_C, PAR_BF:PAR_BF + 1]).then_inc(pre_act, 1)
        eng.wait_ge(pre_dve, 2)
        nc.scalar.activation(fg[3], fg[2], ACT.Exp, scale=-1.0).then_inc(pre_act, 1)
        eng.wait_ge(pre_act, 4)
        nc.scalar.activation(fg[4], fg[3], ACT.Ln, bias=1.0).then_inc(pre_act, 1)

    def pre_dve_f(eng):
        def glu(t):
            eng.wait_ge(pre_act, 1 + t)
            eng.wait_ge(zeroed, 3)
            nc.vector.tensor_tensor(cv_h[t][:, PADC:PADC + TOK], cv_a[t][:], cv_e[t][:], ALU.mult).then_inc(pre_dve, 1)

        def out(n):
            if n == 0:
                eng.wait_ge(x_r, 5)
            if n == 5:
                eng.wait_ge(pl_zeroed, 6)
            eng.wait_ge(tiles, C_PRE + n + 1)
            src = bank(pre_bank(n))[0:HEADS_C, :] if n == FORGET else bank(pre_bank(n))
            r = rms_r[0:HEADS_C, :] if n == FORGET else rms_r[:]
            nc.vector.tensor_tensor(PRE_OUT[n], src, r, ALU.mult).then_inc(pre_out, 1)

        for n in range(N_PRE):
            split_lo(eng, C_PRE + n, 0, None)
            if n >= 1:
                out(n - 1)
            if n == 4:
                glu(0)
            if n >= 5:
                conv_taps(eng, n - 5)
        out(N_PRE - 1)
        eng.wait_ge(pre_act, 3)
        nc.vector.scalar_tensor_tensor(fg[2], fg[1], -1.0, fg[1], ALU.mult, ALU.max).then_inc(pre_dve, 1)
        glu(1)
        eng.wait_ge(pre_act, 5)
        nc.vector.scalar_tensor_tensor(fg[5], fg[1], 0.0, fg[4], ALU.min, ALU.subtract).then_inc(pre_dve, 1)
        eng.wait_ge(pre_dve, 4)
        nc.vector.tensor_tensor_scan(fg[2], con[0:HEADS_C, CON_ONES:CON_ONES + 1].to_broadcast([HEADS_C, TOK]),
                                     fg[5], 0.0, ALU.mult, ALU.add).then_inc(pre_dve, 1)

    def forget_pick(heads):
        for h in heads:
            nc.scalar.activation(pick[h], con[0:HEADS_C, CON_ONES:CON_ONES + P], ACT.Copy,
                                 scale=con[0:HEADS_C, CON_NEG + h:CON_NEG + h + 1]).then_inc(pick_in, 1)

    def pool_zeroes(eng):
        for t in range(2):
            for b in pl[t]:
                nc.gpsimd.memset(b, 0.0).then_inc(pl_zeroed, 1)

    def pre_pool_f(eng):
        n = 0
        for t in range(2):
            eng.wait_ge(pre_out, 6 + t)
            src, k = 0, 1
            steps = ((1, 0, P), (2, HD, P)) if t == 0 else ((1, 0, P), (2, 0, P), (4, 0, P), (8, HD, P))
            for s, p0, p1 in steps:
                dst = 1 if src != 1 else 2
                if p0:
                    nc.gpsimd.tensor_copy(pl[t][dst][0:HD, POOL_PAD:], pl[t][src][0:HD, POOL_PAD:]).then_inc(pre_pool, 1)
                    n += 1
                nc.gpsimd.tensor_tensor(pl[t][dst][p0:p1, s:], pl[t][src][p0:p1, s:],
                                        pl[t][src][p0:p1, 0:POOL_PAD + TOK - s], ALU.add).then_inc(pre_pool, 1)
                n += 1
                eng.wait_ge(pre_pool, n)
                src = dst
            inv = con[:, CON_INV + t * TOK:CON_INV + (t + 1) * TOK]
            s0 = pl[t][src][:, POOL_PAD:]
            nc.gpsimd.tensor_tensor(s0, s0, inv, ALU.mult).then_inc(pre_pool, 1)
            n += 1
            eng.wait_ge(pre_pool, n)
            nc.gpsimd.tensor_tensor(pl[t][3 - src][:, POOL_PAD:], s0, pl[t][0][:, POOL_PAD:], ALU.subtract).then_inc(pre_pool, 1)
            n += 1
            eng.wait_ge(pre_pool, n)
        return n

    POOL_D = [pl[0][1], pl[1][1]]
    N_POOL_STEPS = 3 + 2 + 5 + 2

    TAPS_PER = 3
    PRODS_PER, PRODS_FROM = 4, 3
    prods = qk_swap + [sq_all, rope_2]

    def conv_w(t, j):
        return par[:, PAR_DW + t * CONV_C + j:PAR_DW + t * CONV_C + j + 1]

    def conv_taps(eng, n):
        for j in range(TAPS_PER * n, min(TAPS_PER * (n + 1), CONV_C)):
            src = cv_h[0][:, j:j + TOK]
            if j == 0:
                eng.wait_ge(pre_dve, 1)
                nc.vector.tensor_scalar(cv_acc[0][:], src, conv_w(0, j), par[:, PAR_DWB:PAR_DWB + 1],
                                        ALU.mult, ALU.add).then_inc(tap, 1)
            else:
                eng.wait_ge(tap, j)
                nc.vector.scalar_tensor_tensor(cv_acc[0][:], src, conv_w(0, j), cv_acc[0][:],
                                               ALU.mult, ALU.add).then_inc(tap, 1)

    def conv_prods(eng, n):
        n = n - PRODS_FROM
        for j in range(max(PRODS_PER * n, 0), min(PRODS_PER * (n + 1), CONV_C)):
            src = cv_h[1][:, j:j + TOK]
            if j == 0:
                eng.wait_ge(pre_dve, 3)
                nc.scalar.activation(cv_acc[1][:], src, ACT.Identity, scale=conv_w(1, j),
                                     bias=par[:, PAR_DWB + 1:PAR_DWB + 2]).then_inc(tap_prod, 1)
            else:
                past(eng, tap_pool, j - len(prods), 0, None)
                nc.scalar.activation(prods[j % len(prods)][:], src, ACT.Copy, scale=conv_w(1, j)).then_inc(tap_prod, 1)

    def conv_pool(eng):
        for j in range(1, CONV_C):
            eng.wait_ge(tap_prod, j + 1)
            past(eng, tap_pool, j - 1, 0, None)
            nc.gpsimd.tensor_tensor(cv_acc[1][:], cv_acc[1][:], prods[j % len(prods)][:], ALU.add).then_inc(tap_pool, 1)

    def side_pe(eng):
        ones = con[:, CON_ONES:CON_ONES + P]

        early = out_early(eng, 2)

        def after(k):
            early(k)
            if k == 0:
                eng.wait_ge(att[2].masked, HEADS_C - 2)
                eng.wait_ge(pre_pool, N_POOL_STEPS)
                for t in range(2):
                    for g in range(2):
                        p0, p1 = HD * g, HD * g + HD
                        last = nc.tensor.matmul(bank(3, t * TOK)[p0:p1, :],
                                                par[p0:p1, PAR_POOLW + t * HD:PAR_POOLW + (t + 1) * HD],
                                                POOL_D[t][p0:p1, POOL_PAD:], start=True, stop=True)
                last.then_inc(ln_pe, 1)
            elif k == 1:
                eng.wait_ge(att[2].auxr, 3 * PAIRS_C)
                eng.wait_ge(tap, CONV_C)
                eng.wait_ge(tap_pool, CONV_C - 1)
                for t in range(2):
                    last = nc.tensor.matmul(bank(0), ones, cv_acc[t][:], start=(t == 0), stop=(t == 1))
                last.then_inc(ln_pe, 1)
            elif k == 2:
                eng.wait_ge(ln_act, 4)
                for t in range(2):
                    last = nc.tensor.matmul(bank(0, TOK), ones, cv_e[t][:], start=(t == 0), stop=(t == 1))
                last.then_inc(ln_pe, 1)
            elif k == 5:
                eng.wait_ge(att[2].masked, HEADS_C)
                eng.wait_ge(ln_act, 8)
                for o in range(2):
                    for t in range(2):
                        w = PAR_PW + t * 2 * P + o * P
                        last = nc.tensor.matmul(bank(4 * o), par[:, w:w + P], cv_a[t][:], start=(t == 0), stop=(t == 1))
                last.then_inc(ln_pe, 1)
        return after

    def side_act(eng):
        def after(k):
            if k == 2:
                eng.wait_ge(ln_pe, 1)
                for t in range(2):
                    nc.scalar.activation(mix_hi[:, 6 + t, :], bank(3, t * TOK), ACT.Copy,
                                         scale=par[:, PAR_PSC + t:PAR_PSC + t + 1]).then_inc(ln_act, 1)
                for t in range(2):
                    eng.wait_ge(ln_dve, t + 1)
                    nc.scalar.activation(cv_e[t][:], cv_b[t][:], ACT.Square).then_inc(ln_act, 1)
            elif k == 3:
                eng.wait_ge(ln_pe, 3)
                nc.scalar.activation(ln_x[:], bank(0, TOK), ACT.Ln, scale=1.0 / (2 * P),
                                     bias=con[:, CON_EPS:CON_EPS + 1]).then_inc(ln_act, 1)
                eng.wait_ge(ln_act, 5)
                nc.scalar.activation(ln_x[:], ln_x[:], ACT.Exp, scale=-0.5).then_inc(ln_act, 1)
            elif k == 4:
                nc.scalar.preload_act_table_set("silu_and_others")
                for t in range(2):
                    eng.wait_ge(ln_dve, 3 + t)
                    nc.scalar.activation(cv_a[t][:], cv_b[t][:], ACT.Silu, scale=par[:, PAR_LNG + t:PAR_LNG + t + 1],
                                         bias=par[:, PAR_LNB + t:PAR_LNB + t + 1]).then_inc(ln_act, 1)
                nc.scalar.preload_act_table_set("natural_log_exp_and_others")
            elif k == 6:
                eng.wait_ge(ln_pe, 4)
                for o in range(2):
                    nc.scalar.activation(mix_hi[:, 4 + o, :], bank(4 * o), ACT.Copy).then_inc(ln_act, 1)
        return after

    def side_dve(eng):
        def after(k):
            if k == 2:
                eng.wait_ge(ln_act, 2)
                for t in range(2):
                    nc.vector.scalar_tensor_tensor(mix_lo[:, 6 + t, :], bank(3, t * TOK), par[:, PAR_PSC + t:PAR_PSC + t + 1],
                                                   mix_hi[:, 6 + t, :].bitcast(F32), ALU.mult, ALU.subtract).then_inc(side_lo, 1)
                eng.wait_ge(ln_pe, 2)
                for t in range(2):
                    nc.vector.scalar_tensor_tensor(cv_b[t][:], bank(0), -1.0 / (2 * P), cv_acc[t][:],
                                                   ALU.mult, ALU.add).then_inc(ln_dve, 1)
            elif k == 3:
                eng.wait_ge(ln_act, 6)
                for t in range(2):
                    nc.vector.tensor_tensor(cv_b[t][:], cv_b[t][:], ln_x[:], ALU.mult).then_inc(ln_dve, 1)
            elif k == 6:
                for o in range(2):
                    eng.wait_ge(ln_act, 9 + o)
                    nc.vector.tensor_tensor(mix_lo[:, 4 + o, :], bank(4 * o), mix_hi[:, 4 + o, :].bitcast(F32),
                                            ALU.subtract).then_inc(side_lo, 1)
        return after

    with nc.Block() as block:

        @block.sync
        def _(sp):
            def load(s, c):
                sp.dma_start(w_raw[s][:], stream_d[ds(c, 1)].rearrange("o p n -> (o p) n")).then_inc(w_loaded[s], 16)

            half = KT // 2
            sp.dma_start(par[:, 0:PAR_FFN], par_d[:, 0:PAR_FFN]).then_inc(par_in, 16)
            sp.dma_start(xT[:, 0:half], x_d[0:half].rearrange("k p t -> p k t")).then_inc(x_in[0], 16)
            load(0, 0)
            sp.dma_start(xT[:, half:KT], x_d[half:KT].rearrange("k p t -> p k t")).then_inc(x_in[1], 16)
            load(1, 1)
            sp.dma_start(con[:, 0:CON_COS], con_d[:, 0:CON_COS]).then_inc(con_in, 16)
            load(2, 2)
            sp.dma_start(con[:, CON_COS:CON_MASKA], con_d[:, CON_COS:CON_MASKA]).then_inc(rope_in, 16)
            for s in range(3, RING):
                load(s, s)
            for c in range(RING, 2 * RING):
                sp.wait_ge(w_lo_done, c - RING + 1)
                load(c - RING, c)
                if c == RING + 2:
                    sp.dma_start(con[:, CON_MASKA:], con_d[:, CON_MASKA:]).then_inc(rest_in, 16)
                if c == RING + 4:
                    sp.dma_start(par[:, PAR_FFN:], par_d[:, PAR_FFN:]).then_inc(rest_in, 16)
            turns = N_CHUNKS // RING
            with sp.Fori(2, turns) as i:
                for s in range(RING):
                    sp.wait_ge(w_lo_done, i * RING + (s - RING + 1))
                    load(s, i * RING + s)
            for c in range(turns * RING, N_CHUNKS):
                sp.wait_ge(w_lo_done, c - RING + 1)
                load(c % RING, c)
            for m in range(KT):
                sp.wait_ge(x_new, 5 * KT + m + 1)
                sp.dma_start(out_d[m], xT[:, m, :]).then_inc(stored, 16)
            sp.wait_ge(stored, 16 * KT)

        @block.tensor
        def _(pe):
            for n in range(WARM_UP):
                out_zero(pe, (7,))
            for st in range(3):
                if st == 2:
                    pre_pe(pe)
                    pe.wait_ge(rest_in, 32)
                att_stage(pe, "pe", st, pe_tile, pe_event, side_pe(pe) if st == 2 else out_early(pe, st))
                out_pe(pe, st)
                ffn_stage(pe, st, ffn_pe(st))

        @block.scalar
        def _(act):
            nc.scalar.preload_act_table_set("natural_log_exp_and_others")
            for m in range(KT):
                resid_act(act, 0, m)
                if m == 3:
                    split_hi(act, -AHEAD_HI, 0, None)
            split_hi(act, 1 - AHEAD_HI, 0, None)
            for m in range(X_SQ_POOL, KT):
                resid_act_sq(act, m)
            act.wait_ge(con_in, 16)
            nc.scalar.activation(blk[:], con[:, CON_BLK:CON_BLK + P], ACT.Copy).then_inc(blk_in, 1)
            for c in range(2, AHEAD_HI):
                split_hi(act, c - AHEAD_HI, 0, None)
            act.wait_ge(rope_in, 16)
            resid_act_r(act, 0)
            for st in range(3):
                if st == 2:
                    pre_act_f(act)
                att_stage(act, "act", st, act_tile_c, act_event, side_act(act) if st == 2 else None)
                out_act(act, OUT_C0[st], 2 * st + 1)
                ffn_stage(act, st, ffn_act(st))
                if st < 2:
                    nc.scalar.preload_act_table_set("natural_log_exp_and_others")
                    ffn_end_act(act, 2 * st + 2)

        @block.vector
        def _(dve):
            dve.wait_ge(par_in, 16)
            for m in range(KT):
                resid_dve_lo(dve, 0, m)
                if m == 3:
                    split_lo(dve, -AHEAD, 0, None)
            split_lo(dve, 1 - AHEAD, 0, None)
            dve.wait_ge(rope_in, 16)
            rope_tables_dve(0)
            for c in range(2, AHEAD):
                split_lo(dve, c - AHEAD, 0, None)
            for st in range(3):
                if st == 2:
                    pre_dve_f(dve)
                att_stage(dve, "dve", st, dve_tile, dve_event, side_dve(dve) if st == 2 else None)
                out_dve(dve, OUT_C0[st], 2 * st + 1)
                ffn_stage(dve, st, ffn_dve(st))
                ffn_end_dve(dve, st)

        @block.gpsimd
        def _(pool):
            nc.gpsimd.memset(zero[:], 0.0).then_inc(zeroed, 1)
            nc.gpsimd.memset(cv_h[0][:], 0.0).then_inc(zeroed, 1)
            nc.gpsimd.memset(cv_h[1][:], 0.0).then_inc(zeroed, 1)
            resid_pool(pool, 0)
            pool.wait_ge(zeroed, 3)
            for st in range(3):
                if st > 0:
                    resid_pool(pool, 2 * st)
                if st < 2:
                    att_stage(pool, "pool", st, pool_tile, pool_event)
                else:
                    pool_zeroes(pool)
                    pre_pool_f(pool)
                    pool.wait_ge(cum_hi_done, 1)
                    nc.gpsimd.tensor_tensor(cum_lo, fg[2], cum_hi.bitcast(F32), ALU.subtract).then_inc(cum_lo_done, 1)
                    conv_pool(pool)
                resid_pool(pool, 2 * st + 1)
                ffn_stage(pool, st, ffn_pool(st))


def weight_stream(w):
    def tile(m):
        return m.reshape(KT, P, P).transpose(1, 0, 2).reshape(P, CHUNK)

    chunks = []

    def qkv(m, nd, pairs, cols):
        for pr in range(pairs):
            for g in range(nd):
                for role in range(3):
                    c = cols(role, g, pr)
                    chunks.append(tile(m[:, c:c + P]))

    def outs(m):
        for n in range(KT):
            chunks.append(tile(m[:, n * P:(n + 1) * P]))

    def mlp(up, down):
        for j in range(FT + 2):
            if j < FT:
                chunks.append(tile(up[:, j * P:(j + 1) * P]))
                chunks.append(tile(up[:, D_FF + j * P:D_FF + (j + 1) * P]))
            if j >= 2:
                chunks.append(down[(j - 2) * P:(j - 1) * P, :])

    qkv(w["a_w_qkv"][0], NDIL, PAIRS_AB, lambda r, g, pr: (r * NDIL + g) * D + pr * P)
    outs(w["a_w_o"][0])
    mlp(w["ffn_w_up"][0], w["ffn_w_down"][0])
    qkv(w["b_w_qkv"][0], 1, PAIRS_AB, lambda r, g, pr: r * D + pr * P)
    outs(w["b_w_o"][0])
    mlp(w["ffn_w_up"][1], w["ffn_w_down"][1])
    w_in = w["w_in_2"][0]
    att = HEADS_C * HD
    forget = np.zeros((D, P), np.float32)
    forget[:, 0:HEADS_C] = w_in[:, 3 * att:3 * att + HEADS_C]
    conv = 3 * att + HEADS_C
    for t in range(2):
        for half in range(2):
            c = conv + half * 2 * P + t * P
            chunks.append(tile(w_in[:, c:c + P]))
    chunks.append(tile(forget))
    for t in range(2):
        c = conv + 4 * P + t * P
        chunks.append(tile(w_in[:, c:c + P]))
    qkv(w_in, 1, PAIRS_C, lambda r, g, pr: r * att + pr * P)
    outs(w["w_out_2"][0])
    mlp(w["w_up_2"][0], w["w_down_2"][0])
    return np.stack(chunks)


def parameters(w):
    par = np.zeros((P, N_PAR), np.float32)

    def cols(at, v):
        n = v.shape[0] // P
        par[:, at:at + n] = v.reshape(n, P).T

    norms = (w["attn_norm"][0], w["ffn_norm"][0], w["attn_norm"][1], w["ffn_norm"][1], w["norm1_g_2"][0], w["norm2_g_2"][0])
    for e, v in enumerate(norms):
        cols(PAR_NORM + KT * e, v)
    gains = []
    for g in range(NDIL):
        gains += [w["a_q_norm"][0, g], w["a_k_norm"][0, g]]
    gains += [w["b_q_norm"][0], w["b_k_norm"][0], w["q_norm_g_2"][0], w["k_norm_g_2"][0]]
    half = ROPE_DIM // 2
    for n, v in enumerate(gains):
        par[:, PAR_GAIN + n] = np.concatenate([v, v])
        if n < 2 * NDIL + 2:
            sw = np.concatenate([v[half:ROPE_DIM], v[0:half], v[ROPE_DIM:]])
            par[:, PAR_SWAP + n] = np.concatenate([sw, sw])
    convs = ((w["ffn_conv_w"][0], w["ffn_conv_b"][0]), (w["ffn_conv_w"][1], w["ffn_conv_b"][1]), (w["ffn_dw_w_2"][0], None))
    for f, (cw, cb) in enumerate(convs):
        for j in range(FT):
            for s in range(2):
                c = PAR_FFN + 8 * (f * FT + j) + 4 * s
                rows = slice(s * D_FF + j * P, s * D_FF + (j + 1) * P)
                for k in range(3):
                    par[:, c + k] = cw[k, rows]
                if cb is not None:
                    par[:, c + 3] = cb[rows]
    for t in range(2):
        par[:, PAR_DW + t * CONV_C:PAR_DW + (t + 1) * CONV_C] = w["conv_dw_w_2"][0][:, t * P:(t + 1) * P].T
    cols(PAR_DWB, w["conv_dw_b_2"][0])
    cols(PAR_LNG, w["conv_ln_g_2"][0])
    cols(PAR_LNB, w["conv_ln_b_2"][0])
    cols(PAR_PSC, w["pool_scale_2"][0])
    par[0:HEADS_C, PAR_BF] = w["b_f_2"][0]
    for g in range(4):
        par[HD * (g % 2):HD * (g % 2) + HD, PAR_POOLW + (g // 2) * HD:PAR_POOLW + (g // 2 + 1) * HD] = w["pool_w_2"][0, g]
    for t in range(2):
        par[:, PAR_PW + t * 2 * P:PAR_PW + (t + 1) * 2 * P] = w["conv_pw_w_2"][0][t * P:(t + 1) * P, :]
    return par


def kernel(**inputs):
    import concourse.bacc as bacc
    from concourse.bass_utils import run_bass_kernel_spmd

    w = {k: np.asarray(v) for k, v in inputs.items()}
    con = shape_constants()
    arrays = {
        "x_t": np.ascontiguousarray(w["x"][0].T).reshape(KT, P, TOK),
        "w_stream": weight_stream(w),
        "params": parameters(w),
        "consts": con,
    }
    nc = bacc.Bacc("TRN2", target_bir_lowering=False, num_devices=1)
    f32 = mybir.dt.float32
    args = [nc.dram_tensor(n, a.shape, f32, kind="ExternalInput").ap() for n, a in arrays.items()]
    out = nc.dram_tensor("y_t", (KT, P, TOK), f32, kind="ExternalOutput").ap()
    build(nc, *args, out)
    r = run_bass_kernel_spmd(nc, [arrays], core_ids=[0])
    return r.results[0]["y_t"].reshape(D, TOK).T.reshape(1, TOK, D)
```
